# Optimizing a Trainium2 kernel written in Bass

```python
import jax, jax.numpy as jnp
from jax import lax
import numpy as np
import jax
import jax.numpy as jnp

D_MODEL = 1024
BATCH = 1
SEQ = 256
DEPTH = 2

CHUNK = 64
N_MIXERS = 2
N_ATTN_LAYERS = (DEPTH + 1) // 2
N_REC_LAYERS = DEPTH // 2

N_HEADS = 16
HEAD_DIM = D_MODEL // N_HEADS
LEFT_CHUNKS = 8
BAND_CHUNKS = LEFT_CHUNKS + 1
BAND = BAND_CHUNKS * CHUNK
MAX_REL_DIST = 128
N_REL = 2 * MAX_REL_DIST + 1
NEG_INF = -1e30

D_RNN = D_MODEL
N_RG_BLOCKS = 8
RG_BLOCK = D_RNN // N_RG_BLOCKS
CONV_WIDTH = 4
RG_C = 8.0

D_FF = 4 * D_MODEL
RMS_EPS = 1e-6


def rmsnorm(x, g):
    xf = x.astype(jnp.float32)
    y = xf * lax.rsqrt(jnp.mean(xf * xf, axis=-1, keepdims=True) + RMS_EPS)
    return (y * g.astype(jnp.float32)).astype(x.dtype)

def chunked_band_attention(h, w_qkv, w_o, rel_table):
    B, S, _ = h.shape
    n_chunks = S // CHUNK
    qkv = jnp.einsum('bsd,de->bse', h, w_qkv).reshape(B, S, 3, N_HEADS, HEAD_DIM)
    q, k, v = qkv[:, :, 0], qkv[:, :, 1], qkv[:, :, 2]
    pad = LEFT_CHUNKS * CHUNK
    k_pad = jnp.pad(k, ((0, 0), (pad, 0), (0, 0), (0, 0)))
    v_pad = jnp.pad(v, ((0, 0), (pad, 0), (0, 0), (0, 0)))
    q_chunks = q.reshape(B, n_chunks, CHUNK, N_HEADS, HEAD_DIM).transpose(1, 0, 2, 3, 4)
    qi = jnp.arange(CHUNK)[:, None]
    kj = jnp.arange(BAND)[None, :]
    rel = qi + pad - kj
    idx = jnp.clip(rel, -MAX_REL_DIST, MAX_REL_DIST) + MAX_REL_DIST
    bias = rel_table[:, idx].astype(jnp.float32)
    scale = HEAD_DIM ** -0.5
    band_offsets = jnp.arange(BAND)

    def one_chunk(args):
        c, q_c = args
        start = c * CHUNK
        k_band = lax.dynamic_slice_in_dim(k_pad, start, BAND, axis=1)
        v_band = lax.dynamic_slice_in_dim(v_pad, start, BAND, axis=1)
        s = jnp.einsum('bqhd,bkhd->bhqk', q_c, k_band).astype(jnp.float32) * scale + bias
        key_pos = start - pad + band_offsets
        s = jnp.where(key_pos[None, None, None, :] >= 0, s, NEG_INF)
        p = jax.nn.softmax(s, axis=-1).astype(v_band.dtype)
        return jnp.einsum('bhqk,bkhd->bqhd', p, v_band)

    o = lax.map(one_chunk, (jnp.arange(n_chunks), q_chunks))
    o = o.transpose(1, 0, 2, 3, 4).reshape(B, S, D_MODEL)
    return jnp.einsum('bsd,de->bse', o, w_o)

def rglru_block(h, w_in, b_in, conv_w, conv_b, w_ga, b_ga, w_gx, b_gx, a_param, w_o, b_o):
    B, S, _ = h.shape
    u = jnp.einsum('bsd,de->bse', h, w_in) + b_in
    x_br = u[..., :D_RNN]
    y_br = jax.nn.gelu(u[..., D_RNN:], approximate=True)
    xp = jnp.pad(x_br, ((0, 0), (CONV_WIDTH - 1, 0), (0, 0)))
    xc = conv_b + xp[:, 0:S] * conv_w[0]
    for tap in range(1, CONV_WIDTH):
        xc = xc + xp[:, tap:tap + S] * conv_w[tap]
    xb = xc.reshape(B, S, N_RG_BLOCKS, RG_BLOCK)
    r = jax.nn.sigmoid(jnp.einsum('bsnc,nce->bsne', xb, w_ga) + b_ga).reshape(B, S, D_RNN)
    ig = jax.nn.sigmoid(jnp.einsum('bsnc,nce->bsne', xb, w_gx) + b_gx).reshape(B, S, D_RNN)
    log_a = -RG_C * r.astype(jnp.float32) * jax.nn.softplus(-a_param.astype(jnp.float32))
    a = jnp.exp(log_a)
    mult = jnp.sqrt(-jnp.expm1(2.0 * log_a))
    b_seq = mult * (ig * xc).astype(jnp.float32)

    def combine(left, right):
        a1, b1 = left
        a2, b2 = right
        return a1 * a2, a2 * b1 + b2

    _, hs = lax.associative_scan(combine, (a, b_seq), axis=1)
    out = hs.astype(h.dtype) * y_br
    return jnp.einsum('bse,ed->bsd', out, w_o) + b_o

def sq_relu_mlp(h, w1, w2):
    z = jax.nn.relu(jnp.einsum('bsd,df->bsf', h, w1))
    return jnp.einsum('bsf,fd->bsd', z * z, w2)

def first_inputs(seed: int = 0) -> dict:
    key = jax.random.key(seed)
    ks = jax.random.split(key, 20)
    nrm = lambda k, shape, s: jax.random.normal(k, shape, jnp.float32) * s
    x = jax.random.normal(ks[0], (BATCH, SEQ, D_MODEL), jnp.float32)
    norm_mix = 1.0 + nrm(ks[1], (DEPTH, D_MODEL), 0.05)
    norm_mlp = 1.0 + nrm(ks[2], (DEPTH, D_MODEL), 0.05)
    attn_w_qkv = nrm(ks[3], (N_ATTN_LAYERS, D_MODEL, 3 * D_MODEL), D_MODEL ** -0.5)
    attn_w_o = nrm(ks[4], (N_ATTN_LAYERS, D_MODEL, D_MODEL), D_MODEL ** -0.5)
    attn_rel_bias = nrm(ks[5], (N_ATTN_LAYERS, N_HEADS, N_REL), 0.2)
    rec_w_in = nrm(ks[6], (N_REC_LAYERS, D_MODEL, 2 * D_RNN), D_MODEL ** -0.5)
    rec_b_in = nrm(ks[7], (N_REC_LAYERS, 2 * D_RNN), 0.02)
    rec_conv_w = nrm(ks[8], (N_REC_LAYERS, CONV_WIDTH, D_RNN), CONV_WIDTH ** -0.5)
    rec_conv_b = nrm(ks[9], (N_REC_LAYERS, D_RNN), 0.02)
    rec_w_ga = nrm(ks[10], (N_REC_LAYERS, N_RG_BLOCKS, RG_BLOCK, RG_BLOCK), RG_BLOCK ** -0.5)
    rec_b_ga = nrm(ks[11], (N_REC_LAYERS, N_RG_BLOCKS, RG_BLOCK), 0.02)
    rec_w_gx = nrm(ks[12], (N_REC_LAYERS, N_RG_BLOCKS, RG_BLOCK, RG_BLOCK), RG_BLOCK ** -0.5)
    rec_b_gx = nrm(ks[13], (N_REC_LAYERS, N_RG_BLOCKS, RG_BLOCK), 0.02)
    a0 = jax.random.uniform(ks[14], (N_REC_LAYERS, D_RNN), jnp.float32, 0.81, 0.998)
    s0 = a0 ** (1.0 / RG_C)
    rec_a_param = jnp.log(s0) - jnp.log1p(-s0)
    rec_w_o = nrm(ks[15], (N_REC_LAYERS, D_RNN, D_MODEL), D_RNN ** -0.5)
    rec_b_o = nrm(ks[16], (N_REC_LAYERS, D_MODEL), 0.02)
    mlp_w1 = nrm(ks[17], (DEPTH, D_MODEL, D_FF), D_MODEL ** -0.5)
    mlp_w2 = nrm(ks[18], (DEPTH, D_FF, D_MODEL), D_FF ** -0.5)
    norm_final = 1.0 + nrm(ks[19], (D_MODEL,), 0.05)
    return {"x": x, "norm_mix": norm_mix, "norm_mlp": norm_mlp,
            "attn_w_qkv": attn_w_qkv, "attn_w_o": attn_w_o, "attn_rel_bias": attn_rel_bias,
            "rec_w_in": rec_w_in, "rec_b_in": rec_b_in, "rec_conv_w": rec_conv_w,
            "rec_conv_b": rec_conv_b, "rec_w_ga": rec_w_ga, "rec_b_ga": rec_b_ga,
            "rec_w_gx": rec_w_gx, "rec_b_gx": rec_b_gx, "rec_a_param": rec_a_param,
            "rec_w_o": rec_w_o, "rec_b_o": rec_b_o,
            "mlp_w1": mlp_w1, "mlp_w2": mlp_w2, "norm_final": norm_final}

def first_block(x, norm_mix, norm_mlp, attn_w_qkv, attn_w_o, attn_rel_bias,
              rec_w_in, rec_b_in, rec_conv_w, rec_conv_b, rec_w_ga, rec_b_ga,
              rec_w_gx, rec_b_gx, rec_a_param, rec_w_o, rec_b_o,
              mlp_w1, mlp_w2, norm_final):
    h = x
    for layer in range(DEPTH):
        hn = rmsnorm(h, norm_mix[layer])
        j = layer // N_MIXERS
        if layer % N_MIXERS == 0:
            mix = chunked_band_attention(hn, attn_w_qkv[j], attn_w_o[j], attn_rel_bias[j])
        else:
            mix = rglru_block(hn, rec_w_in[j], rec_b_in[j], rec_conv_w[j], rec_conv_b[j],
                              rec_w_ga[j], rec_b_ga[j], rec_w_gx[j], rec_b_gx[j],
                              rec_a_param[j], rec_w_o[j], rec_b_o[j])
        h = h + mix
        h = h + sq_relu_mlp(rmsnorm(h, norm_mlp[layer]), mlp_w1[layer], mlp_w2[layer])
    return rmsnorm(h, norm_final)


DEPTH_2 = 1

HEAD_DIM_2 = 64
ATTN_WIDTH = D_MODEL // 2
N_ATTN_HEADS = ATTN_WIDTH // HEAD_DIM_2
N_KV_HEADS = 2
KV_WIDTH = N_KV_HEADS * HEAD_DIM_2
WINDOW = 128
BLOCK = 128
ROPE_THETA = 500000.0
ROTARY_DIM = HEAD_DIM_2 // 4
POOL_WINDOWS = (2, 4, 8, 16)
N_POOL_GROUPS = len(POOL_WINDOWS)
POOL_WIDTH = D_MODEL // 2
POOL_GROUP_WIDTH = POOL_WIDTH // N_POOL_GROUPS
MIX_WIDTH = ATTN_WIDTH + POOL_WIDTH
IN_WIDTH = ATTN_WIDTH + 2 * KV_WIDTH + POOL_WIDTH
D_FF_2 = 2816
EPS = 1e-6


def rms_norm(x, g):
    xf = x.astype(jnp.float32)
    y = xf * lax.rsqrt(jnp.mean(xf * xf, axis=-1, keepdims=True) + EPS)
    return (y * g.astype(jnp.float32)).astype(x.dtype)

def swiglu(x, w_gate, w_up, w_down):
    return (jax.nn.silu(x @ w_gate) * (x @ w_up)) @ w_down

def rope_tables(positions):
    inv_freq = ROPE_THETA ** (-jnp.arange(0, ROTARY_DIM, 2, dtype=jnp.float32) / ROTARY_DIM)
    ang = positions.astype(jnp.float32)[:, None] * inv_freq[None, :]
    emb = jnp.concatenate([ang, ang], axis=-1)
    return jnp.cos(emb)[None, :, None, :], jnp.sin(emb)[None, :, None, :]

def apply_partial_rope(t, cos, sin):
    tf = t.astype(jnp.float32)
    rot, rest = tf[..., :ROTARY_DIM], tf[..., ROTARY_DIM:]
    half = ROTARY_DIM // 2
    rot_half = jnp.concatenate([-rot[..., half:], rot[..., :half]], axis=-1)
    rot = rot * cos + rot_half * sin
    return jnp.concatenate([rot, rest], axis=-1).astype(t.dtype)

def window_attention(q, k, v, sink):
    B, S, H, D = q.shape
    nb = S // BLOCK
    G = H // N_KV_HEADS
    qb = q.reshape(B, nb, BLOCK, N_KV_HEADS, G, D)

    def bands(t):
        tp = jnp.pad(t, ((0, 0), (BLOCK, BLOCK), (0, 0), (0, 0)))
        tb = tp.reshape(B, nb + 2, BLOCK, N_KV_HEADS, D)
        return jnp.concatenate([tb[:, :-2], tb[:, 1:-1], tb[:, 2:]], axis=2)

    kb, vb = bands(k), bands(v)
    scores = jnp.einsum('bnqkgd,bnskd->bnkgqs', qb, kb,
                        preferred_element_type=jnp.float32) * (D ** -0.5)
    qpos = jnp.arange(nb)[:, None] * BLOCK + jnp.arange(BLOCK)[None, :]
    kpos = jnp.arange(nb)[:, None] * BLOCK + jnp.arange(3 * BLOCK)[None, :] - BLOCK
    dist = qpos[:, :, None] - kpos[:, None, :]
    valid = (jnp.abs(dist) <= WINDOW) & (kpos[:, None, :] >= 0) & (kpos[:, None, :] < S)
    scores = jnp.where(valid[None, :, None, None], scores, -1e30)
    sink_l = sink.astype(jnp.float32).reshape(N_KV_HEADS, G)[None, None, :, :, None, None]
    m = jnp.maximum(jnp.max(scores, axis=-1, keepdims=True), sink_l)
    p = jnp.exp(scores - m)
    denom = jnp.sum(p, axis=-1, keepdims=True) + jnp.exp(sink_l - m)
    p = (p / denom).astype(v.dtype)
    out = jnp.einsum('bnkgqs,bnskd->bnqkgd', p, vb)
    return out.reshape(B, S, H * D)

def multiscale_pool(u, w_pool, pool_scale):
    B, S, _ = u.shape
    uf = u.astype(jnp.float32)
    csum = jnp.concatenate([jnp.zeros((B, 1, POOL_WIDTH), jnp.float32),
                            jnp.cumsum(uf, axis=1)], axis=1)
    t = jnp.arange(S)
    means = []
    for gi, w in enumerate(POOL_WINDOWS):
        cg = csum[..., gi * POOL_GROUP_WIDTH:(gi + 1) * POOL_GROUP_WIDTH]
        half = w // 2

        def win_mean(lo, hi):
            a = jnp.clip(lo, 0, S)
            b = jnp.clip(hi + 1, 0, S)
            s = jnp.take(cg, b, axis=1) - jnp.take(cg, a, axis=1)
            return s / (b - a).astype(jnp.float32)[None, :, None]

        means.append(0.5 * (win_mean(t - half, t + half - 1) + win_mean(t - half + 1, t + half)))
    mean = jnp.concatenate(means, axis=-1)
    d = (mean - uf).reshape(B, S, N_POOL_GROUPS, POOL_GROUP_WIDTH)
    y = jnp.einsum('bsgc,gcd->bsgd', d, w_pool.astype(jnp.float32)).reshape(B, S, POOL_WIDTH)
    return (y * pool_scale.astype(jnp.float32)).astype(u.dtype)

def second_inputs(seed: int = 0) -> dict:
    key = jax.random.key(seed)
    ks = jax.random.split(key, 18)
    f32 = jnp.float32
    L = DEPTH_2

    def nrm(k, shape, scale):
        return jax.random.normal(k, shape, f32) * scale

    def gain(k, shape, s=0.05):
        return 1.0 + s * jax.random.normal(k, shape, f32)

    return {
        'x': nrm(ks[0], (BATCH, SEQ, D_MODEL), 1.0),
        'ffn1_norm': gain(ks[1], (L, D_MODEL)),
        'ffn1_w_gate': nrm(ks[2], (L, D_MODEL, D_FF_2), D_MODEL ** -0.5),
        'ffn1_w_up': nrm(ks[3], (L, D_MODEL, D_FF_2), D_MODEL ** -0.5),
        'ffn1_w_down': nrm(ks[4], (L, D_FF_2, D_MODEL), D_FF_2 ** -0.5),
        'mix_norm': gain(ks[5], (L, D_MODEL)),
        'w_in': nrm(ks[6], (L, D_MODEL, IN_WIDTH), D_MODEL ** -0.5),
        'sink_logits': nrm(ks[7], (L, N_ATTN_HEADS), 0.5),
        'pool_w': nrm(ks[8], (L, N_POOL_GROUPS, POOL_GROUP_WIDTH, POOL_GROUP_WIDTH), POOL_GROUP_WIDTH ** -0.5),
        'pool_scale': gain(ks[9], (L, POOL_WIDTH), 0.1),
        'w_out': nrm(ks[10], (L, MIX_WIDTH, D_MODEL), MIX_WIDTH ** -0.5),
        'ffn2_norm': gain(ks[11], (L, D_MODEL)),
        'ffn2_w_gate': nrm(ks[12], (L, D_MODEL, D_FF_2), D_MODEL ** -0.5),
        'ffn2_w_up': nrm(ks[13], (L, D_MODEL, D_FF_2), D_MODEL ** -0.5),
        'ffn2_w_down': nrm(ks[14], (L, D_FF_2, D_MODEL), D_FF_2 ** -0.5),
        'final_norm': gain(ks[15], (D_MODEL,)),
    }

def second_block(x, ffn1_norm, ffn1_w_gate, ffn1_w_up, ffn1_w_down, mix_norm, w_in,
              sink_logits, pool_w, pool_scale, w_out, ffn2_norm, ffn2_w_gate,
              ffn2_w_up, ffn2_w_down, final_norm):
    B, S, _ = x.shape
    positions = jnp.arange(S, dtype=jnp.int32)
    cos, sin = rope_tables(positions)
    h = x
    for l in range(DEPTH_2):
        h = h + 0.5 * swiglu(rms_norm(h, ffn1_norm[l]), ffn1_w_gate[l], ffn1_w_up[l], ffn1_w_down[l])
        u = rms_norm(h, mix_norm[l]) @ w_in[l]
        q, k, v, pc = jnp.split(u, [ATTN_WIDTH, ATTN_WIDTH + KV_WIDTH, ATTN_WIDTH + 2 * KV_WIDTH], axis=-1)
        q = apply_partial_rope(q.reshape(B, S, N_ATTN_HEADS, HEAD_DIM_2), cos, sin)
        k = apply_partial_rope(k.reshape(B, S, N_KV_HEADS, HEAD_DIM_2), cos, sin)
        v = v.reshape(B, S, N_KV_HEADS, HEAD_DIM_2)
        a = window_attention(q, k, v, sink_logits[l])
        p = multiscale_pool(pc, pool_w[l], pool_scale[l])
        h = h + jnp.concatenate([a, p], axis=-1) @ w_out[l]
        h = h + 0.5 * swiglu(rms_norm(h, ffn2_norm[l]), ffn2_w_gate[l], ffn2_w_up[l], ffn2_w_down[l])
    return rms_norm(h, final_norm)


def setup_inputs(seed=0):
    out = dict(first_inputs(seed))
    for name, value in second_inputs(seed + 1).items():
        if name != "x":
            out[name + "_2"] = value
    return out


def reference(
    x, norm_mix, norm_mlp, attn_w_qkv, attn_w_o, attn_rel_bias, rec_w_in, rec_b_in, rec_conv_w,
    rec_conv_b, rec_w_ga, rec_b_ga, rec_w_gx, rec_b_gx, rec_a_param, rec_w_o, rec_b_o, mlp_w1,
    mlp_w2, norm_final, ffn1_norm_2, ffn1_w_gate_2, ffn1_w_up_2, ffn1_w_down_2, mix_norm_2,
    w_in_2, sink_logits_2, pool_w_2, pool_scale_2, w_out_2, ffn2_norm_2, ffn2_w_gate_2,
    ffn2_w_up_2, ffn2_w_down_2, final_norm_2,
):
    x = first_block(
        x, norm_mix, norm_mlp, attn_w_qkv, attn_w_o, attn_rel_bias, rec_w_in, rec_b_in,
        rec_conv_w, rec_conv_b, rec_w_ga, rec_b_ga, rec_w_gx, rec_b_gx, rec_a_param, rec_w_o,
        rec_b_o, mlp_w1, mlp_w2, norm_final,
    )
    return second_block(
        x, ffn1_norm_2, ffn1_w_gate_2, ffn1_w_up_2, ffn1_w_down_2, mix_norm_2, w_in_2,
        sink_logits_2, pool_w_2, pool_scale_2, w_out_2, ffn2_norm_2, ffn2_w_gate_2, ffn2_w_up_2,
        ffn2_w_down_2, final_norm_2,
    )


_drawn_inputs = setup_inputs


def setup_inputs(seed=0):
    import zlib

    import numpy as np

    out = dict(_drawn_inputs(seed))
    spreads = {}
    factors = {'rec_b_ga': 28.226,
     'rec_b_gx': 8.0,
     'rec_b_o': 4.418,
     'sink_logits_2': 30.501,
     'ffn2_norm_2': 3.067}
    for name, (base, spread) in spreads.items():
        noise = np.random.default_rng([zlib.crc32(name.encode()), seed]).standard_normal(out[name].shape)
        drawn = base * np.exp(spread * noise) if base else spread * noise
        out[name] = jnp.asarray(drawn.astype(out[name].dtype))
    for name, factor in factors.items():
        out[name] = (out[name] * factor).astype(out[name].dtype)
    return out
```

```python
from contextlib import ExitStack, contextmanager

import numpy as np
import concourse.bass as bass
from concourse import mybir

F32 = mybir.dt.float32
F32R = mybir.dt.float32r
BF16 = mybir.dt.bfloat16
ACT = mybir.ActivationFunctionType
ALU = mybir.AluOpType

P = 128
S = 256
T = S // P
D = 1024
KB = D // P
EPS = 1e-6
HD = 64
QSCALE = HD ** -0.5
N_HEADS, CHUNK, MAX_REL = 16, 64, 128
CONV = 4
D_FF, D_FF_2 = 4096, 2816
HEADS_2, KV_2, WINDOW, ROT, THETA = 8, 2, 128, 16, 500000.0
POOL_WINDOWS = (2, 4, 8, 16)
PG = len(POOL_WINDOWS)
NEG = -1e30

PIECE = 2048
RING = 3
RAW = 6
LOOK = RING - 1
BODY = 6

VECTORS = [("norm_mix0", 8), ("norm_mlp0", 8), ("norm_mix1", 8), ("norm_mlp1", 8), ("norm_final", 8),
           ("ffn1_norm", 8), ("mix_norm", 8), ("ffn2_norm", 8), ("b_in", 16), ("conv_b", 8), ("b_ga", 8),
           ("b_gx", 8), ("a_param", 8), ("conv_w", 8 * CONV), ("pool_scale", PG)]


class Loop:

    def __init__(self, count):
        self.count, self.reg = count, None


class Step:

    def __init__(self, c, loop=None, per=0):
        self.c, self.loop, self.per = c, loop, per

    def of(self, mult=1, plus=0):
        return Step(self.c * mult + plus, self.loop, self.per * mult)

    def value(self):
        return self.c if self.loop is None else self.loop.reg * self.per + self.c

    def slot(self, n):
        assert self.loop is None or self.per % n == 0
        return self.c % n


def as_step(x):
    return x if isinstance(x, Step) else Step(x)


class Series:

    def __init__(self, nc, name, unit=1):
        self.sem, self.unit, self.claimed = nc.alloc_semaphore(name), unit, 0

    def claim(self, n):
        self.claimed += n
        return self.claimed - n


class Plan:

    def __init__(self, nc, engines):
        self.queues = {e: [] for e in engines}
        self.done = {e: Series(nc, f"{e}_done") for e in engines}
        self.named, self.loop_now = {}, None

    def op(self, engine, emit, after=(), name=None, signal=None):
        if name:
            assert signal is None and self.loop_now is None and name not in self.named, name
            signal = self.done[engine]
            self.named[name] = (signal, Step(signal.claim(1)))
        self.queues[engine].append((emit, list(after), signal))

    @contextmanager
    def loop(self, count):
        self.loop_now = loop = Loop(count)
        outer, self.queues = self.queues, {e: [] for e in self.queues}
        yield loop
        for e, body in self.queues.items():
            if body:
                outer[e].append((loop, body, None))
        self.queues, self.loop_now = outer, None

    def write(self, engine, e):
        self._write(e, self.queues[engine], {})

    def _write(self, e, entries, met):
        for emit, after, signal in entries:
            if isinstance(emit, Loop):
                with e.Fori(0, emit.count) as i:
                    emit.reg = i
                    self._write(e, after, dict(met))
                emit.reg = None
                continue
            for w in after:
                series, step = self.named[w] if isinstance(w, str) else w
                step = as_step(step)
                if step.loop is None:
                    need = (step.c + 1) * series.unit
                    if need <= met.get(series, 0):
                        continue
                    met[series] = need
                    e.wait_ge(series.sem, need)
                else:
                    e.wait_ge(series.sem, step.of(series.unit, series.unit).value())
            last = emit(e)
            if signal is not None:
                last.then_inc(signal.sem, signal.unit)


def steps(plan, first, count, per, body, straight=0):
    turns = (count - straight) // per
    if turns > 1:
        with plan.loop(turns) as loop:
            for k in range(per):
                body(Step(first + k, loop, per))
    else:
        turns = 0
    for k in range(first + turns * per, first + count):
        body(Step(k))


def bcast(ap, *dims):
    return bass.AP(tensor=ap.tensor, offset=ap.offset, ap=[list(ap.ap[0])] + [list(d) for d in dims])


def build(nc, A, out):
    plan = Plan(nc, ("sp", "act", "dve", "pool", "pe"))
    op = plan.op

    def sb(name, shape, dt=F32):
        return nc.alloc_sbuf_tensor(name, shape, dt)[tuple(slice(None) for _ in shape)]

    raw = [sb(f"raw{i}", [P, PIECE]) for i in range(RAW)]
    w_hi = [sb(f"w_hi{i}", [P, PIECE], F32R) for i in range(RING)]
    w_lo = [sb(f"w_lo{i}", [P, PIECE], F32R) for i in range(RING)]
    h = sb("h", [P, T, D])
    xT_hi, xT_lo = sb("xT_hi", [P, KB, S], F32R), sb("xT_lo", [P, KB, S], F32R)
    z_hi, z_lo = sb("z_hi", [P, 3, 2 * S], F32R), sb("z_lo", [P, 3, 2 * S], F32R)
    rms = sb("rms", [P, S])
    ident, ones = sb("ident", [P, P]), sb("ones", [P, S])
    zeros = sb("zeros", [P, P], BF16)
    diag = sb("diag", [P, T, P])
    rstd, ssq = sb("rstd", [P, 2 * T]), sb("ssq", [P, 2 * T])
    minus_half = sb("minus_half", [P, 1])
    ncols = sum(n for _, n in VECTORS)
    cols = sb("cols", [P, ncols])
    extra = sb("extra", [P, 3 * KB])
    gate_w = sb("gate_w", [P, 2, KB, P])
    pool_w = sb("pool_w", [P, PG, P])
    tiny = sb("tiny", [P, 6, 4])
    sink = sb("sink", [P, HEADS_2])
    work_bytes = 47 * 1024
    work = nc.alloc_sbuf_tensor("work", [P, work_bytes // 4], F32)
    bank = [nc.alloc_psum_tensor(f"bank{i}", [P, 512], F32)[:, :] for i in range(8)]
    acc = [[bank[0], bank[1]], [bank[2], bank[3]]]
    RMS_BANK = bank[7]

    def at(kib, *shape):
        n, o = int(np.prod(shape)), int(kib * 256)
        assert (o + n) * 4 <= work_bytes, (kib, shape)
        v = work[:, o:o + n]
        if len(shape) == 1:
            return v
        names = "abcd"[:len(shape)]
        return v.rearrange(f"p ({' '.join(names)}) -> p {' '.join(names)}", **dict(zip(names, shape)))

    def r32(ap):
        return ap.bitcast(F32)

    col_at, c = {}, 0
    for name, n in VECTORS:
        col_at[name], c = c, c + n

    def col(name, k):
        return cols[:, col_at[name] + k:col_at[name] + k + 1]

    def gain(name):
        return cols[:, col_at[name]:col_at[name] + KB]

    landed = [Series(nc, f"landed{i}", 16) for i in range(RAW)]
    hi_done = Series(nc, "hi_done")
    lo_done = Series(nc, "lo_done")
    used = Series(nc, "used")
    z_t = Series(nc, "z_t")
    z_g = Series(nc, "z_g")
    z_f = Series(nc, "z_f")
    zhi_done = Series(nc, "zhi_done")
    zlo_done = Series(nc, "zlo_done")
    acc_done = Series(nc, "acc_done")
    turned = Series(nc, "turned")
    x_full = Series(nc, "x_full")
    xhi_done = Series(nc, "xhi_done")
    xlo_done = Series(nc, "xlo_done")
    mix_hi = Series(nc, "mix_hi")
    mix_lo = Series(nc, "mix_lo")
    const_in = {}

    def load(name, dst, src, engine="pool", after=()):
        const_in[name] = Series(nc, f"in_{name}", 16)
        op(engine, lambda e: e.dma_start(dst, src), after=after, signal=const_in[name])

    def has(name):
        return (const_in[name], 0)

    class Stream:
        n = 0

    def u_src(w, cstep):
        v = w.rearrange("(k p) c -> p k c", p=P)
        return lambda: v[:, :, bass.ds(cstep.value(), 2 * P)]

    def d_src(w, rstep):
        return lambda: w[bass.ds(rstep.value(), 2 * P), :].rearrange("(k p) c -> p k c", p=P)

    def load_piece(n, src, kind):
        n, slot = as_step(n), as_step(n).slot(RAW)
        nth = Step(n.c // RAW, n.loop, n.per // RAW)
        dst = raw[slot].rearrange("p (k c) -> p k c", k=KB if kind == "U" else 2)
        del nth
        op("sp", lambda e: e.dma_start(dst, src()), after=[(lo_done, n.of(1, -RAW))] if free(n, RAW) else [],
           signal=landed[slot])

    def free(n, ring):
        return n.loop is not None or n.c >= ring

    def split_piece(n):
        n = as_step(n)
        if n.loop is None and n.c >= TOTAL:
            return
        s, r = n.slot(RING), n.slot(RAW)
        nth = Step(n.c // RAW, n.loop, n.per // RAW)
        after = [(landed[r], nth)]
        if free(n, RING):
            after.append((used, n.of(1, -RING)))
        op("act", lambda e: e.activation(w_hi[s], raw[r], ACT.Copy), after=after, signal=hi_done)
        op("dve", lambda e: e.tensor_tensor(w_lo[s], raw[r], r32(w_hi[s]), ALU.subtract),
           after=[(hi_done, n)], signal=lo_done)

    def split_now(n):
        return [(hi_done, n), (lo_done, n)]

    def u_piece(n, dst, after=(), after_k=None):
        n, s = as_step(n), as_step(n).slot(RING)
        whi = w_hi[s].rearrange("p (k c) -> p k c", k=KB)
        wlo = w_lo[s].rearrange("p (k c) -> p k c", k=KB)

        def block(k):
            def emit(e):
                for b in range(2):
                    o, c = dst[:, b * S:(b + 1) * S], slice(b * P, (b + 1) * P)
                    e.matmul(o, whi[:, k, c], xT_hi[:, k, :], start=(k == 0 and b == 0), stop=False,
                             skip_group_check=True)
                    e.matmul(o, whi[:, k, c], xT_lo[:, k, :], start=False, stop=False, skip_group_check=True)
                    last = e.matmul(o, wlo[:, k, c], xT_hi[:, k, :], start=False, stop=(k == KB - 1),
                                    skip_group_check=True)
                return last
            return emit
        for k in range(KB):
            op("pe", block(k), after=(list(after) + split_now(n) if k == 0 else []) + (after_k(k) if after_k else []),
               signal=used if k == KB - 1 else None)

    def d_piece(n, lhs, first, last, after=()):
        n, s = as_step(n), as_step(n).slot(RING)
        whi = w_hi[s].rearrange("p (k c) -> p k c", k=2)
        wlo = w_lo[s].rearrange("p (k c) -> p k c", k=2)

        def tile(t):
            def emit(e):
                for kk in range(2):
                    xhi, xlo = lhs(kk, t)
                    for x, ws in ((xhi, (whi, wlo)), (xlo, (whi,))):
                        for w in ws:
                            for half in range(2):
                                mm = e.matmul(acc[t][half], x, w[:, kk, half * 512:(half + 1) * 512],
                                              start=(first and kk == 0 and x is xhi and w is whi),
                                              stop=(last and kk == 1 and x is xlo), skip_group_check=True)
                return mm
            return emit
        for t in range(T):
            op("pe", tile(t), after=list(after) + split_now(n) if t == 0 else [],
               signal=used if t == T - 1 else (acc_done if last else None))

    vec_rows = at(0, 2, P)
    plan_rows = []
    for name, n in VECTORS:
        plan_rows.append((A[name].rearrange("(n p) -> n p", p=P), col_at[name], n))
    VEC_ROWS = [P, ncols - P]
    NVL = 0
    vec_in = Series(nc, "vec_in", 16)
    for src, at0, n in plan_rows:
        done = 0
        while done < n:
            g = (at0 + done) // P
            k = min(n - done, (g + 1) * P - at0 - done)
            row = at0 + done - g * P
            op("act",
               lambda e, d=vec_rows[row:row + k, g, :], s_=src[done:done + k, :]: e.dma_start(d, s_),
               signal=vec_in)
            NVL += 1
            done += k

    x_in = [Series(nc, f"x_in{t}", 16) for t in range(T)]
    for t in range(T):
        op("sp", lambda e, t=t: e.dma_start(h[:, t, :], A["x"][t * P:(t + 1) * P, :]), signal=x_in[t])

    op("pool", lambda e: e.memset(ident, 0.0), name="ident0")
    op("pool", lambda e: e.affine_select(out=ident, in_=ident, compare_op=ALU.not_equal, fill=1.0, base=0,
                                         pattern=[[-1, P]], channel_multiplier=1), after=["ident0"], name="ident")
    op("pool", lambda e: e.memset(ones, 1.0), name="ones")
    op("pool", lambda e: e.memset(minus_half, -0.5), name="minus_half")
    op("pool", lambda e: e.memset(zeros, 0.0), name="zeros")
    op("act", lambda e: e.activation(tiny[:, 0, 0:1], ones[:, 0:1], ACT.Copy), after=["ones"])

    def turn_vectors(g):
        rows = VEC_ROWS[g]
        return lambda e: e.transpose(bank[5][:, g * P:g * P + rows], vec_rows[0:rows, g, :], ident[0:rows, 0:rows])
    for g in range(2):
        op("pe", turn_vectors(g), after=["ident", (vec_in, NVL - 1)], name=f"vec_turn{g}")
    op("dve", lambda e: e.tensor_copy(cols, bank[5][:, 0:ncols]), after=["vec_turn1"], name="cols")

    norms = []

    def turn_h(name, gains, acc0=None, scale=1.0, between=None, x_at=4):
        j = len(norms)
        norms.append(name)
        base = turned.claim(2 * T)
        assert x_full.claim(2 * T) == xhi_done.claim(2 * T) == xlo_done.claim(2 * T) == base == 2 * T * j
        full = at(x_at, 2, 512)
        for t in range(T):
            for half in range(2):
                if acc0 is not None:
                    op("dve", lambda e, hh=h[:, t, half * 512:(half + 1) * 512], a=acc[t][half]:
                       e.scalar_tensor_tensor(out=hh, in0=a, scalar=scale, in1=hh, op0=ALU.mult, op1=ALU.add),
                       after=[acc0[t]], name=f"{name}_h{t}{half}")
            for half in range(2):
                i, b = base + 2 * t + half, bank[6 + half]
                have = [f"{name}_h{t}{half}"] if acc0 is not None else [(x_in[t], 0)]

                def turn4(e, t=t, half=half, b=b):
                    for kk in range(4):
                        k = half * 4 + kk
                        tr = e.transpose(b[:, kk * P:(kk + 1) * P], h[:, t, k * P:(k + 1) * P], ident)
                    return tr
                op("pe", turn4, after=have + ["ident"] + ([(x_full, i - 2)] if t else []), signal=turned)
                op("dve", lambda e, b=b, half=half: e.tensor_tensor(
                    full[:, half, :].rearrange("p (k s) -> p k s", k=4), b.rearrange("p (k s) -> p k s", k=4),
                    bcast(gains[:, half * 4:half * 4 + 4], [1, 4], [0, P]), ALU.mult),
                   after=[(turned, i), "cols"] + ([(xlo_done, i - 2)] if t else []), signal=x_full)
            for half in range(2):
                i = base + 2 * t + half
                src = full[:, half, :].rearrange("p (k s) -> p k s", k=4)
                hi, lo = (x[:, half * 4:half * 4 + 4, t * P:(t + 1) * P] for x in (xT_hi, xT_lo))
                op("act", lambda e, hi=hi, src=src: e.activation(hi, src, ACT.Copy), after=[(x_full, i)],
                   signal=xhi_done)
                op("dve", lambda e, hi=hi, lo=lo, src=src: e.tensor_tensor(lo, src, r32(hi), ALU.subtract),
                   after=[(xhi_done, i)], signal=xlo_done)
        junk = at(0, D)
        for t in range(T):
            have = [f"{name}_h{t}1"] if acc0 is not None else [(x_in[t], 0)]
            op("act", lambda e, t=t: e.activation(junk, h[:, t, :], ACT.Square, accum_out=ssq[:, t:t + 1]),
               after=have + ([f"{name}_ss0"] if t else ["cols"]), name=f"{name}_ss{t}")
        for t in range(T):
            make_rstd(f"{name}_r{t}", t, f"{name}_ss{t}")
            last = f"{name}_r{t}"
            if between is not None:
                op("dve", lambda e, t=t: e.scalar_tensor_tensor(
                    out=h[:, t, :], in0=h[:, t, :], scalar=rstd[:, t:t + 1], in1=between, op0=ALU.mult,
                    op1=ALU.mult),
                   after=[last, f"{name}_ss{t}", (turned, base + 2 * t + 1), has("norm_final")],
                   name=f"{name}_n{t}")
                op("act", lambda e, t=t: e.activation(junk, h[:, t, :], ACT.Square,
                                                      accum_out=ssq[:, T + t:T + t + 1]),
                   after=[f"{name}_n{t}", f"{name}_ns{t - 1}" if t else f"{name}_ss{T - 1}"], name=f"{name}_ns{t}")
                make_rstd(f"{name}_nr{t}", T + t, f"{name}_ns{t}")
                op("pool", lambda e, t=t: e.tensor_tensor(rstd[:, t:t + 1], rstd[:, t:t + 1],
                                                          rstd[:, T + t:T + t + 1], ALU.mult),
                   after=[f"{name}_nr{t}", f"{name}_n{t}"], name=f"{name}_rr{t}")
                last = f"{name}_rr{t}"
            op("pool", lambda e, t=t: e.tensor_scalar(diag[:, t, :], ident, rstd[:, t:t + 1], None, ALU.mult),
               after=[last], name=f"{name}_diag{t}")

    def make_rstd(name, i, ss):
        v = rstd[:, i:i + 1]
        op("pool", lambda e: e.tensor_scalar(v, ssq[:, i:i + 1], 1.0 / D, EPS, ALU.mult, ALU.add), after=[ss],
           name=f"{name}_v")
        op("pool", lambda e: e.tensor_tensor(v, v, minus_half, ALU.pow), after=[f"{name}_v", "minus_half"],
           name=name)

    def spread_rms(name):
        for t in range(T):
            op("pe", lambda e, t=t: e.matmul(RMS_BANK[:, t * P:(t + 1) * P], ones[:, 0:P], diag[:, t, :],
                                             start=True, stop=True),
               after=[f"{name}_diag{t}", "ones", (xlo_done, 2 * T * len(norms) - 1)], name=f"{name}_spread{t}")
        op("dve", lambda e: e.tensor_copy(rms, RMS_BANK[:, 0:S]), after=[f"{name}_spread{T - 1}"],
           name=f"{name}_rms")

    def x_block_ready(j):
        return lambda k: [(xlo_done, 2 * T * j - 2 + k // 4)]

    def rms_pair():
        return bcast(rms, [0, 2], [1, S])

    def pair(ap):
        return ap.rearrange("p (b s) -> p b s", b=2)

    def feed_forward(name, ups, down, width, straight=0):
        pairs, nu = width // (2 * P), len(ups)
        each, n0, bufs = nu + 1, Stream.n, (3 if nu == 1 else 2)
        b_zt, b_zf = z_t.claim(pairs), z_f.claim(pairs)
        b_zg = z_g.claim(pairs) if nu == 2 else 0
        b_hi, b_lo = zhi_done.claim(pairs), zlo_done.claim(pairs)
        acc0 = [(acc_done, acc_done.claim(1)), (used, n0 + each * pairs - 1)]
        j = len(norms)
        tmp = [at(0, 2 * S), at(2, 2 * S), at(4, 2 * S)]

        def ups_at(p):
            return Step(n0) if p.loop is None and p.c == 0 else p.of(each, n0 - 1)

        def d_at(p):
            return p.of(each, n0 + each - 1) if p.loop is None and p.c == pairs - 1 \
                else p.of(each, n0 + 2 * each - 2)

        def psum_of(p, i):
            return bank[4 + p.slot(bufs) * nu + i]

        def up(p):
            n = ups_at(p)
            for i, w in enumerate(ups):
                load_piece(n.of(1, i), u_src(w, p.of(2 * P)), "U")
            for i in range(nu):
                after = []
                if free(p, bufs):
                    after = [(z_t, p.of(1, b_zt - bufs))]
                first = p.loop is None and p.c == 0 and i == 0
                u_piece(n.of(1, i), psum_of(p, i), after=after, after_k=x_block_ready(j) if first else None)

        def down_of(p, last=False):
            n = d_at(p)
            load_piece(n, d_src(down, p.of(2 * P)), "D")
            s = p.slot(bufs)
            d_piece(n, lambda kk, t: (z_hi[:, s, kk * S + t * P:kk * S + (t + 1) * P],
                                      z_lo[:, s, kk * S + t * P:kk * S + (t + 1) * P]),
                    first=False, last=last, after=[(zhi_done, p.of(1, b_hi)), (zlo_done, p.of(1, b_lo))])

        def finish_z(p):
            s, src = p.slot(bufs), psum_of(p, nu - 1)
            freed = []
            if free(p, bufs):
                freed = [(used, p.of(each, n0 + 2 * each - 2 - bufs * each))]
            here = [(used, ups_at(p).of(1, nu - 1)), f"{name}_rms"]
            if nu == 1:
                t, z = tmp[0], tmp[1]
                op("dve", lambda e: e.scalar_tensor_tensor(out=pair(t), in0=pair(src), scalar=0.0, in1=rms_pair(),
                                                           op0=ALU.max, op1=ALU.mult),
                   after=here + [(zhi_done, p.of(1, b_hi - 1))], signal=z_t)
                op("dve", lambda e: e.tensor_tensor(z, t, t, ALU.mult), after=[(z_t, p.of(1, b_zt))], signal=z_f)
                op("act", lambda e: e.activation(z_hi[:, s, :], t, ACT.Square),
                   after=[(z_t, p.of(1, b_zt))] + freed, signal=zhi_done)
            else:
                g, u, z = tmp
                op("dve", lambda e: e.tensor_tensor(pair(g), pair(psum_of(p, 0)), rms_pair(), ALU.mult),
                   after=here, name=None, signal=z_g)
                op("act", lambda e: e.activation(g, g, ACT.Silu), after=[(z_g, p.of(1, b_zg))], signal=z_s)
                op("dve", lambda e: e.tensor_tensor(pair(u), pair(src), rms_pair(), ALU.mult), signal=z_t)
                op("dve", lambda e: e.tensor_tensor(z, g, u, ALU.mult),
                   after=[(z_s, p.of(1, b_zg)), (z_t, p.of(1, b_zt)), (zhi_done, p.of(1, b_hi - 1))], signal=z_f)
                op("act", lambda e: e.activation(z_hi[:, s, :], z, ACT.Copy),
                   after=[(z_f, p.of(1, b_zf))] + freed, signal=zhi_done)
            op("dve", lambda e: e.tensor_tensor(z_lo[:, s, :], z, r32(z_hi[:, s, :]), ALU.subtract),
               after=[(zhi_done, p.of(1, b_hi)), (z_f, p.of(1, b_zf))], signal=zlo_done)

        up(Step(0))
        spread_rms(name)
        for half in range(4):
            op("pe", lambda e, half=half: e.matmul(bank[half][:, 0:2], zeros, zeros[:, 0:2], start=True, stop=False,
                                                   skip_group_check=True), after=["zeros"])
        for i in range(nu):
            split_piece(n0 + i + LOOK)
        finish_z(Step(0))

        def turn(p):
            up(p)
            down_of(p.of(1, -1))
            n = ups_at(p)
            for i in range(each):
                split_piece(n.of(1, i + LOOK))
            finish_z(p)
        steps(plan, 1, pairs - 1, BODY // each, turn, straight=straight)
        down_of(Step(pairs - 1), last=True)
        split_piece(n0 + each * pairs - 1 + LOOK)
        Stream.n += each * pairs
        return acc0

    z_s = Series(nc, "z_s")

    def project(name, w, order, ready):
        n0 = Stream.n
        acc0 = [(acc_done, acc_done.claim(1)), (used, n0 + len(order) - 1)]
        for m, i in enumerate(order):
            load_piece(n0 + m, d_src(w, Step(i * 2 * P)), "D")
            d_piece(n0 + m, lambda kk, t, i=i: (xT_hi[:, 2 * i + kk, t * P:(t + 1) * P],
                                                xT_lo[:, 2 * i + kk, t * P:(t + 1) * P]),
                    first=(m == 0), last=(m == len(order) - 1), after=ready(i))
            split_piece(n0 + m + LOOK)
        Stream.n += len(order)
        return acc0

    def attention(name, pairs, widths, masks, qT, kT, v, o, pt, pp, ready, sinks=False, stage_mask=None):
        A_ = {k: Series(nc, f"{name}_{k}") for k in
              ("qkhi", "qklo", "s", "tm", "nm", "ex", "tr", "pt0", "pt1", "pv", "rc", "o", "sd", "es", "sx", "msk")}
        off = [0, widths[0]]
        tiles = [(t, kt) for t in range(T) for kt in range(widths[t] // P)]
        q_hi, q_lo = z_hi[:, 0, 0:S], z_lo[:, 0, 0:S]
        k_hi, k_lo = z_hi[:, 0, S:2 * S], z_lo[:, 0, S:2 * S]
        mx, nm, sm, rc, sd, es = (tiny[:, i, :] for i in range(6))

        def prev(series, j, n=1, plus=0):
            return [(series, j.of(n, plus))] if j.loop is not None or j.c * n + plus >= 0 else []

        def split_qk(j):
            for i, (x, xh, xl) in enumerate(((qT, q_hi, q_lo), (kT, k_hi, k_lo))):
                op("act", lambda e, x=x, xh=xh: e.activation(xh, x[:, bass.ds(j.value(), 1), :].squeeze(1)
                                                             if j.loop else x[:, j.c, :], ACT.Copy),
                   after=prev(A_["s"], j, 2, -1) + ready, signal=A_["qkhi"])
                op("dve", lambda e, x=x, xh=xh, xl=xl: e.tensor_tensor(
                    xl, x[:, bass.ds(j.value(), 1), :].squeeze(1) if j.loop else x[:, j.c, :], r32(xh),
                    ALU.subtract), after=[(A_["qkhi"], j.of(2, i))], signal=A_["qklo"])

        def scores(j):
            for hd in range(2):
                r = slice(hd * HD, (hd + 1) * HD)

                def emit(e, r=r, hd=hd):
                    for t in range(T):
                        dst = bank[4 + hd][:, off[t]:off[t] + widths[t]]
                        for i, (q_, k_) in enumerate(((q_hi, k_hi), (q_hi, k_lo), (q_lo, k_hi))):
                            mm = e.matmul(dst, q_[r, t * P:(t + 1) * P], k_[r, 0:widths[t]], start=(i == 0),
                                          stop=(i == 2))
                    return mm
                op("pe", emit, after=[(A_["qklo"], j.of(2, 1))] + prev(A_["tm"], j, 4, 2 * hd - 3),
                   signal=A_["s"])

        def mask_and_max(j, hd):
            op("dve", lambda e: e.memset(waited, 0.0),
               after=[(A_["s"], j.of(2, hd))] + prev(A_["tr"], j, 2, hd - 2) +
               ([(A_["msk"], j)] if stage_mask else ready))
            for t in range(T):
                m = masks(hd, t)
                sl = slice(off[t], off[t] + widths[t])
                c = 2 * hd + t
                op("dve", lambda e, m=m, sl=sl, c=c: e.tensor_tensor_reduce(
                    pp[hd][:, sl], bank[4 + hd][:, sl], m, 1.0, NEG, ALU.add, ALU.max, mx[:, c:c + 1]),
                   signal=A_["tm"])
            c = slice(2 * hd, 2 * hd + 2)
            done = [(A_["tm"], j.of(4, 2 * hd + 1))]
            if sinks:
                def sink_of(e):
                    s_ = sink[:, bass.ds(j.of(2, hd).value(), 1)] if j.loop else sink[:, j.c * 2 + hd:j.c * 2 + hd + 1]
                    return s_
                op("dve", lambda e: e.tensor_scalar(mx[:, c], mx[:, c], sink_pair[:, hd:hd + 1], None, ALU.max),
                   after=done + [(A_["sx"], j)], signal=A_["sd"])
                done = [(A_["sd"], j.of(4, 2 * hd))]
                op("dve", lambda e: e.tensor_scalar(sd[:, c], mx[:, c], -1.0, sink_pair[:, hd:hd + 1], ALU.mult,
                                                    ALU.add),
                   after=done + prev(A_["es"], j, 1, -1), signal=A_["sd"])
            op("dve", lambda e: e.tensor_scalar(nm[:, c], mx[:, c], -1.0, None, ALU.mult),
               after=done + prev(A_["ex"], j, 2, hd - 2), signal=A_["nm"])

        def exps(j, hd):
            for t in range(T):
                sl = slice(off[t], off[t] + widths[t])
                c = 2 * hd + t
                op("act", lambda e, sl=sl, c=c: e.activation(pp[hd][:, sl], pp[hd][:, sl], ACT.Exp,
                                                             bias=nm[:, c:c + 1], accum_out=sm[:, c:c + 1]),
                   after=[(A_["nm"], j.of(2, hd))], signal=A_["ex"] if t == T - 1 else None)
            if sinks and hd == 1:
                op("act", lambda e: e.activation(es, sd, ACT.Exp), after=[(A_["sd"], j.of(4, 3))],
                   signal=A_["es"])

        def turn_weights(j):
            for hd in range(2):
                def emit(e, hd=hd):
                    for i, (t, kt) in enumerate(tiles):
                        a = off[t] + kt * P
                        tr = e.transpose(bank[6 + hd][:, i * P:(i + 1) * P], pp[hd][:, a:a + P], ident)
                    return tr
                op("pe", emit, after=[(A_["ex"], j.of(2, hd))] + prev(A_[f"pt{hd}"], j, 1, -1),
                   signal=A_["tr"])

        def copy_turned(j, hd):
            n = len(tiles) * P
            after = [(A_["tr"], j.of(2, hd))] + prev(A_["pv"], j, 1, -1)
            if hd:
                op("act", lambda e: e.activation(pt[hd][:, 0:n], bank[6 + hd][:, 0:n], ACT.Copy), after=after,
                   signal=A_["pt1"])
            else:
                op("dve", lambda e: e.tensor_copy(pt[hd][:, 0:n], bank[6 + hd][:, 0:n]), after=after,
                   signal=A_["pt0"])

        def apply_weights(j):
            def emit(e):
                for hd in range(2):
                    for t in range(T):
                        mine = [(i, kt) for i, (tt, kt) in enumerate(tiles) if tt == t]
                        for m, (i, kt) in enumerate(mine):
                            src = v[:, kt, bass.ds(j.of(P, hd * HD).value(), HD)] if j.loop else \
                                v[:, kt, j.c * P + hd * HD:j.c * P + (hd + 1) * HD]
                            mm = e.matmul(bank[0][:, (2 * hd + t) * HD:(2 * hd + t + 1) * HD],
                                          pt[hd][:, i * P:(i + 1) * P], src, start=(m == 0),
                                          stop=(m == len(mine) - 1))
                return mm
            op("pe", emit, after=[(A_["pt0"], j), (A_["pt1"], j)] + prev(A_["o"], j, 1, -1) + ready,
               signal=A_["pv"])

        def recips(j):
            done = [(A_["ex"], j.of(2, 1))]
            if sinks:
                op("dve", lambda e: e.tensor_tensor(sm, sm, es, ALU.add), after=done + [(A_["es"], j)],
                   signal=A_["sa"])
                done = [(A_["sa"], j)]
            op("dve", lambda e: e.reciprocal(rc, sm), after=done + prev(A_["o"], j, 1, -1), signal=A_["rc"])

        def store_o(j):
            def emit(e):
                dst = o[:, bass.ds(j.value(), 1), :, :].squeeze(1) if j.loop else o[:, j.c, :, :]
                return e.tensor_tensor(dst.rearrange("p t (h d) -> p h t d", h=2),
                                       bank[0][:, 0:4 * HD].rearrange("p (h t d) -> p h t d", h=2, t=2),
                                       bcast(rc, [2, 2], [1, 2], [0, HD]), ALU.mult)
            op("dve", emit, after=[(A_["pv"], j), (A_["rc"], j), (A_["qklo"], j.of(2, 1))], signal=A_["o"])

        if sinks:
            A_["sa"] = Series(nc, f"{name}_sa")
        sink_pair = tiny2

        def side(j):
            if stage_mask:
                op("pool", lambda e: stage_mask(e, j), after=prev(A_["tm"], j, 4, -1) + ready, signal=A_["msk"])
            if sinks:
                op("pool", lambda e: e.tensor_copy(sink_pair, sink[:, bass.ds(j.of(2).value(), 2)] if j.loop
                                                   else sink[:, 2 * j.c:2 * j.c + 2]),
                   after=prev(A_["sd"], j, 4, -1) + [has("sink")], signal=A_["sx"])

        def turn(j, more):
            side(j)
            scores(j)
            before = j.of(1, -1)
            have_before = j.loop is not None or j.c > 0
            if have_before:
                recips(before)
                turn_weights(before)
            if more:
                split_qk_act(j.of(1, 1))
            if have_before:
                copy_turned(before, 1)
            mask_and_max(j, 0)
            exps(j, 0)
            if have_before:
                copy_turned(before, 0)
            mask_and_max(j, 1)
            exps(j, 1)
            if more:
                split_qk_dve(j.of(1, 1))
            if have_before:
                apply_weights(before)
                store_o(before)

        def split_qk_act(j):
            q = plan.queues["dve"]
            k = len(q)
            split_qk(j)
            held.extend(q[k:])
            del q[k:]

        def split_qk_dve(j):
            plan.queues["dve"].extend(held)
            held.clear()
        held = []

        split_qk(Step(0))
        turn(Step(0), True)
        steps(plan, 1, pairs - 2, 1, lambda j: turn(j, True))
        turn(Step(pairs - 1), False)
        last = Step(pairs - 1)
        recips(last)
        turn_weights(last)
        copy_turned(last, 1)
        copy_turned(last, 0)
        apply_weights(last)
        store_o(last)
        b = mix_hi.claim(pairs // 2)
        assert mix_lo.claim(pairs // 2) == b
        for m in range(pairs // 2):
            dst = bank[4 + m]

            def emit(e, m=m, dst=dst):
                for i in range(4):
                    tr = e.transpose(dst[:, i * P:(i + 1) * P], o[:, 2 * m + i // 2, i % 2, :], ident)
                return tr
            op("pe", emit, after=[(A_["o"], 2 * m + 1), (A_["pt0"], pairs - 1), (A_["pt1"], pairs - 1)],
               name=f"{name}_oT{m}")
            op("act", lambda e, m=m, dst=dst: e.activation(xT_hi[:, 2 * m:2 * m + 2, :], pair(dst), ACT.Copy),
               after=[f"{name}_oT{m}"], signal=mix_hi)
            op("dve", lambda e, m=m, dst=dst: e.tensor_tensor(xT_lo[:, 2 * m:2 * m + 2, :], pair(dst),
                                                              r32(xT_hi[:, 2 * m:2 * m + 2, :]), ALU.subtract),
               after=[(mix_hi, b + m)], signal=mix_lo)
        return b

    tiny2 = sb("sink_pair", [P, 2])
    waited = sb("waited", [P, 1])

    TOTAL = 4 + 8 + 4 + 2 * (D_FF // 256) + 8 + 4 + 2 * (D_FF // 256) + 3 * (D_FF_2 // 256) + 5 + 4 \
        + 3 * (D_FF_2 // 256)

    for n in range(LOOK):
        split_piece(n)
    turn_h("L0", gain("norm_mix0"), x_at=40)
    ER, FAR = 384, 2 * MAX_REL
    table, er = at(2, FAR + 1), at(4, ER)
    load("rel", table[0:N_HEADS, :], A["rel"], engine="pool")
    op("dve", lambda e: e.tensor_copy(er[0:N_HEADS, 0:FAR], table[0:N_HEADS, 1:FAR + 1]), after=[has("rel")],
       name="er_near")
    op("dve", lambda e: e.tensor_copy(er[0:N_HEADS, FAR:ER], bcast(table[0:N_HEADS, FAR:FAR + 1], [0, ER - FAR])),
       name="er_far")
    er_dram = nc.dram_tensor("er_scratch", [N_HEADS, ER], F32, kind="Internal").ap()
    er_out = Series(nc, "er_out", 16)
    op("pool", lambda e: e.dma_start(er_dram, er[0:N_HEADS, :]), after=["er_far"], signal=er_out)
    bias, falling = at(8, N_HEADS, S), at(24, N_HEADS, S)
    load("bias", falling, bass.AP(tensor=er_dram.tensor, offset=0, ap=[[1, P], [ER, N_HEADS], [1, S]]), engine="pool",
         after=[(er_out, 0)])
    op("pool", lambda e: e.tensor_copy(bias, falling[:, :, ::-1]), after=[has("bias")], name="bias_rising")
    op("pool", lambda e: e.memset(bias[0:CHUNK, :, S - CHUNK:], NEG), after=["bias_rising"], name="bias")
    load("gate_a", gate_w[:, 0], A["w_ga"].rearrange("n c e -> c n e"), engine="pool")
    load("gate_x", gate_w[:, 1], A["w_gx"].rearrange("n c e -> c n e"), engine="pool")
    load("pool_w", pool_w, A["pool_w"].rearrange("n c e -> c n e"), engine="pool")
    load("sink", sink, bass.AP(tensor=A["sink"].tensor, offset=A["sink"].offset, ap=[[0, P], [1, HEADS_2]]),
         engine="pool")

    sp = [at(6 + i / 16, KB) for i in range(6)]
    a_ = cols[:, col_at["a_param"]:col_at["a_param"] + KB]
    spp, spn, gg = extra[:, 0:KB], extra[:, KB:2 * KB], extra[:, 2 * KB:]
    chain = []

    def small(fn, extra_after=()):
        prior = [chain[-1]] if chain else ["cols"]
        chain.append(f"sp{len(chain)}")
        op("dve", fn, after=prior + list(extra_after), name=chain[-1])

    small(lambda e: e.tensor_scalar(sp[0], a_, -1.0, None, ALU.mult))
    small(lambda e: e.tensor_tensor(sp[1], a_, sp[0], ALU.min))
    op("act", lambda e: e.activation(sp[2], sp[1], ACT.Exp), after=[chain[-1]], name="sp_exp")
    small(lambda e: e.tensor_scalar(sp[3], sp[2], 2.0, None, ALU.add), ["sp_exp"])
    small(lambda e: e.reciprocal(sp[4], sp[3]))
    small(lambda e: e.tensor_tensor(sp[3], sp[2], sp[4], ALU.mult))
    small(lambda e: e.tensor_tensor(sp[4], sp[3], sp[3], ALU.mult))
    TERMS = 9
    small(lambda e: e.tensor_scalar(sp[5], sp[4], 1.0 / (2 * TERMS + 1), 1.0 / (2 * TERMS - 1), ALU.mult, ALU.add))
    for m in range(TERMS - 2, -1, -1):
        small(lambda e: e.tensor_tensor(sp[5], sp[5], sp[4], ALU.mult))
        small(lambda e, m=m: e.tensor_scalar(sp[5], sp[5], 1.0 / (2 * m + 1), None, ALU.add))
    small(lambda e: e.tensor_tensor(sp[5], sp[5], sp[3], ALU.mult))
    small(lambda e: e.tensor_scalar(sp[0], sp[0], 0.0, None, ALU.max))
    small(lambda e: e.scalar_tensor_tensor(out=sp[5], in0=sp[5], scalar=2.0, in1=sp[0], op0=ALU.mult, op1=ALU.add))
    small(lambda e: e.tensor_scalar(spp, sp[5], 8.0, None, ALU.mult))
    small(lambda e: e.tensor_scalar(spn, sp[5], -8.0, None, ALU.mult))
    small(lambda e: e.tensor_tensor(gg, cols[:, col_at["norm_final"]:col_at["norm_final"] + KB],
                                    cols[:, col_at["ffn1_norm"]:col_at["ffn1_norm"] + KB], ALU.mult))

    w_qkv = A["w_qkv"]
    qT, kT, v = at(24, KB, S), at(32, KB, S), None
    j0 = len(norms)
    acc0 = project("v", w_qkv[:, 2 * D:3 * D], range(4),
                   lambda i: [(xlo_done, 2 * T * j0 - 2 + i // 2)])
    v = vbuf = sb("v", [P, T, D])
    for t in range(T):
        for half in range(2):
            op("act", lambda e, t=t, half=half: e.activation(v[:, t, half * 512:(half + 1) * 512], acc[t][half],
                                                             ACT.Copy, scale=rstd[:, t:t + 1]),
               after=[acc0[t], f"L0_r{t}"], name=f"v{t}{half}")
    spread_rms("L0")
    n0, b_zt = Stream.n, z_t.claim(8)
    for p in range(8):
        dst = bank[4 + p % 3]
        load_piece(n0 + p, u_src(w_qkv, Step(p * 2 * P)), "U")
        u_piece(n0 + p, dst, after=[(z_t, b_zt + p - 3)] if p >= 3 else [])
        split_piece(n0 + p + LOOK)
        to = (qT if p < 4 else kT)[:, 2 * (p % 4):2 * (p % 4) + 2, :]
        op("dve", lambda e, to=to, dst=dst, p=p: e.scalar_tensor_tensor(
            out=to, in0=pair(dst), scalar=QSCALE if p < 4 else 1.0, in1=rms_pair(), op0=ALU.mult, op1=ALU.mult),
           after=[(used, n0 + p), "L0_rms"] + ([chain[-1], "bias_rising"] if p == 0 else []), signal=z_t)
    Stream.n += 8
    stage = sb("stage", [P, 2, S])

    def stage_bias(e, j):
        src = bias[:, bass.ds(j.of(2).value(), 2), :] if j.loop else bias[:, 2 * j.c:2 * j.c + 2, :]
        return e.tensor_copy(stage, src)

    pp = [at(0, 384), at(1.5, 384)]
    pt = [at(3, 384), at(4.5, 384)]
    mb = attention("a1", KB, [P, S], lambda hd, t: stage[:, hd, S - [P, S][t]:], qT, kT, v,
                   o=qT.rearrange("p j (t c) -> p j t c", t=T), pt=pt, pp=pp,
                   ready=[(z_t, b_zt + 7), "v11", "bias", "L0_ss1"],
                   stage_mask=stage_bias)
    a0 = project("wo", A["w_o"], range(4), lambda i: [(mix_lo, mb + i)])
    turn_h("M0", gain("norm_mlp0"), a0)
    a0 = feed_forward("M0", [A["w1"][0]], A["w2"][0], D_FF)

    turn_h("L1", gain("norm_mix1"), a0)
    BP = S + CONV - 1
    xb, xc, rr, nt = at(4, KB, BP), at(13, KB, S), at(21, KB, S), at(29, KB, S)
    ig, sq = [at(37 + i, S) for i in range(2)], [at(39 + i, S) for i in range(2)]
    bo = at(41, D)
    load("b_o", bo, bass.AP(tensor=A["b_o"].tensor, offset=A["b_o"].offset, ap=[[0, P], [1, D]]), after=["L1_h11"])
    for t in range(T):
        op("pool", lambda e, t=t: e.tensor_tensor(h[:, t, :], h[:, t, :], bo, ALU.add),
           after=[has("b_o"), (turned, 2 * T * len(norms) - 1), f"L1_ss{t}"], name=f"h_bo{t}")
    op("pool", lambda e: e.memset(xb[:, :, 0:CONV - 1], 0.0), after=["L1_ss1", (xlo_done, 2 * T * len(norms) - 1)],
       name="conv_pad")
    w_in = A["w_in"]
    n0, b_zt, j1 = Stream.n, z_t.claim(8), len(norms)

    def x_pair(p):
        dst = bank[4 + p % 3]
        op("dve", lambda e: e.tensor_tensor(xb[:, 2 * p:2 * p + 2, CONV - 1:], pair(dst), rms_pair(), ALU.mult),
           after=[(used, n0 + p), "L1_rms", "L1_ss1"], signal=z_t)
        for n in (2 * p, 2 * p + 1):
            op("pool", lambda e, n=n: e.tensor_scalar(xb[:, n, CONV - 1:], xb[:, n, CONV - 1:], col("b_in", n), None,
                                                      ALU.add), after=[(z_t, b_zt + p)], name=f"x{n}")
        for n in (2 * p, 2 * p + 1):
            op("dve", lambda e, n=n: e.tensor_scalar(xc[:, n, :], xb[:, n, 0:S], col("conv_w", n), col("conv_b", n),
                                                     ALU.mult, ALU.add), after=[f"x{n}", "conv_pad"],
               name=f"conv{n}_0")
            for tap in range(1, CONV):
                op("dve", lambda e, n=n, tap=tap: e.scalar_tensor_tensor(
                    out=xc[:, n, :], in0=xb[:, n, tap:tap + S], scalar=col("conv_w", tap * KB + n), in1=xc[:, n, :],
                    op0=ALU.mult, op1=ALU.add), after=[f"conv{n}_{tap - 1}"], name=f"conv{n}_{tap}")

    def gates(n):
        dst = bank[n % 4]

        def emit(e):
            e.matmul(dst[:, 0:S], gate_w[:, 0, n, :], xc[:, n, :], start=True, stop=True)
            return e.matmul(dst[:, S:2 * S], gate_w[:, 1, n, :], xc[:, n, :], start=True, stop=True)
        op("pe", emit, after=[f"conv{n}_{CONV - 1}", has("gate_a"), has("gate_x")] +
           ([f"ig{n - 4}"] if n >= 4 else []), name=f"gates{n}")
        op("act", lambda e: e.activation(rr[:, n, :], dst[:, 0:S], ACT.Sigmoid, bias=col("b_ga", n)),
           after=[f"gates{n}", chain[-1]], name=f"r{n}")
        op("act", lambda e: e.activation(ig[n % 2], dst[:, S:2 * S], ACT.Sigmoid, bias=col("b_gx", n)),
           after=[f"bx{n - 2}"] if n >= 2 else [], name=f"ig{n}")
        op("act", lambda e: e.activation(nt[:, n, :], rr[:, n, :], ACT.Tanh, scale=spp[:, n:n + 1]),
           after=[f"r{n}"], name=f"nt{n}")
        op("pool", lambda e: e.tensor_tensor(xc[:, n, :], xc[:, n, :], ig[n % 2], ALU.mult), after=[f"ig{n}"],
           name=f"bx{n}")

    def scan_inputs():
        for n in range(KB):
            op("act", lambda e, n=n: e.activation(rr[:, n, :], rr[:, n, :], ACT.Exp, scale=spn[:, n:n + 1]),
               after=[f"nt{n}"], name=f"a{n}")
            op("pool", lambda e, n=n: e.tensor_tensor(sq[n % 2], rr[:, n, :], rr[:, n, :], ALU.mult),
               after=[f"a{n}"] + ([f"m{n - 2}"] if n >= 2 else []), name=f"sq{n}")
            op("dve", lambda e, n=n: e.scalar_tensor_tensor(out=nt[:, n, :], in0=sq[n % 2], scalar=1.0,
                                                            in1=nt[:, n, :], op0=ALU.add, op1=ALU.mult),
               after=[f"sq{n}"], name=f"m{n}")
        for n in range(KB):
            op("act", lambda e, n=n: e.activation(nt[:, n, :], nt[:, n, :], ACT.Sqrt), after=[f"m{n}"],
               name=f"mult{n}")
            op("pool", lambda e, n=n: e.tensor_tensor(xc[:, n, :], xc[:, n, :], nt[:, n, :], ALU.mult),
               after=[f"mult{n}", f"bx{n}"], name=f"b{n}")
            op("dve", lambda e, n=n: e.tensor_tensor_scan(nt[:, n, :], rr[:, n, :], xc[:, n, :], 0.0, ALU.mult,
                                                          ALU.add), after=[f"b{n}"], name=f"hs{n}")

    def y_pair(p):
        dst = bank[[5, 6, 7, 4][p]]
        op("dve", lambda e: e.tensor_tensor(xb[:, 2 * p:2 * p + 2, 0:S], pair(dst), rms_pair(), ALU.mult),
           after=[(used, n0 + 4 + p)] + [f"conv{n}_{CONV - 1}" for n in range(2 * p, 2 * p + 2)], signal=z_t)
        for n in (2 * p, 2 * p + 1):
            op("act", lambda e, n=n: e.activation(xb[:, n, 0:S], xb[:, n, 0:S], ACT.Gelu_apprx_tanh,
                                                  bias=col("b_in", KB + n)), after=[(z_t, b_zt + 4 + p)],
               name=f"y{n}")
            op("dve", lambda e, n=n: e.tensor_tensor(xc[:, n, :], xb[:, n, 0:S], nt[:, n, :], ALU.mult),
               after=[f"y{n}", f"hs{n}"], name=f"o{n}")
            op("act", lambda e, n=n: e.activation(xT_hi[:, n, :], xc[:, n, :], ACT.Copy),
               after=[f"o{n}", (used, n0 + 7)], signal=mix_hi)
            op("dve", lambda e, n=n: e.tensor_tensor(xT_lo[:, n, :], xc[:, n, :], r32(xT_hi[:, n, :]), ALU.subtract),
               after=[(mix_hi, mbr + n)], signal=mix_lo)

    mbr = mix_hi.claim(KB)
    assert mix_lo.claim(KB) == mbr

    def rec_piece(m):
        load_piece(n0 + m, u_src(w_in, Step(m * 2 * P)), "U")
        after = [(z_t, b_zt + m - 3)] if m == 3 else []
        u_piece(n0 + m, bank[4 + m % 3] if m < 4 else bank[[5, 6, 7, 4][m - 4]], after=after +
                ([(z_t, b_zt + {4: 1, 5: 2, 6: 2, 7: 3}[m])] if m >= 4 else []) +
                (["L1_rms"] if m == 6 else []),
                after_k=x_block_ready(j1) if m == 0 else None)
        split_piece(n0 + m + LOOK)
    rec_piece(0)
    spread_rms("L1")
    rec_piece(1)
    x_pair(0)
    rec_piece(2)
    x_pair(1)
    gates(0), gates(1)
    rec_piece(3)
    x_pair(2)
    gates(2), gates(3)
    rec_piece(4)
    x_pair(3)
    gates(4), gates(5)
    rec_piece(5)
    gates(6), gates(7)
    rec_piece(6)
    rec_piece(7)
    scan_inputs()
    for p in range(4):
        y_pair(p)
    Stream.n += 8
    a0 = project("rec_wo", A["rec_w_o"], range(4), lambda i: [(mix_lo, mbr + 2 * i + 1)])
    turn_h("M1", gain("norm_mlp1"), a0)
    nf = at(8, D)
    load("norm_final", nf, bass.AP(tensor=A["norm_final"].tensor, offset=A["norm_final"].offset,
                                   ap=[[0, P], [1, D]]), after=["M1_h11"])
    a0 = feed_forward("M1", [A["w1"][1]], A["w2"][1], D_FF)

    turn_h("F1", gg, a0, between=nf)
    a0 = feed_forward("F1", [A["f1_gate"], A["f1_up"]], A["f1_down"], D_FF_2)

    turn_h("X", gain("mix_norm"), a0, scale=0.5)
    q2, k2, v2 = at(24, 4, S), at(28, 4, S), vbuf.rearrange("p t (a b) -> p t a b", a=2)[:, :, 0, :]
    cs_t, mats, mask2 = at(18, 2, S), at(20, 5, P), at(32, T, S)
    pc, csum, dd = at(4, PG, S), at(8, 9 * 32 + 3)[:, 0:S + 17], [at(10 + i, S) for i in range(2)]
    inv, kv = at(36, PG, 2, S), at(12, 2 * S)
    qf, tq = at(14, 2 * S), at(16, 2 * S)
    load("tables", cs_t, A["rope"], after=["X_h11"])
    load("mats", mats, A["mats"], after=["X_h11"])
    load("mask2", mask2, A["mask2"], after=["X_h11"])
    load("inv", inv.rearrange("p g w s -> p (g w s)"),
         bass.AP(tensor=A["inv"].tensor, offset=A["inv"].offset, ap=[[0, P], [1, PG * 2 * S]]), after=["X_h11"])
    w2_in = A["w_in2"]
    j2, n0, b_zt = len(norms), Stream.n, z_t.claim(5)
    first_col = [768, 1024, 512, 0, 256]

    def mix_piece(m):
        load_piece(n0 + m, u_src(w2_in, Step(first_col[m])), "U")
        u_piece(n0 + m, bank[4 + m % 3], after=[(z_t, b_zt + m - 3)] if m >= 3 else [],
                after_k=x_block_ready(j2) if m == 0 else None)
        split_piece(n0 + m + LOOK)

    def leave(m, dst, scale=1.0, after=()):
        op("dve", lambda e: e.scalar_tensor_tensor(out=dst, in0=pair(bank[4 + m % 3]), scalar=scale, in1=rms_pair(),
                                                   op0=ALU.mult, op1=ALU.mult),
           after=[(used, n0 + m), "X_rms", "X_ss1"] + list(after), signal=z_t)

    op("pool", lambda e: e.memset(csum[:, 0:9], 0.0), after=["X_ss1", (xlo_done, 2 * T * len(norms) - 1)], name="csum0")

    def pool_group(g):
        half = POOL_WINDOWS[g] // 2
        op("dve", lambda e: e.tensor_tensor_scan(csum[:, 9:9 + S], ones, pc[:, g, :], 0.0, ALU.mult, ALU.add),
           after=[(z_t, b_zt + g // 2), "csum0"] + ([f"d{g - 1}_2"] if g else []), name=f"cs{g}_0")
        op("dve", lambda e: e.tensor_copy(csum[:, 9 + S:17 + S], bcast(csum[:, 8 + S:9 + S], [0, 8])),
           after=[f"cs{g}_0"], name=f"cs{g}_1")
        for w in range(2):
            a, b = 8 - half + w, 8 + half + w
            op("pool", lambda e, a=a, b=b, w=w: e.tensor_tensor(dd[w], csum[:, b:b + S], csum[:, a:a + S],
                                                                ALU.subtract),
               after=[f"cs{g}_1"] + ([f"pool{g - 1}"] if g else []), name=f"d{g}_{1 + w}")
            op("pool", lambda e, w=w: e.tensor_tensor(dd[w], dd[w], inv[:, g, w, :], ALU.mult),
               after=[has("inv"), f"d{g}_{1 + w}"], name=f"e{g}_{w}")
        op("pool", lambda e: e.tensor_tensor(dd[0], dd[0], dd[1], ALU.add), after=[f"e{g}_0", f"e{g}_1"],
           name=f"mean{g}")
        op("pool", lambda e: e.tensor_tensor(pc[:, g, :], dd[0], pc[:, g, :], ALU.subtract), after=[f"mean{g}"],
           name=f"pool{g}")

    def pool_product(g):
        op("pe", lambda e: e.matmul(bank[2 + g // 2][:, (g % 2) * S:(g % 2 + 1) * S], pool_w[:, g, :], pc[:, g, :],
                                    start=True, stop=True), after=[f"pool{g}", has("pool_w")], name=f"pool_y{g}")

    cos, sin = cs_t[:, 0, :], cs_t[:, 1, :]

    def two(ap):
        return bcast(ap, [0, 2], [1, S])

    mix_piece(0)
    spread_rms("X")
    mix_piece(1)
    leave(0, pc[:, 0:2, :])
    pool_group(0), pool_group(1)
    mix_piece(2)
    leave(1, pc[:, 2:4, :])
    pool_group(2), pool_group(3)
    mix_piece(3)
    leave(2, pair(kv))
    pool_product(0), pool_product(1)
    for g in range(KV_2):
        def emit(e, g=g):
            e.matmul(bank[g][:, 0:S], mats[:, 1 + 2 * g, :], kv[:, 0:S], start=True, stop=True)
            return e.matmul(bank[g][:, S:2 * S], mats[:, 2 + 2 * g, :], kv[:, 0:S], start=True, stop=True)
        op("pe", emit, after=[(z_t, b_zt + 2), has("mats")], name=f"k_rot{g}")
    for t in range(T):
        op("pe", lambda e, t=t: e.transpose(bank[7][:, t * P:(t + 1) * P], kv[:, S + t * P:S + (t + 1) * P], ident),
           after=["X_rms"], name=f"v_turn{t}")
    for t in range(T):
        for g in range(KV_2):
            op("act", lambda e, t=t, g=g: e.activation(
                v2[:, t, g * 4 * HD:(g + 1) * 4 * HD].rearrange("p (r d) -> p r d", d=HD),
                bcast(bank[7][:, t * P + g * HD:t * P + (g + 1) * HD], [0, 4], [1, HD]), ACT.Copy),
               after=["v_turn1"], name=f"v2_{t}{g}")
    for g in range(KV_2):
        op("dve", lambda e, g=g: e.tensor_tensor(tq[:, 0:S], bank[g][:, 0:S], cos, ALU.mult),
           after=[f"k_rot{g}", has("tables")] + ([f"k2_{g - 1}"] if g else []), name=f"kc{g}")
        op("dve", lambda e, g=g: e.tensor_tensor(tq[:, S:2 * S], bank[g][:, S:2 * S], sin, ALU.mult), name=f"ks{g}")
        op("dve", lambda e, g=g: e.tensor_tensor(k2[:, 2 * g:2 * g + 2, :], two(tq[:, 0:S]), two(tq[:, S:2 * S]),
                                                 ALU.add), after=[f"kc{g}", f"ks{g}"], name=f"k2_{g}")

    def rope_q(m):
        i = m - 3
        leave(m, pair(qf), scale=QSCALE, after=["k2_1"] if i == 0 else ["q2_0", "qsin0"])
        op("pe", lambda e: e.matmul(bank[i], mats[:, 0, :], qf, start=True, stop=True),
           after=[(z_t, b_zt + m), "k2_1"], name=f"q_rot{i}")
        op("dve", lambda e: e.tensor_tensor(q2[:, 2 * i:2 * i + 2, :], pair(qf), two(cos), ALU.mult),
           after=[(z_t, b_zt + m)], name=f"qcos{i}")
        op("dve", lambda e: e.tensor_tensor(pair(tq), pair(bank[i]), two(sin), ALU.mult), after=[f"q_rot{i}"],
           name=f"qsin{i}")
        op("dve", lambda e: e.tensor_tensor(q2[:, 2 * i:2 * i + 2, :], q2[:, 2 * i:2 * i + 2, :], pair(tq), ALU.add),
           after=[f"qcos{i}", f"qsin{i}"], name=f"q2_{i}")
    mix_piece(4)
    pool_product(2), pool_product(3)
    rope_q(3)
    rope_q(4)
    mp = mix_hi.claim(PG)
    assert mix_lo.claim(PG) == mp
    for g in range(PG):
        src = bank[2 + g // 2][:, (g % 2) * S:(g % 2 + 1) * S]
        op("act", lambda e, g=g, src=src: e.activation(xT_hi[:, 4 + g, :], src, ACT.Copy, scale=col("pool_scale", g)),
           after=[f"pool_y{g | 1}", (used, n0 + 4)], signal=mix_hi)
        op("dve", lambda e, g=g, src=src: e.scalar_tensor_tensor(
            out=xT_lo[:, 4 + g, :], in0=src, scalar=col("pool_scale", g), in1=r32(xT_hi[:, 4 + g, :]), op0=ALU.mult,
            op1=ALU.subtract), after=[(mix_hi, mp + (g | 1))], signal=mix_lo)
    Stream.n += 5
    pp2 = [at(36, 2 * S), at(38, 2 * S)]
    pt2 = [at(40, 2 * S), at(42, 2 * S)]
    ma = attention("a2", HEADS_2 // 2, [S, S], lambda hd, t: mask2[:, t, :], q2, k2, v2,
                   o=q2.rearrange("p j (t c) -> p j t c", t=T), pt=pt2, pp=pp2,
                   ready=["q2_1", "v2_11", has("mask2"), "pool3"], sinks=True)
    a0 = project("w_out", A["w_out"], [2, 3, 0, 1],
                 lambda i: [(mix_lo, mp + 2 * (i - 2) + 1)] if i >= 2 else [(mix_lo, ma + i)])
    turn_h("F2", gain("ffn2_norm"), a0)
    load("norm_last", nf, bass.AP(tensor=A["norm_last"].tensor, offset=A["norm_last"].offset,
                                  ap=[[0, P], [1, D]]), after=["F2_h11"])
    a0 = feed_forward("F2", [A["f2_gate"], A["f2_up"]], A["f2_down"], D_FF_2, straight=2)
    assert Stream.n == TOTAL, (Stream.n, TOTAL)
    junk, res = at(12, D), at(16, T, D)
    out_done = Series(nc, "out_done", 16)
    for t in range(T):
        for half in range(2):
            hh = h[:, t, half * 512:(half + 1) * 512]
            op("dve", lambda e, hh=hh, a=acc[t][half]: e.scalar_tensor_tensor(
                out=hh, in0=a, scalar=0.5, in1=hh, op0=ALU.mult, op1=ALU.add), after=[a0[t]],
               name=f"last_h{t}{half}")
        op("act", lambda e, t=t: e.activation(junk, h[:, t, :], ACT.Square, accum_out=ssq[:, t:t + 1]),
           after=[f"last_h{t}0", f"last_h{t}1"] + ([f"last_ss{t - 1}"] if t else []), name=f"last_ss{t}")
        make_rstd(f"last_r{t}", t, f"last_ss{t}")
    for t in range(T):
        op("dve", lambda e, t=t: e.scalar_tensor_tensor(out=res[:, t, :], in0=h[:, t, :], scalar=rstd[:, t:t + 1],
                                                        in1=nf, op0=ALU.mult, op1=ALU.mult),
           after=[f"last_r{t}", has("norm_last")], name=f"last{t}")
        op("sp", lambda e, t=t: e.dma_start(out[t * P:(t + 1) * P, :], res[:, t, :]), after=[f"last{t}"],
           signal=out_done)
    op("sp", lambda e: e.nop(), after=[(out_done, T - 1), (er_out, 0)])

    with nc.Block() as block:
        @block.sync
        def _(e):
            plan.write("sp", e)

        @block.scalar
        def _(e):
            plan.write("act", e)

        @block.vector
        def _(e):
            plan.write("dve", e)

        @block.gpsimd
        def _(e):
            plan.write("pool", e)

        @block.tensor
        def _(e):
            plan.write("pe", e)


def shape_constants():
    f = np.float32
    freq = f(THETA) ** (-np.arange(0, ROT, 2, dtype=f) / f(ROT))
    ang = np.arange(S, dtype=f)[:, None] * freq[None, :]
    ang = np.concatenate([ang, ang], axis=-1).T
    rope = np.zeros((P, 2, S), f)
    rope[:, 0] = 1.0
    rot = np.zeros((HD, HD), f)
    for d in range(ROT // 2):
        rot[d + ROT // 2, d] = -1.0
        rot[d, d + ROT // 2] = 1.0
    for head in range(P // HD):
        rope[head * HD:head * HD + ROT, 0] = np.cos(ang)
        rope[head * HD:head * HD + ROT, 1] = np.sin(ang)
    mats = np.zeros((P, 5, P), f)
    for a in range(2):
        s = slice(a * HD, (a + 1) * HD)
        mats[s, 0, s] = rot
        for g in range(KV_2):
            mats[g * HD:(g + 1) * HD, 1 + 2 * g, s] = np.eye(HD, dtype=f)
            mats[g * HD:(g + 1) * HD, 2 + 2 * g, s] = rot
    qpos = np.arange(T)[None, :, None] * P + np.arange(P)[:, None, None]
    kpos = np.arange(S)[None, None, :]
    mask = np.where(np.abs(qpos - kpos) <= WINDOW, 0.0, NEG).astype(f)
    t = np.arange(S)
    inv = np.zeros((PG, 2, S), f)
    for g, w in enumerate(POOL_WINDOWS):
        for i in range(2):
            lo, hi = np.clip(t - w // 2 + i, 0, S), np.clip(t + w // 2 + i, 0, S)
            inv[g, i] = 0.5 / (hi - lo)
    return {"rope": rope, "mats": mats, "mask2": mask, "inv": inv}


def kernel(**inputs):
    import concourse.bacc as bacc
    from concourse.bass_utils import run_bass_kernel_spmd

    def flat(name, *shape):
        return np.ascontiguousarray(inputs[name]).reshape(shape)

    nm, nl, conv = inputs["norm_mix"], inputs["norm_mlp"], inputs["rec_conv_w"]
    arrays = {
        "x": flat("x", S, D), "norm_mix0": np.ascontiguousarray(nm[0]), "norm_mix1": np.ascontiguousarray(nm[1]),
        "norm_mlp0": np.ascontiguousarray(nl[0]), "norm_mlp1": np.ascontiguousarray(nl[1]),
        "norm_final": flat("norm_final", D), "w_qkv": flat("attn_w_qkv", D, 3 * D), "w_o": flat("attn_w_o", D, D),
        "rel": flat("attn_rel_bias", N_HEADS, 2 * MAX_REL + 1), "w_in": flat("rec_w_in", D, 2 * D),
        "b_in": flat("rec_b_in", 2 * D), "conv_w": flat("rec_conv_w", CONV * D), "conv_b": flat("rec_conv_b", D),
        "w_ga": flat("rec_w_ga", KB, P, P), "b_ga": flat("rec_b_ga", D), "w_gx": flat("rec_w_gx", KB, P, P),
        "b_gx": flat("rec_b_gx", D), "a_param": flat("rec_a_param", D), "rec_w_o": flat("rec_w_o", D, D),
        "b_o": flat("rec_b_o", D), "w1": flat("mlp_w1", 2, D, D_FF), "w2": flat("mlp_w2", 2, D_FF, D),
        "ffn1_norm": flat("ffn1_norm_2", D), "f1_gate": flat("ffn1_w_gate_2", D, D_FF_2),
        "f1_up": flat("ffn1_w_up_2", D, D_FF_2), "f1_down": flat("ffn1_w_down_2", D_FF_2, D),
        "mix_norm": flat("mix_norm_2", D), "w_in2": flat("w_in_2", D, 1280), "sink": flat("sink_logits_2", HEADS_2),
        "pool_w": flat("pool_w_2", PG, P, P), "pool_scale": flat("pool_scale_2", PG * P),
        "w_out": flat("w_out_2", D, D), "ffn2_norm": flat("ffn2_norm_2", D),
        "f2_gate": flat("ffn2_w_gate_2", D, D_FF_2), "f2_up": flat("ffn2_w_up_2", D, D_FF_2),
        "f2_down": flat("ffn2_w_down_2", D_FF_2, D), "norm_last": flat("final_norm_2", D),
    }
    arrays.update(shape_constants())
    nc = bacc.Bacc("TRN2", target_bir_lowering=False, num_devices=1)
    A = {k: nc.dram_tensor(f"in_{k}", a.shape, F32, kind="ExternalInput").ap() for k, a in arrays.items()}
    out = nc.dram_tensor("out", (1, S, D), F32, kind="ExternalOutput").ap()
    build(nc, A, out[0])
    r = run_bass_kernel_spmd(nc, [{f"in_{k}": a for k, a in arrays.items()}], core_ids=[0])
    return r.results[0]["out"]
```

```python
from contextlib import ExitStack, contextmanager

import numpy as np
import concourse.bass as bass
from concourse import mybir

F32 = mybir.dt.float32
F32R = mybir.dt.float32r
BF16 = mybir.dt.bfloat16
ACT = mybir.ActivationFunctionType
ALU = mybir.AluOpType

P = 128
S = 256
T = S // P
D = 1024
KB = D // P
EPS = 1e-6
HD = 64
QSCALE = HD ** -0.5
N_HEADS, CHUNK, MAX_REL = 16, 64, 128
CONV = 4
D_FF, D_FF_2 = 4096, 2816
HEADS_2, KV_2, WINDOW, ROT, THETA = 8, 2, 128, 16, 500000.0
POOL_WINDOWS = (2, 4, 8, 16)
PG = len(POOL_WINDOWS)
NEG = -1e30

PIECE = 2048
RING = 3
RAW = 6
LOOK = RING - 1
BODY = 6

VECTORS = [("norm_mix0", 8), ("norm_mlp0", 8), ("norm_mix1", 8), ("norm_mlp1", 8), ("norm_final", 8),
           ("ffn1_norm", 8), ("mix_norm", 8), ("ffn2_norm", 8), ("b_in", 16), ("conv_b", 8), ("b_ga", 8),
           ("b_gx", 8), ("a_param", 8), ("conv_w", 8 * CONV), ("pool_scale", PG)]


class Loop:

    def __init__(self, count):
        self.count, self.reg = count, None


class Step:

    def __init__(self, c, loop=None, per=0):
        self.c, self.loop, self.per = c, loop, per

    def of(self, mult=1, plus=0):
        return Step(self.c * mult + plus, self.loop, self.per * mult)

    def value(self):
        return self.c if self.loop is None else self.loop.reg * self.per + self.c

    def slot(self, n):
        assert self.loop is None or self.per % n == 0
        return self.c % n


def as_step(x):
    return x if isinstance(x, Step) else Step(x)


class Series:

    def __init__(self, nc, name, unit=1):
        self.sem, self.unit, self.claimed = nc.alloc_semaphore(name), unit, 0

    def claim(self, n):
        self.claimed += n
        return self.claimed - n


class Plan:

    def __init__(self, nc, engines):
        self.queues = {e: [] for e in engines}
        self.done = {e: Series(nc, f"{e}_done") for e in engines}
        self.named, self.loop_now = {}, None

    def op(self, engine, emit, after=(), name=None, signal=None):
        if name:
            assert signal is None and self.loop_now is None and name not in self.named, name
            signal = self.done[engine]
            self.named[name] = (signal, Step(signal.claim(1)))
        self.queues[engine].append((emit, list(after), signal))

    @contextmanager
    def loop(self, count):
        self.loop_now = loop = Loop(count)
        outer, self.queues = self.queues, {e: [] for e in self.queues}
        yield loop
        for e, body in self.queues.items():
            if body:
                outer[e].append((loop, body, None))
        self.queues, self.loop_now = outer, None

    def write(self, engine, e):
        self._write(e, self.queues[engine], {})

    def _write(self, e, entries, met):
        for emit, after, signal in entries:
            if isinstance(emit, Loop):
                with e.Fori(0, emit.count) as i:
                    emit.reg = i
                    self._write(e, after, dict(met))
                emit.reg = None
                continue
            for w in after:
                series, step = self.named[w] if isinstance(w, str) else w
                step = as_step(step)
                if step.loop is None:
                    need = (step.c + 1) * series.unit
                    if need <= met.get(series, 0):
                        continue
                    met[series] = need
                    e.wait_ge(series.sem, need)
                else:
                    e.wait_ge(series.sem, step.of(series.unit, series.unit).value())
            last = emit(e)
            if signal is not None:
                last.then_inc(signal.sem, signal.unit)


def steps(plan, first, count, per, body, straight=0):
    turns = (count - straight) // per
    if turns > 1:
        with plan.loop(turns) as loop:
            for k in range(per):
                body(Step(first + k, loop, per))
    else:
        turns = 0
    for k in range(first + turns * per, first + count):
        body(Step(k))


def bcast(ap, *dims):
    return bass.AP(tensor=ap.tensor, offset=ap.offset, ap=[list(ap.ap[0])] + [list(d) for d in dims])


def build(nc, A, out):
    plan = Plan(nc, ("sp", "act", "dve", "pool", "pe"))
    op = plan.op

    def sb(name, shape, dt=F32):
        return nc.alloc_sbuf_tensor(name, shape, dt)[tuple(slice(None) for _ in shape)]

    raw = [sb(f"raw{i}", [P, PIECE]) for i in range(RAW)]
    w_hi = [sb(f"w_hi{i}", [P, PIECE], F32R) for i in range(RING)]
    w_lo = [sb(f"w_lo{i}", [P, PIECE], F32R) for i in range(RING)]
    h = sb("h", [P, T, D])
    xT_hi, xT_lo = sb("xT_hi", [P, KB, S], F32R), sb("xT_lo", [P, KB, S], F32R)
    z_hi, z_lo = sb("z_hi", [P, 3, 2 * S], F32R), sb("z_lo", [P, 3, 2 * S], F32R)
    rms = sb("rms", [P, S])
    ident, ones = sb("ident", [P, P]), sb("ones", [P, S])
    zeros = sb("zeros", [P, P], BF16)
    diag = sb("diag", [P, T, P])
    rstd, ssq = sb("rstd", [P, 2 * T]), sb("ssq", [P, 2 * T])
    minus_half = sb("minus_half", [P, 1])
    ncols = sum(n for _, n in VECTORS)
    cols = sb("cols", [P, ncols])
    extra = sb("extra", [P, 4 * KB])
    gate_w = sb("gate_w", [P, 2, KB, P])
    pool_w = sb("pool_w", [P, PG, P])
    tiny = sb("tiny", [P, 6, 4])
    sink = sb("sink", [P, HEADS_2])
    work_bytes = 47 * 1024
    work = nc.alloc_sbuf_tensor("work", [P, work_bytes // 4], F32)
    bank = [nc.alloc_psum_tensor(f"bank{i}", [P, 512], F32)[:, :] for i in range(8)]
    acc = [[bank[0], bank[1]], [bank[2], bank[3]]]
    RMS_BANK = bank[7]

    def at(kib, *shape):
        n, o = int(np.prod(shape)), int(kib * 256)
        assert (o + n) * 4 <= work_bytes, (kib, shape)
        v = work[:, o:o + n]
        if len(shape) == 1:
            return v
        names = "abcd"[:len(shape)]
        return v.rearrange(f"p ({' '.join(names)}) -> p {' '.join(names)}", **dict(zip(names, shape)))

    def r32(ap):
        return ap.bitcast(F32)

    col_at, c = {}, 0
    for name, n in VECTORS:
        col_at[name], c = c, c + n

    def col(name, k):
        return cols[:, col_at[name] + k:col_at[name] + k + 1]

    def gain(name):
        return cols[:, col_at[name]:col_at[name] + KB]

    landed = [Series(nc, f"landed{i}", 16) for i in range(RAW)]
    hi_done = Series(nc, "hi_done")
    lo_done = Series(nc, "lo_done")
    used = Series(nc, "used")
    z_t = Series(nc, "z_t")
    z_g = Series(nc, "z_g")
    z_f = Series(nc, "z_f")
    zhi_done = Series(nc, "zhi_done")
    zlo_done = Series(nc, "zlo_done")
    acc_done = Series(nc, "acc_done")
    turned = Series(nc, "turned")
    x_full = Series(nc, "x_full")
    xhi_done = Series(nc, "xhi_done")
    xlo_done = [Series(nc, "xlo0_done"), Series(nc, "xlo1_done")]
    mix_hi = Series(nc, "mix_hi")
    mix_lo = Series(nc, "mix_lo")
    const_in = {}

    def load(name, dst, src, engine="pool", after=()):
        const_in[name] = Series(nc, f"in_{name}", 16)
        op(engine, lambda e: e.dma_start(dst, src), after=after, signal=const_in[name])

    def has(name):
        return (const_in[name], 0)

    class Stream:
        n = 0

    def u_src(w, cstep):
        v = w.rearrange("(k p) c -> p k c", p=P)
        return lambda: v[:, :, bass.ds(cstep.value(), 2 * P)]

    def d_src(w, rstep):
        return lambda: w[bass.ds(rstep.value(), 2 * P), :].rearrange("(k p) c -> p k c", p=P)

    def load_piece(n, src, kind):
        n, slot = as_step(n), as_step(n).slot(RAW)
        dst = raw[slot].rearrange("p (k c) -> p k c", k=KB if kind == "U" else 2)
        op("sp", lambda e: e.dma_start(dst, src()), after=[(lo_done, n.of(1, -RAW))] if free(n, RAW) else [],
           signal=landed[slot])

    def free(n, ring):
        return n.loop is not None or n.c >= ring

    def split_hi(n):
        n = as_step(n)
        s, r = n.slot(RING), n.slot(RAW)
        after = [(landed[r], Step(n.c // RAW, n.loop, n.per // RAW))]
        if free(n, RING):
            after.append((used, n.of(1, -RING)))
        op("act", lambda e: e.activation(w_hi[s], raw[r], ACT.Copy), after=after, signal=hi_done)

    def split_lo(n):
        n = as_step(n)
        s, r = n.slot(RING), n.slot(RAW)
        op("dve", lambda e: e.tensor_tensor(w_lo[s], raw[r], r32(w_hi[s]), ALU.subtract),
           after=[(hi_done, n)], signal=lo_done)

    def split_piece(n):
        if as_step(n).loop is not None or as_step(n).c < TOTAL:
            split_hi(n), split_lo(n)

    def split_now(n):
        return [(hi_done, n), (lo_done, n)]

    def u_piece(n, dst, after=(), after_k=None, between=None, freed=None):
        n, s = as_step(n), as_step(n).slot(RING)
        whi = w_hi[s].rearrange("p (k c) -> p k c", k=KB)
        wlo = w_lo[s].rearrange("p (k c) -> p k c", k=KB)

        def block(k):
            def emit(e):
                for b in range(2):
                    o = dst[:, b * S:(b + 1) * S]
                    for i, (w, x) in enumerate(((whi, xT_hi), (whi, xT_lo), (wlo, xT_hi))):
                        last = e.matmul(o, w[:, k, b * P:(b + 1) * P], x[:, k, :],
                                        start=(k == 0 and b == 0 and i == 0), stop=(k == KB - 1 and i == 2),
                                        skip_group_check=True)
                return last
            return emit
        for k in range(KB):
            op("pe", block(k), after=(list(after) + split_now(n) if k == 0 else []) + (after_k(k) if after_k else []),
               signal=used if k == KB - 1 else None, name=f"{freed}{k}" if freed and k < KB - 1 else None)
            if after_k and turn_later:
                turn_later.pop(0)()
            if between and k in between:
                between[k]()

    def d_part(n, lhs, t, kks, halves, first=False, last=False, after=(), signal=None):
        s = as_step(n).slot(RING)
        whi = w_hi[s].rearrange("p (k c) -> p k c", k=2)
        wlo = w_lo[s].rearrange("p (k c) -> p k c", k=2)

        def emit(e):
            for kk in kks:
                xhi, xlo = lhs(kk, t)
                for x, ws in ((xhi, (whi, wlo)), (xlo, (whi,))):
                    for w in ws:
                        for half in halves:
                            mm = e.matmul(acc[t][half], x, w[:, kk, half * 512:(half + 1) * 512],
                                          start=(first and kk == 0 and x is xhi and w is whi),
                                          stop=(last and kk == 1 and x is xlo), skip_group_check=True)
            return mm
        op("pe", emit, after=after, signal=signal)

    def d_piece(n, lhs, first=False, after=()):
        n = as_step(n)
        for t in range(T):
            d_part(n, lhs, t, (0, 1), (0, 1), first, after=list(after) + split_now(n) if t == 0 else (),
                   signal=used if t == T - 1 else None)

    def last_d_pieces(one, two):
        (n1, lhs1, after1), (n2, lhs2, after2) = one, two
        c = acc_done.claim(2)
        d_part(n1, lhs1, 0, (0, 1), (0, 1), after=list(after1) + split_now(n1))
        d_part(n2, lhs2, 0, (0, 1), (0, 1), last=True, after=list(after2) + split_now(n2), signal=acc_done)
        closing.extend([
            lambda: d_part(n1, lhs1, 1, (0,), (0, 1)),
            lambda: d_part(n1, lhs1, 1, (1,), (0, 1), signal=used),
            lambda: d_part(n2, lhs2, 1, (0, 1), (0,), last=True, signal=acc_done),
            lambda: d_part(n2, lhs2, 1, (0,), (1,)),
            lambda: d_part(n2, lhs2, 1, (1,), (1,), last=True, signal=used)])
        return [[(acc_done, c)] * 2, [(acc_done, c + 1), (used, n2)]]

    closing, split_later = [], []

    def close(n=5):
        for part in closing[:n]:
            part()
        del closing[:n]

    vec_rows = at(0, 2, P)
    VEC_ROWS = [P, ncols - P]
    vec_in = [Series(nc, f"vec_in{g}", 16) for g in range(2)]
    for g, n in enumerate(VEC_ROWS):
        op("act", lambda e, g=g, n=n: e.dma_start(vec_rows[0:n, g, :], A["vectors"][g * P:g * P + n, :]),
           signal=vec_in[g])

    x_in = [Series(nc, f"x_in{t}", 16) for t in range(T)]
    for t in range(T):
        op("sp", lambda e, t=t: e.dma_start(h[:, t, :], A["x"][t * P:(t + 1) * P, :]), signal=x_in[t])

    op("pool", lambda e: e.memset(ident, 0.0), name="ident0")
    op("pool", lambda e: e.affine_select(out=ident, in_=ident, compare_op=ALU.not_equal, fill=1.0, base=0,
                                         pattern=[[-1, P]], channel_multiplier=1), after=["ident0"], name="ident")
    op("pool", lambda e: e.memset(ones, 1.0), name="ones")
    op("pool", lambda e: e.memset(minus_half, -0.5), name="minus_half")
    op("pool", lambda e: e.memset(zeros, 0.0), name="zeros")
    op("act", lambda e: e.activation(tiny[:, 0, 0:1], ones[:, 0:1], ACT.Copy), after=["ones"])

    def turn_vectors(g):
        rows = VEC_ROWS[g]
        return lambda e: e.transpose(bank[0][:, g * P:g * P + rows], vec_rows[0:rows, g, :], ident[0:rows, 0:rows])
    for g in range(2):
        op("pe", turn_vectors(g), after=["ident", (vec_in[g], 0)], name=f"vec_turn{g}")
    op("dve", lambda e: e.tensor_copy(cols, bank[0][:, 0:ncols]), after=["vec_turn1"], name="cols")

    norms, turn_later, QS = [], [], 4

    def turn_h(name, gains, acc0=None, scale=1.0, between=None, x_at=4,
               turn_banks=(5, 6, 7, 0), h_ready=()):
        j = len(norms)
        norms.append(name)
        base = turned.claim(QS * T)
        assert x_full.claim(QS * T) == xhi_done.claim(QS * T) == base == QS * T * j
        assert xlo_done[0].claim(QS) == xlo_done[1].claim(QS) == QS * j
        full = at(x_at, QS, 2 * P)
        banks = [bank[i] for i in turn_banks]

        def add(t, q):
            if acc0 is not None:
                op("dve", lambda e: e.scalar_tensor_tensor(
                    out=h[:, t, q * 2 * P:(q + 1) * 2 * P], in0=acc[t][q // 2][:, (q % 2) * 2 * P:(q % 2 + 1) * 2 * P],
                    scalar=scale, in1=h[:, t, q * 2 * P:(q + 1) * 2 * P], op0=ALU.mult, op1=ALU.add),
                    after=[acc0[t][q // 2]] + list(h_ready), name=f"{name}_h{t}{q}")

        def turn(t, q):
            def emit(e):
                for i in range(2):
                    k = 2 * q + i
                    tr = e.transpose(banks[q][:, i * P:(i + 1) * P], h[:, t, k * P:(k + 1) * P], ident)
                return tr
            have = [f"{name}_h{t}{q}"] if acc0 is not None else [(x_in[t], 0)]
            op("pe", emit, after=have + ["ident"] + ([(x_full, base + q)] if t else []), signal=turned)

        def gained(t, q):
            op("dve", lambda e: e.tensor_tensor(
                full[:, q, :].rearrange("p (k s) -> p k s", k=2),
                banks[q][:, 0:2 * P].rearrange("p (k s) -> p k s", k=2),
                bcast(gains[:, q * 2:q * 2 + 2], [1, 2], [0, P]), ALU.mult),
                after=[(turned, base + QS * t + q), "cols"] + ([(xlo_done[0], QS * j + q)] if t else []),
                signal=x_full)

        def halves(t, q):
            i = base + QS * t + q
            src = full[:, q, :].rearrange("p (k s) -> p k s", k=2)
            hi, lo = (x[:, q * 2:q * 2 + 2, t * P:(t + 1) * P] for x in (xT_hi, xT_lo))
            op("act", lambda e: e.activation(hi, src, ACT.Copy), after=[(x_full, i)], signal=xhi_done)
            op("dve" if t else "pool", lambda e: e.tensor_tensor(lo, src, r32(hi), ALU.subtract),
               after=[(xhi_done, i)], signal=xlo_done[t])

        junk = at(0, D)

        def square(t):
            have = [f"{name}_h{t}3"] if acc0 is not None else [(x_in[t], 0)]
            op("act", lambda e, t=t: e.activation(junk, h[:, t, :], ACT.Square, accum_out=ssq[:, t:t + 1]),
               after=have + ([f"{name}_ss0"] if t else ["cols"]), name=f"{name}_ss{t}")

        for t in range(T):
            add(t, 0)
            for q in range(QS + 1):
                if q + 1 < QS:
                    add(t, q + 1)
                if q < QS:
                    gained(t, q)
                if q:
                    halves(t, q - 1)
            if t == 0:
                for n in split_later:
                    split_hi(n)
            if (t == 0) == (acc0 is None):
                for n in split_later:
                    split_lo(n)
        split_later.clear()
        square(0), square(1)
        if acc0 is None:
            for t in range(T):
                for q in range(QS):
                    turn(t, q)
        else:
            close(1)
            turn(0, 0), turn(0, 1)
            close(1)
            turn(0, 2), turn(0, 3)
            close(2)
            turn(1, 0)
            close(1)
            turn(1, 1)
            turn_later.extend([lambda q=q: turn(1, q) for q in range(2, QS)])
        for t in range(T):
            make_rstd(f"{name}_r{t}", t, f"{name}_ss{t}")
            last = f"{name}_r{t}"
            if between is not None:
                op("dve", lambda e, t=t: e.scalar_tensor_tensor(
                    out=h[:, t, :], in0=h[:, t, :], scalar=rstd[:, t:t + 1], in1=between, op0=ALU.mult,
                    op1=ALU.mult),
                   after=[last, f"{name}_ss{t}", (turned, base + QS * t + QS - 1), has("norm_final")],
                   name=f"{name}_n{t}")
                op("act", lambda e, t=t: e.activation(junk, h[:, t, :], ACT.Square,
                                                      accum_out=ssq[:, T + t:T + t + 1]),
                   after=[f"{name}_n{t}", f"{name}_ns{t - 1}" if t else f"{name}_ss{T - 1}"], name=f"{name}_ns{t}")
                make_rstd(f"{name}_nr{t}", T + t, f"{name}_ns{t}")
                op("pool", lambda e, t=t: e.tensor_tensor(rstd[:, t:t + 1], rstd[:, t:t + 1],
                                                          rstd[:, T + t:T + t + 1], ALU.mult),
                   after=[f"{name}_nr{t}", f"{name}_n{t}"], name=f"{name}_rr{t}")
                last = f"{name}_rr{t}"
            op("pool", lambda e, t=t: e.tensor_scalar(diag[:, t, :], ident, rstd[:, t:t + 1], None, ALU.mult),
               after=[last], name=f"{name}_diag{t}")

    def make_rstd(name, i, ss):
        v = rstd[:, i:i + 1]
        op("pool", lambda e: e.tensor_scalar(v, ssq[:, i:i + 1], 1.0 / D, EPS, ALU.mult, ALU.add), after=[ss],
           name=f"{name}_v")
        op("pool", lambda e: e.tensor_tensor(v, v, minus_half, ALU.pow), after=[f"{name}_v", "minus_half"],
           name=name)

    def spread_rms(name):
        for t in range(T):
            op("pe", lambda e, t=t: e.matmul(RMS_BANK[:, t * P:(t + 1) * P], ones[:, 0:P], diag[:, t, :],
                                             start=True, stop=True),
               after=[f"{name}_diag{t}", "ones", (xlo_done[1], QS * len(norms) - 1)], name=f"{name}_spread{t}")
        op("dve", lambda e: e.tensor_copy(rms, RMS_BANK[:, 0:S]), after=[f"{name}_spread{T - 1}"],
           name=f"{name}_rms")

    def x_block_ready(j):
        return lambda k: [(xlo_done[t], QS * (j - 1) + k // 2) for t in range(T)]

    def rms_pair():
        return bcast(rms, [0, 2], [1, S])

    def pair(ap):
        return ap.rearrange("p (b s) -> p b s", b=2)

    def feed_forward(name, ups, down, width, straight=0):
        pairs, nu = width // (2 * P), len(ups)
        each, n0, bufs = nu + 1, Stream.n, (3 if nu == 1 else 2)
        b_zt, b_zf = z_t.claim(pairs), z_f.claim(pairs)
        b_zg = z_g.claim(pairs) if nu == 2 else 0
        b_hi, b_lo = zhi_done.claim(pairs), zlo_done.claim(pairs)
        j = len(norms)
        tmp = [at(0, 2 * S), at(2, 2 * S), at(4, 2 * S)]

        def ups_at(p):
            return Step(n0) if p.loop is None and p.c == 0 else p.of(each, n0 - 1)

        def d_at(p):
            return p.of(each, n0 + each - 1) if p.loop is None and p.c == pairs - 1 \
                else p.of(each, n0 + 2 * each - 2)

        def psum_of(p, i):
            return bank[4 + p.slot(bufs) * nu + i]

        def up(p):
            n = ups_at(p)
            for i, w in enumerate(ups):
                load_piece(n.of(1, i), u_src(w, p.of(2 * P)), "U")
            for i in range(nu):
                after = []
                if free(p, bufs):
                    after = [(z_t, p.of(1, b_zt - bufs))]
                first = p.loop is None and p.c == 0 and i == 0
                u_piece(n.of(1, i), psum_of(p, i), after=after, after_k=x_block_ready(j) if first else None)

        def down_of(p):
            n = d_at(p)
            load_piece(n, d_src(down, p.of(2 * P)), "D")
            s = p.slot(bufs)
            return n, lambda kk, t: (z_hi[:, s, kk * S + t * P:kk * S + (t + 1) * P],
                                     z_lo[:, s, kk * S + t * P:kk * S + (t + 1) * P]), \
                [(zhi_done, p.of(1, b_hi)), (zlo_done, p.of(1, b_lo))]

        def finish_z(p):
            s, src = p.slot(bufs), psum_of(p, nu - 1)
            freed = []
            if free(p, bufs):
                freed = [(used, p.of(each, n0 + 2 * each - 2 - bufs * each))]
            here = [(used, ups_at(p).of(1, nu - 1)), f"{name}_rms"]
            if nu == 1:
                t, z = tmp[0], tmp[1]
                op("dve", lambda e: e.scalar_tensor_tensor(out=pair(t), in0=pair(src), scalar=0.0, in1=rms_pair(),
                                                           op0=ALU.max, op1=ALU.mult),
                   after=here + [(zhi_done, p.of(1, b_hi - 1))], signal=z_t)
                op("dve", lambda e: e.tensor_tensor(z, t, t, ALU.mult), after=[(z_t, p.of(1, b_zt))], signal=z_f)
                op("act", lambda e: e.activation(z_hi[:, s, :], t, ACT.Square),
                   after=[(z_t, p.of(1, b_zt))] + freed, signal=zhi_done)
            else:
                g, u, z = tmp
                op("dve", lambda e: e.tensor_tensor(pair(g), pair(psum_of(p, 0)), rms_pair(), ALU.mult),
                   after=here, name=None, signal=z_g)
                op("act", lambda e: e.activation(g, g, ACT.Silu), after=[(z_g, p.of(1, b_zg))], signal=z_s)
                op("dve", lambda e: e.tensor_tensor(pair(u), pair(src), rms_pair(), ALU.mult), signal=z_t)
                op("dve", lambda e: e.tensor_tensor(z, g, u, ALU.mult),
                   after=[(z_s, p.of(1, b_zg)), (z_t, p.of(1, b_zt)), (zhi_done, p.of(1, b_hi - 1))], signal=z_f)
                op("act", lambda e: e.activation(z_hi[:, s, :], z, ACT.Copy),
                   after=[(z_f, p.of(1, b_zf))] + freed, signal=zhi_done)
            op("dve", lambda e: e.tensor_tensor(z_lo[:, s, :], z, r32(z_hi[:, s, :]), ALU.subtract),
               after=[(zhi_done, p.of(1, b_hi)), (z_f, p.of(1, b_zf))], signal=zlo_done)

        up(Step(0))
        spread_rms(name)
        for half in range(4):
            op("pe", lambda e, half=half: e.matmul(bank[half][:, 0:2], zeros, zeros[:, 0:2], start=True, stop=False,
                                                   skip_group_check=True), after=["zeros"])
        for i in range(nu):
            split_piece(n0 + i + LOOK)
        finish_z(Step(0))

        def turn(p):
            up(p)
            n, lhs, after = down_of(p.of(1, -1))
            d_piece(n, lhs, after=after)
            n = ups_at(p)
            for i in range(each - 1):
                split_piece(n.of(1, i + LOOK))
            finish_z(p)
            split_piece(n.of(1, each - 1 + LOOK))
        steps(plan, 1, pairs - 2, BODY // each, turn, straight=straight)
        last = Step(pairs - 1)
        up(last)
        ready = last_d_pieces(down_of(last.of(1, -1)), down_of(last))
        n = ups_at(last)
        for i in range(each - 1):
            split_piece(n.of(1, i + LOOK))
        finish_z(last)
        split_piece(n.of(1, each - 1 + LOOK))
        split_later.append(n0 + each * pairs - 1 + LOOK)
        Stream.n += each * pairs
        return ready

    z_s = Series(nc, "z_s")

    def project(name, w, order, ready):
        n0, pieces = Stream.n, []
        for m, i in enumerate(order):
            load_piece(n0 + m, d_src(w, Step(i * 2 * P)), "D")
            pieces.append((Step(n0 + m), lambda kk, t, i=i: (xT_hi[:, 2 * i + kk, t * P:(t + 1) * P],
                                                             xT_lo[:, 2 * i + kk, t * P:(t + 1) * P]), ready(i)))
            if m < len(order) - 2:
                d_piece(*pieces[m][:2], first=(m == 0), after=pieces[m][2])
            if m < len(order) - 1:
                split_piece(n0 + m + LOOK)
        split_later.append(n0 + len(order) - 1 + LOOK)
        Stream.n += len(order)
        return last_d_pieces(*pieces[-2:])

    def attention(name, pairs, widths, masks, qT, kT, v, o, pt, pp, ready, sinks=False, stage_mask=None):
        A_ = {k: Series(nc, f"{name}_{k}") for k in
              ("qkhi", "qklo", "s", "tm", "nm", "ex", "tr", "pt0", "pt1", "pv", "rc", "o", "sd", "es", "sx", "msk")}
        off = [0, widths[0]]
        tiles = [(t, kt) for t in range(T) for kt in range(widths[t] // P)]
        q_hi, q_lo = z_hi[:, 0, 0:S], z_lo[:, 0, 0:S]
        k_hi, k_lo = z_hi[:, 0, S:2 * S], z_lo[:, 0, S:2 * S]
        mx, nm, sm, rc, sd, es = (tiny[:, i, :] for i in range(6))

        def prev(series, j, n=1, plus=0):
            return [(series, j.of(n, plus))] if j.loop is not None or j.c * n + plus >= 0 else []

        def split_qk(j):
            for i, (x, xh, xl) in enumerate(((qT, q_hi, q_lo), (kT, k_hi, k_lo))):
                op("act", lambda e, x=x, xh=xh: e.activation(xh, x[:, bass.ds(j.value(), 1), :].squeeze(1)
                                                             if j.loop else x[:, j.c, :], ACT.Copy),
                   after=prev(A_["s"], j, 2, -1) + ready, signal=A_["qkhi"])
                op("dve", lambda e, x=x, xh=xh, xl=xl: e.tensor_tensor(
                    xl, x[:, bass.ds(j.value(), 1), :].squeeze(1) if j.loop else x[:, j.c, :], r32(xh),
                    ALU.subtract), after=[(A_["qkhi"], j.of(2, i))], signal=A_["qklo"])

        def scores(j):
            for hd in range(2):
                r = slice(hd * HD, (hd + 1) * HD)

                def emit(e, r=r, hd=hd):
                    for t in range(T):
                        dst = bank[4 + hd][:, off[t]:off[t] + widths[t]]
                        for i, (q_, k_) in enumerate(((q_hi, k_hi), (q_hi, k_lo), (q_lo, k_hi))):
                            mm = e.matmul(dst, q_[r, t * P:(t + 1) * P], k_[r, 0:widths[t]], start=(i == 0),
                                          stop=(i == 2))
                    return mm
                op("pe", emit, after=[(A_["qklo"], j.of(2, 1))] + prev(A_["tm"], j, 4, 2 * hd - 3),
                   signal=A_["s"])

        def mask_and_max(j, hd):
            op("dve", lambda e: e.memset(waited, 0.0),
               after=[(A_["s"], j.of(2, hd))] + prev(A_["tr"], j, 2, hd - 2) +
               ([(A_["msk"], j)] if stage_mask else ready))
            for t in range(T):
                m = masks(hd, t)
                sl = slice(off[t], off[t] + widths[t])
                c = 2 * hd + t
                op("dve", lambda e, m=m, sl=sl, c=c: e.tensor_tensor_reduce(
                    pp[hd][:, sl], bank[4 + hd][:, sl], m, 1.0, NEG, ALU.add, ALU.max, mx[:, c:c + 1]),
                   signal=A_["tm"])
            c = slice(2 * hd, 2 * hd + 2)
            done = [(A_["tm"], j.of(4, 2 * hd + 1))]
            if sinks:
                def sink_of(e):
                    s_ = sink[:, bass.ds(j.of(2, hd).value(), 1)] if j.loop else sink[:, j.c * 2 + hd:j.c * 2 + hd + 1]
                    return s_
                op("dve", lambda e: e.tensor_scalar(mx[:, c], mx[:, c], sink_pair[:, hd:hd + 1], None, ALU.max),
                   after=done + [(A_["sx"], j)], signal=A_["sd"])
                done = [(A_["sd"], j.of(4, 2 * hd))]
                op("dve", lambda e: e.tensor_scalar(sd[:, c], mx[:, c], -1.0, sink_pair[:, hd:hd + 1], ALU.mult,
                                                    ALU.add),
                   after=done + prev(A_["es"], j, 1, -1), signal=A_["sd"])
            op("dve", lambda e: e.tensor_scalar(nm[:, c], mx[:, c], -1.0, None, ALU.mult),
               after=done + prev(A_["ex"], j, 2, hd - 2), signal=A_["nm"])

        def exps(j, hd):
            for t in range(T):
                sl = slice(off[t], off[t] + widths[t])
                c = 2 * hd + t
                op("act", lambda e, sl=sl, c=c: e.activation(pp[hd][:, sl], pp[hd][:, sl], ACT.Exp,
                                                             bias=nm[:, c:c + 1], accum_out=sm[:, c:c + 1]),
                   after=[(A_["nm"], j.of(2, hd))], signal=A_["ex"] if t == T - 1 else None)
            if sinks and hd == 1:
                op("act", lambda e: e.activation(es, sd, ACT.Exp), after=[(A_["sd"], j.of(4, 3))],
                   signal=A_["es"])

        def turn_weights(j):
            for hd in range(2):
                def emit(e, hd=hd):
                    for i, (t, kt) in enumerate(tiles):
                        a = off[t] + kt * P
                        tr = e.transpose(bank[6 + hd][:, i * P:(i + 1) * P], pp[hd][:, a:a + P], ident)
                    return tr
                op("pe", emit, after=[(A_["ex"], j.of(2, hd))] + prev(A_[f"pt{hd}"], j, 1, -1),
                   signal=A_["tr"])

        def copy_turned(j, hd):
            n = len(tiles) * P
            after = [(A_["tr"], j.of(2, hd))] + prev(A_["pv"], j, 1, -1)
            if hd:
                op("act", lambda e: e.activation(pt[hd][:, 0:n], bank[6 + hd][:, 0:n], ACT.Copy), after=after,
                   signal=A_["pt1"])
            else:
                op("dve", lambda e: e.tensor_copy(pt[hd][:, 0:n], bank[6 + hd][:, 0:n]), after=after,
                   signal=A_["pt0"])

        def apply_weights(j):
            def emit(e):
                for hd in range(2):
                    for t in range(T):
                        mine = [(i, kt) for i, (tt, kt) in enumerate(tiles) if tt == t]
                        for m, (i, kt) in enumerate(mine):
                            src = v[:, kt, bass.ds(j.of(P).value(), P)] if j.loop else \
                                v[:, kt, j.c * P:(j.c + 1) * P]
                            mm = e.matmul(bank[0][:, (2 * hd + t) * P:(2 * hd + t + 1) * P],
                                          pt[hd][:, i * P:(i + 1) * P], src, start=(m == 0),
                                          stop=(m == len(mine) - 1))
                return mm
            op("pe", emit, after=[(A_["pt0"], j), (A_["pt1"], j)] + prev(A_["o"], j, 1, -1) + ready,
               signal=A_["pv"])

        def recips(j):
            done = [(A_["ex"], j.of(2, 1))]
            if sinks:
                op("dve", lambda e: e.tensor_tensor(sm, sm, es, ALU.add), after=done + [(A_["es"], j)],
                   signal=A_["sa"])
                done = [(A_["sa"], j)]
            op("dve", lambda e: e.reciprocal(rc, sm), after=done + prev(A_["o"], j, 1, -1), signal=A_["rc"])

        def store_o(j):
            def emit(e):
                dst = o[:, bass.ds(j.value(), 1), :, :].squeeze(1) if j.loop else o[:, j.c, :, :]
                return e.tensor_tensor(dst.rearrange("p t (h d) -> p h t d", h=2),
                                       bass.AP(tensor=bank[0].tensor, offset=bank[0].offset,
                                               ap=[list(bank[0].ap[0]), [2 * P + HD, 2], [P, 2], [1, HD]]),
                                       bcast(rc, [2, 2], [1, 2], [0, HD]), ALU.mult)
            op("dve", emit, after=[(A_["pv"], j), (A_["rc"], j), (A_["qklo"], j.of(2, 1))], signal=A_["o"])

        if sinks:
            A_["sa"] = Series(nc, f"{name}_sa")
        sink_pair = tiny2

        def side(j):
            if stage_mask:
                op("pool", lambda e: stage_mask(e, j), after=prev(A_["tm"], j, 4, -1) + ready, signal=A_["msk"])
            if sinks:
                op("pool", lambda e: e.tensor_copy(sink_pair, sink[:, bass.ds(j.of(2).value(), 2)] if j.loop
                                                   else sink[:, 2 * j.c:2 * j.c + 2]),
                   after=prev(A_["sd"], j, 4, -1) + [has("sink")], signal=A_["sx"])

        def turn(j, more):
            side(j)
            scores(j)
            before = j.of(1, -1)
            have_before = j.loop is not None or j.c > 0
            if have_before:
                recips(before)
                turn_weights(before)
            if more:
                split_qk_act(j.of(1, 1))
            if have_before:
                copy_turned(before, 1)
            mask_and_max(j, 0)
            exps(j, 0)
            if have_before:
                copy_turned(before, 0)
            mask_and_max(j, 1)
            exps(j, 1)
            if more:
                split_qk_dve(j.of(1, 1))
            if have_before:
                apply_weights(before)
                store_o(before)

        def split_qk_act(j):
            q = plan.queues["dve"]
            k = len(q)
            split_qk(j)
            held.extend(q[k:])
            del q[k:]

        def split_qk_dve(j):
            plan.queues["dve"].extend(held)
            held.clear()
        held = []

        split_qk(Step(0))
        turn(Step(0), True)
        steps(plan, 1, pairs - 2, 1, lambda j: turn(j, True))
        turn(Step(pairs - 1), False)
        last = Step(pairs - 1)
        recips(last)
        turn_weights(last)
        copy_turned(last, 1)
        copy_turned(last, 0)
        apply_weights(last)
        store_o(last)
        b = mix_hi.claim(pairs // 2)
        assert mix_lo.claim(pairs // 2) == b
        for m in range(pairs // 2):
            dst = bank[4 + m]

            def emit(e, m=m, dst=dst):
                for i in range(4):
                    tr = e.transpose(dst[:, i * P:(i + 1) * P], o[:, 2 * m + i // 2, i % 2, :], ident)
                return tr
            op("pe", emit, after=[(A_["o"], 2 * m + 1), (A_["pt0"], pairs - 1), (A_["pt1"], pairs - 1)],
               name=f"{name}_oT{m}")
            op("act", lambda e, m=m, dst=dst: e.activation(xT_hi[:, 2 * m:2 * m + 2, :], pair(dst), ACT.Copy),
               after=[f"{name}_oT{m}"], signal=mix_hi)
            op("dve", lambda e, m=m, dst=dst: e.tensor_tensor(xT_lo[:, 2 * m:2 * m + 2, :], pair(dst),
                                                              r32(xT_hi[:, 2 * m:2 * m + 2, :]), ALU.subtract),
               after=[(mix_hi, b + m)], signal=mix_lo)
        return b

    tiny2 = sb("sink_pair", [P, 2])
    waited = sb("waited", [P, 1])

    TOTAL = 4 + 8 + 4 + 2 * (D_FF // 256) + 8 + 4 + 2 * (D_FF // 256) + 3 * (D_FF_2 // 256) + 5 + 4 \
        + 3 * (D_FF_2 // 256)

    split_later.append(0)
    turn_h("L0", gain("norm_mix0"), x_at=40, turn_banks=(5, 6, 7, 4))
    split_piece(1)
    ER, FAR = 384, 2 * MAX_REL
    table, er = at(4, FAR + 1), at(5.5, ER)
    load("rel", table[0:N_HEADS, :], A["rel"])
    sp = [at(7 + i / 16, KB) for i in range(6)]
    a_ = cols[:, col_at["a_param"]:col_at["a_param"] + KB]
    spp, spn, gg = extra[:, 0:KB], extra[:, KB:2 * KB], extra[:, 2 * KB:3 * KB]
    conv_bias = extra[:, 3 * KB:]
    chain = []

    def small(fn, extra_after=()):
        def queue():
            prior = [chain[-1]] if chain else ["cols"]
            chain.append(f"sp{len(chain)}")
            op("dve", fn, after=prior + list(extra_after), name=chain[-1])
        smalls.append(queue)

    def small_steps(n):
        for queue in smalls[:n]:
            queue()
        del smalls[:n]
    smalls = []

    small(lambda e: e.tensor_scalar(sp[0], a_, -1.0, None, ALU.mult))
    small(lambda e: e.tensor_tensor(sp[1], a_, sp[0], ALU.min))
    small_steps(2)
    op("act", lambda e: e.activation(sp[2], sp[1], ACT.Exp), after=[chain[-1]], name="sp_exp")
    small(lambda e: e.tensor_scalar(sp[3], sp[2], 2.0, None, ALU.add), ["sp_exp"])
    small(lambda e: e.reciprocal(sp[4], sp[3]))
    small(lambda e: e.tensor_tensor(sp[3], sp[2], sp[4], ALU.mult))
    small(lambda e: e.tensor_tensor(sp[4], sp[3], sp[3], ALU.mult))
    TERMS = 9
    small(lambda e: e.tensor_scalar(sp[5], sp[4], 1.0 / (2 * TERMS + 1), 1.0 / (2 * TERMS - 1), ALU.mult, ALU.add))
    for m in range(TERMS - 2, -1, -1):
        small(lambda e: e.tensor_tensor(sp[5], sp[5], sp[4], ALU.mult))
        small(lambda e, m=m: e.tensor_scalar(sp[5], sp[5], 1.0 / (2 * m + 1), None, ALU.add))
    small(lambda e: e.tensor_tensor(sp[5], sp[5], sp[3], ALU.mult))
    small(lambda e: e.tensor_scalar(sp[0], sp[0], 0.0, None, ALU.max))
    small(lambda e: e.scalar_tensor_tensor(out=sp[5], in0=sp[5], scalar=2.0, in1=sp[0], op0=ALU.mult, op1=ALU.add))
    small(lambda e: e.tensor_scalar(spp, sp[5], 8.0, None, ALU.mult))
    small(lambda e: e.tensor_scalar(spn, sp[5], -8.0, None, ALU.mult))
    small(lambda e: e.tensor_tensor(gg, cols[:, col_at["norm_final"]:col_at["norm_final"] + KB],
                                    cols[:, col_at["ffn1_norm"]:col_at["ffn1_norm"] + KB], ALU.mult))

    def vec(name, i=0):
        return cols[:, col_at[name] + i * KB:col_at[name] + (i + 1) * KB]
    small(lambda e: e.tensor_tensor(conv_bias, vec("conv_w"), vec("conv_w", 1), ALU.add))
    for tap in range(2, CONV):
        small(lambda e, tap=tap: e.tensor_tensor(conv_bias, conv_bias, vec("conv_w", tap), ALU.add))
    small(lambda e: e.tensor_tensor(conv_bias, conv_bias, vec("b_in"), ALU.mult))
    small(lambda e: e.tensor_tensor(conv_bias, conv_bias, vec("conv_b"), ALU.add))

    w_qkv = A["w_qkv"]
    qT, kT, v = at(24, KB, S), at(32, KB, S), None
    j0 = len(norms)
    acc0 = project("v", w_qkv[:, 2 * D:3 * D], range(4),
                   lambda i: [(xlo_done[t], QS * (j0 - 1) + i) for t in range(T)])
    close()
    op("dve", lambda e: e.tensor_copy(er[0:N_HEADS, 0:FAR], table[0:N_HEADS, 1:FAR + 1]), after=[has("rel")],
       name="er_near")
    op("dve", lambda e: e.tensor_copy(er[0:N_HEADS, FAR:ER], bcast(table[0:N_HEADS, FAR:FAR + 1], [0, ER - FAR])),
       name="er_far")
    er_dram = nc.dram_tensor("er_scratch", [N_HEADS, ER], F32, kind="Internal").ap()
    er_out = Series(nc, "er_out", 16)
    op("pool", lambda e: e.dma_start(er_dram, er[0:N_HEADS, :]), after=["er_far"], signal=er_out)
    bias = at(8, N_HEADS, S)
    load("bias", bias, bass.AP(tensor=er_dram.tensor, offset=0, ap=[[1, P], [ER, N_HEADS], [1, S]]),
         after=[(er_out, 0)])
    op("pool", lambda e: e.memset(bias[0:CHUNK, :, 0:CHUNK], NEG), after=[has("bias")], name="bias")
    load("gate_a", gate_w[:, 0], A["w_ga"].rearrange("n c e -> c n e"), engine="pool")
    load("gate_x", gate_w[:, 1], A["w_gx"].rearrange("n c e -> c n e"), engine="pool")
    load("pool_w", pool_w, A["pool_w"].rearrange("n c e -> c n e"), engine="pool")
    load("sink", sink, bass.AP(tensor=A["sink"].tensor, offset=A["sink"].offset, ap=[[0, P], [1, HEADS_2]]),
         engine="pool")

    v = vbuf = sb("v", [P, T, D])
    for t in range(T):
        for half in range(2):
            op("act", lambda e, t=t, half=half: e.activation(v[:, t, half * 512:(half + 1) * 512], acc[t][half],
                                                             ACT.Copy, scale=rstd[:, t:t + 1]),
               after=[acc0[t][half], f"L0_r{t}"], name=f"v{t}{half}")
    split_piece(split_later.pop())
    spread_rms("L0")
    n0, b_zt = Stream.n, z_t.claim(8)
    for p in range(8):
        dst = bank[4 + p % 3]
        load_piece(n0 + p, u_src(w_qkv, Step(p * 2 * P)), "U")
        u_piece(n0 + p, dst, after=[(z_t, b_zt + p - 3)] if p >= 3 else [])
        split_piece(n0 + p + LOOK)
        to = (qT if p < 4 else kT)[:, 2 * (p % 4):2 * (p % 4) + 2, :]
        op("dve", lambda e, to=to, dst=dst, p=p: e.scalar_tensor_tensor(
            out=to, in0=pair(dst), scalar=QSCALE if p < 4 else 1.0, in1=rms_pair(), op0=ALU.mult, op1=ALU.mult),
           after=[(used, n0 + p), "L0_rms"], signal=z_t)
        small_steps(6)
    Stream.n += 8
    assert not smalls
    stage = sb("stage", [P, 2, S])

    def stage_bias(e, j):
        src = bias[:, bass.ds(j.of(2).value(), 2), :] if j.loop else bias[:, 2 * j.c:2 * j.c + 2, :]
        return e.tensor_copy(stage, src)

    pp = [at(0, 384), at(1.5, 384)]
    pt = [at(3, 384), at(4.5, 384)]
    mb = attention("a1", KB, [P, S], lambda hd, t: stage[:, hd, 0:[P, S][t]][:, ::-1], qT, kT, v,
                   o=qT.rearrange("p j (t c) -> p j t c", t=T), pt=pt, pp=pp,
                   ready=[(z_t, b_zt + 7), "v11", "bias", "L0_ss1"],
                   stage_mask=stage_bias)
    a0 = project("wo", A["w_o"], range(4), lambda i: [(mix_lo, mb + i)])
    turn_h("M0", gain("norm_mlp0"), a0)
    a0 = feed_forward("M0", [A["w1"][0]], A["w2"][0], D_FF)

    turn_h("L1", gain("norm_mix1"), a0)
    BP = S + CONV - 1
    xb, xc, rr, nt = at(4, KB, BP), at(13, KB, S), at(21, KB, S), at(29, KB, S)
    ig, sq = [at(37 + i, S) for i in range(2)], [at(39 + i, S) for i in range(2)]
    bo = at(41, D)
    load("b_o", bo, bass.AP(tensor=A["b_o"].tensor, offset=A["b_o"].offset, ap=[[0, P], [1, D]]), after=["L1_h13"])
    op("dve", lambda e: e.tensor_scalar(xb[:, :, 0:CONV - 1],
                                        bcast(cols[:, col_at["b_in"]:col_at["b_in"] + 1], [1, KB], [0, CONV - 1]),
                                        -1.0, None, ALU.mult),
       after=["L1_ss1", (xlo_done[1], QS * len(norms) - 1)], name="conv_pad")
    w_in = A["w_in"]
    n0, b_zt, j1 = Stream.n, z_t.claim(8), len(norms)

    def x_pair(p):
        op("dve", lambda e: e.tensor_tensor(xb[:, 2 * p:2 * p + 2, CONV - 1:], pair(bank[4 + p % 3]), rms_pair(),
                                            ALU.mult), after=[(used, n0 + p), "L1_rms", "L1_ss1"], signal=z_t)

    def conv(p):
        for n in (2 * p, 2 * p + 1):
            op("pool", lambda e, n=n: e.tensor_scalar(xc[:, n, :], xb[:, n, 0:S], col("conv_w", n),
                                                      conv_bias[:, n:n + 1], ALU.mult, ALU.add),
               after=[(z_t, b_zt + p), "conv_pad"], name=f"conv{n}_0")
        for n in (2 * p, 2 * p + 1):
            for tap in range(1, CONV):
                op("dve", lambda e, n=n, tap=tap: e.scalar_tensor_tensor(
                    out=xc[:, n, :], in0=xb[:, n, tap:tap + S], scalar=col("conv_w", tap * KB + n), in1=xc[:, n, :],
                    op0=ALU.mult, op1=ALU.add), after=[f"conv{n}_{tap - 1}"], name=f"conv{n}_{tap}")

    def gates(n):
        dst = bank[n % 4]

        def emit(e):
            e.matmul(dst[:, 0:S], gate_w[:, 0, n, :], xc[:, n, :], start=True, stop=True)
            return e.matmul(dst[:, S:2 * S], gate_w[:, 1, n, :], xc[:, n, :], start=True, stop=True)
        op("pe", emit, after=[f"conv{n}_{CONV - 1}", has("gate_a"), has("gate_x")] +
           ([f"ig{n - 4}"] if n >= 4 else []), name=f"gates{n}")
        op("act", lambda e: e.activation(rr[:, n, :], dst[:, 0:S], ACT.Sigmoid, bias=col("b_ga", n)),
           after=[f"gates{n}", chain[-1]], name=f"r{n}")
        op("act", lambda e: e.activation(ig[n % 2], dst[:, S:2 * S], ACT.Sigmoid, bias=col("b_gx", n)),
           after=[f"bx{n - 2}"] if n >= 2 else [], name=f"ig{n}")
        op("act", lambda e: e.activation(nt[:, n, :], rr[:, n, :], ACT.Tanh, scale=spp[:, n:n + 1]),
           after=[f"r{n}"], name=f"nt{n}")
        op("pool", lambda e: e.tensor_tensor(xc[:, n, :], xc[:, n, :], ig[n % 2], ALU.mult), after=[f"ig{n}"],
           name=f"bx{n}")

    def decays():
        for n in range(KB):
            op("act", lambda e, n=n: e.activation(rr[:, n, :], rr[:, n, :], ACT.Exp, scale=spn[:, n:n + 1]),
               after=[f"nt{n}"], name=f"a{n}")
            op("pool", lambda e, n=n: e.tensor_tensor(sq[n % 2], rr[:, n, :], rr[:, n, :], ALU.mult),
               after=[f"a{n}"] + ([f"m{n - 2}"] if n >= 2 else []), name=f"sq{n}")
            op("dve", lambda e, n=n: e.scalar_tensor_tensor(out=nt[:, n, :], in0=sq[n % 2], scalar=1.0,
                                                            in1=nt[:, n, :], op0=ALU.add, op1=ALU.mult),
               after=[f"sq{n}"], name=f"m{n}")

    def roots():
        for n in range(KB):
            op("act", lambda e, n=n: e.activation(nt[:, n, :], nt[:, n, :], ACT.Sqrt), after=[f"m{n}"],
               name=f"mult{n}")

    def scans(blocks):
        for n in blocks:
            op("dve" if n < KB // 2 else "pool", lambda e, n=n: e.tensor_tensor(xc[:, n, :], xc[:, n, :],
                                                                                nt[:, n, :], ALU.mult),
               after=[f"mult{n}", f"bx{n}"], name=f"b{n}")
            op("dve", lambda e, n=n: e.tensor_tensor_scan(nt[:, n, :], rr[:, n, :], xc[:, n, :], 0.0, ALU.mult,
                                                          ALU.add), after=[f"b{n}"], name=f"hs{n}")

    def y_pair(p):
        op("dve", lambda e: e.tensor_tensor(xb[:, 2 * p:2 * p + 2, 0:S], pair(bank[[5, 6, 7, 4][p]]), rms_pair(),
                                            ALU.mult),
           after=[(used, n0 + 4 + p)] + [f"conv{n}_{CONV - 1}" for n in range(2 * p, 2 * p + 2)], signal=z_t)

    def mixed(p):
        for n in (2 * p, 2 * p + 1):
            op("act", lambda e, n=n: e.activation(xb[:, n, 0:S], xb[:, n, 0:S], ACT.Gelu_apprx_tanh,
                                                  bias=col("b_in", KB + n)), after=[(z_t, b_zt + 4 + p)],
               name=f"y{n}")
            op("dve", lambda e, n=n: e.tensor_tensor(xc[:, n, :], xb[:, n, 0:S], nt[:, n, :], ALU.mult),
               after=[f"y{n}", f"hs{n}"], name=f"o{n}")
        for n in (2 * p, 2 * p + 1):
            op("act", lambda e, n=n: e.activation(xT_hi[:, n, :], xc[:, n, :], ACT.Copy),
               after=[f"o{n}", f"xT_read{n}" if n < KB - 1 else (used, n0 + 7)], signal=mix_hi)
            op("dve", lambda e, n=n: e.tensor_tensor(xT_lo[:, n, :], xc[:, n, :], r32(xT_hi[:, n, :]), ALU.subtract),
               after=[(mix_hi, mbr + n)], signal=mix_lo)

    mbr = mix_hi.claim(KB)
    assert mix_lo.claim(KB) == mbr

    def rec_piece(m, leave=None, convolve=None, gate=None):
        load_piece(n0 + m, u_src(w_in, Step(m * 2 * P)), "U")
        if m + LOOK < 8:
            split_hi(n0 + m + LOOK)
        if leave:
            leave(m - 1 if m <= 4 else m - 5)
        if m + LOOK < 8:
            split_lo(n0 + m + LOOK)
        if convolve:
            conv(m - 1)
        after = [(z_t, b_zt + m - 3)] if m == 3 else []
        between = {3: lambda: gates(2 * m - 4), 6: lambda: gates(2 * m - 3)} if gate else None
        u_piece(n0 + m, bank[4 + m % 3] if m < 4 else bank[[5, 6, 7, 4][m - 4]], after=after +
                ([(z_t, b_zt + {4: 1, 5: 2, 6: 2, 7: 3}[m])] if m >= 4 else []) +
                (["L1_rms"] if m == 6 else []),
                after_k=x_block_ready(j1) if m == 0 else None, between=between, freed="xT_read" if m == 7 else None)
    rec_piece(0)
    spread_rms("L1")
    rec_piece(1, x_pair, True)
    rec_piece(2, x_pair, True, True)
    rec_piece(3, x_pair, True, True)
    rec_piece(4, x_pair, True, True)
    rec_piece(5, y_pair, False, True)
    decays()
    rec_piece(6, y_pair)
    split_piece(n0 + 8)
    roots()
    scans(range(0, 2))
    rec_piece(7)
    mixed(0)
    scans(range(2, 8))
    split_piece(n0 + 9)
    y_pair(2)
    mixed(1)
    y_pair(3)
    mixed(2), mixed(3)
    for t in range(T):
        op("pool", lambda e, t=t: e.tensor_tensor(h[:, t, :], h[:, t, :], bo, ALU.add),
           after=[has("b_o"), (turned, QS * T * len(norms) - 1), f"L1_ss{t}"], name=f"h_bo{t}")
    Stream.n += 8
    a0 = project("rec_wo", A["rec_w_o"], range(4), lambda i: [(mix_lo, mbr + 2 * i + 1)])
    turn_h("M1", gain("norm_mlp1"), a0, h_ready=["h_bo1"])
    nf = at(8, D)
    load("norm_final", nf, bass.AP(tensor=A["norm_final"].tensor, offset=A["norm_final"].offset,
                                   ap=[[0, P], [1, D]]), after=["M1_h13"])
    a0 = feed_forward("M1", [A["w1"][1]], A["w2"][1], D_FF)

    turn_h("F1", gg, a0, between=nf)
    a0 = feed_forward("F1", [A["f1_gate"], A["f1_up"]], A["f1_down"], D_FF_2)

    turn_h("X", gain("mix_norm"), a0, scale=0.5)
    q2, k2, v2 = at(24, 4, S), at(28, 4, S), vbuf.rearrange("p t (a b) -> p t a b", a=2)[:, :, 0, :]
    cs_t, mats, mask2 = at(18, 2, S), at(20, 5, P), at(32, T, S)
    pc, csum, dd = at(4, PG, S), at(8, 9 * 32 + 3)[:, 0:S + 17], [at(10 + i, S) for i in range(2)]
    inv, kv = at(36, PG, 2, S), at(12, 2 * S)
    qf, tq = at(14, 2 * S), at(16, 2 * S)
    load("tables", cs_t, A["rope"], after=["X_h13"])
    load("mats", mats, A["mats"], after=["X_h13"])
    load("mask2", mask2, A["mask2"], after=["X_h13"])
    load("inv", inv.rearrange("p g w s -> p (g w s)"),
         bass.AP(tensor=A["inv"].tensor, offset=A["inv"].offset, ap=[[0, P], [1, PG * 2 * S]]), after=["X_h13"])
    w2_in = A["w_in2"]
    j2, n0, b_zt = len(norms), Stream.n, z_t.claim(5)
    first_col = [768, 1024, 512, 0, 256]

    def mix_piece(m):
        load_piece(n0 + m, u_src(w2_in, Step(first_col[m])), "U")
        u_piece(n0 + m, bank[4 + m % 3], after=[(z_t, b_zt + m - 3)] if m >= 3 else [],
                after_k=x_block_ready(j2) if m == 0 else None)
        split_piece(n0 + m + LOOK)

    def leave(m, dst, scale=1.0, after=()):
        op("dve", lambda e: e.scalar_tensor_tensor(out=dst, in0=pair(bank[4 + m % 3]), scalar=scale, in1=rms_pair(),
                                                   op0=ALU.mult, op1=ALU.mult),
           after=[(used, n0 + m), "X_rms", "X_ss1"] + list(after), signal=z_t)

    op("pool", lambda e: e.memset(csum[:, 0:9], 0.0), after=["X_ss1", (xlo_done[1], QS * len(norms) - 1)], name="csum0")

    def pool_group(g):
        half = POOL_WINDOWS[g] // 2
        op("dve", lambda e: e.tensor_tensor_scan(csum[:, 9:9 + S], ones, pc[:, g, :], 0.0, ALU.mult, ALU.add),
           after=[(z_t, b_zt + g // 2), "csum0"] + ([f"d{g - 1}_2"] if g else []), name=f"cs{g}_0")
        op("dve", lambda e: e.tensor_copy(csum[:, 9 + S:17 + S], bcast(csum[:, 8 + S:9 + S], [0, 8])),
           after=[f"cs{g}_0"], name=f"cs{g}_1")
        for w in range(2):
            a, b = 8 - half + w, 8 + half + w
            op("pool", lambda e, a=a, b=b, w=w: e.tensor_tensor(dd[w], csum[:, b:b + S], csum[:, a:a + S],
                                                                ALU.subtract),
               after=[f"cs{g}_1"] + ([f"pool{g - 1}"] if g else []), name=f"d{g}_{1 + w}")
            op("pool", lambda e, w=w: e.tensor_tensor(dd[w], dd[w], inv[:, g, w, :], ALU.mult),
               after=[has("inv"), f"d{g}_{1 + w}"], name=f"e{g}_{w}")
        op("pool", lambda e: e.tensor_tensor(dd[0], dd[0], dd[1], ALU.add), after=[f"e{g}_0", f"e{g}_1"],
           name=f"mean{g}")
        op("pool", lambda e: e.tensor_tensor(pc[:, g, :], dd[0], pc[:, g, :], ALU.subtract), after=[f"mean{g}"],
           name=f"pool{g}")

    def pool_product(g):
        op("pe", lambda e: e.matmul(bank[2 + g // 2][:, (g % 2) * S:(g % 2 + 1) * S], pool_w[:, g, :], pc[:, g, :],
                                    start=True, stop=True), after=[f"pool{g}", has("pool_w")], name=f"pool_y{g}")

    cos, sin = cs_t[:, 0, :], cs_t[:, 1, :]

    def two(ap):
        return bcast(ap, [0, 2], [1, S])

    mix_piece(0)
    spread_rms("X")
    mix_piece(1)
    leave(0, pc[:, 0:2, :])
    pool_group(0), pool_group(1)
    mix_piece(2)
    leave(1, pc[:, 2:4, :])
    pool_group(2), pool_group(3)
    mix_piece(3)
    leave(2, pair(kv))
    pool_product(0), pool_product(1)
    for g in range(KV_2):
        def emit(e, g=g):
            e.matmul(bank[g][:, 0:S], mats[:, 1 + 2 * g, :], kv[:, 0:S], start=True, stop=True)
            return e.matmul(bank[g][:, S:2 * S], mats[:, 2 + 2 * g, :], kv[:, 0:S], start=True, stop=True)
        op("pe", emit, after=[(z_t, b_zt + 2), has("mats")], name=f"k_rot{g}")
    for t in range(T):
        op("pe", lambda e, t=t: e.transpose(bank[7][:, t * P:(t + 1) * P], kv[:, S + t * P:S + (t + 1) * P], ident),
           after=["X_rms"], name=f"v_turn{t}")
    for t in range(T):
        for g in range(KV_2):
            op("act", lambda e, t=t, g=g: e.activation(
                v2[:, t, g * 4 * HD:(g + 1) * 4 * HD].rearrange("p (r d) -> p r d", d=HD),
                bcast(bank[7][:, t * P + g * HD:t * P + (g + 1) * HD], [0, 4], [1, HD]), ACT.Copy),
               after=["v_turn1"], name=f"v2_{t}{g}")
    for g in range(KV_2):
        op("dve", lambda e, g=g: e.tensor_tensor(tq[:, 0:S], bank[g][:, 0:S], cos, ALU.mult),
           after=[f"k_rot{g}", has("tables")] + ([f"k2_{g - 1}"] if g else []), name=f"kc{g}")
        op("dve", lambda e, g=g: e.tensor_tensor(tq[:, S:2 * S], bank[g][:, S:2 * S], sin, ALU.mult), name=f"ks{g}")
        op("dve", lambda e, g=g: e.tensor_tensor(k2[:, 2 * g:2 * g + 2, :], two(tq[:, 0:S]), two(tq[:, S:2 * S]),
                                                 ALU.add), after=[f"kc{g}", f"ks{g}"], name=f"k2_{g}")

    def rope_q(m):
        i = m - 3
        leave(m, pair(qf), scale=QSCALE, after=["k2_1"] if i == 0 else ["q2_0", "qsin0"])
        op("pe", lambda e: e.matmul(bank[i], mats[:, 0, :], qf, start=True, stop=True),
           after=[(z_t, b_zt + m), "k2_1"], name=f"q_rot{i}")
        op("dve", lambda e: e.tensor_tensor(q2[:, 2 * i:2 * i + 2, :], pair(qf), two(cos), ALU.mult),
           after=[(z_t, b_zt + m)], name=f"qcos{i}")
        op("dve", lambda e: e.tensor_tensor(pair(tq), pair(bank[i]), two(sin), ALU.mult), after=[f"q_rot{i}"],
           name=f"qsin{i}")
        op("dve", lambda e: e.tensor_tensor(q2[:, 2 * i:2 * i + 2, :], q2[:, 2 * i:2 * i + 2, :], pair(tq), ALU.add),
           after=[f"qcos{i}", f"qsin{i}"], name=f"q2_{i}")
    mix_piece(4)
    pool_product(2), pool_product(3)
    rope_q(3)
    rope_q(4)
    mp = mix_hi.claim(PG)
    assert mix_lo.claim(PG) == mp
    for g in range(PG):
        src = bank[2 + g // 2][:, (g % 2) * S:(g % 2 + 1) * S]
        op("act", lambda e, g=g, src=src: e.activation(xT_hi[:, 4 + g, :], src, ACT.Copy, scale=col("pool_scale", g)),
           after=[f"pool_y{g | 1}", (used, n0 + 4)], signal=mix_hi)
        op("dve", lambda e, g=g, src=src: e.scalar_tensor_tensor(
            out=xT_lo[:, 4 + g, :], in0=src, scalar=col("pool_scale", g), in1=r32(xT_hi[:, 4 + g, :]), op0=ALU.mult,
            op1=ALU.subtract), after=[(mix_hi, mp + (g | 1))], signal=mix_lo)
    Stream.n += 5
    pp2 = [at(36, 2 * S), at(38, 2 * S)]
    pt2 = [at(40, 2 * S), at(42, 2 * S)]
    ma = attention("a2", HEADS_2 // 2, [S, S], lambda hd, t: mask2[:, t, :], q2, k2, v2,
                   o=q2.rearrange("p j (t c) -> p j t c", t=T), pt=pt2, pp=pp2,
                   ready=["q2_1", "v2_11", has("mask2"), "pool3"], sinks=True)
    a0 = project("w_out", A["w_out"], [2, 3, 0, 1],
                 lambda i: [(mix_lo, mp + 2 * (i - 2) + 1)] if i >= 2 else [(mix_lo, ma + i)])
    turn_h("F2", gain("ffn2_norm"), a0)
    load("norm_last", nf, bass.AP(tensor=A["norm_last"].tensor, offset=A["norm_last"].offset,
                                  ap=[[0, P], [1, D]]), after=["F2_h13"])
    a0 = feed_forward("F2", [A["f2_gate"], A["f2_up"]], A["f2_down"], D_FF_2, straight=2)
    assert Stream.n == TOTAL, (Stream.n, TOTAL)
    close()
    junk, res = at(12, D), at(16, T, D)
    out_done = Series(nc, "out_done", 16)
    for t in range(T):
        for half in range(2):
            hh = h[:, t, half * 512:(half + 1) * 512]
            op("dve", lambda e, hh=hh, a=acc[t][half]: e.scalar_tensor_tensor(
                out=hh, in0=a, scalar=0.5, in1=hh, op0=ALU.mult, op1=ALU.add), after=[a0[t][half]],
               name=f"last_h{t}{half}")
        op("act", lambda e, t=t: e.activation(junk, h[:, t, :], ACT.Square, accum_out=ssq[:, t:t + 1]),
           after=[f"last_h{t}0", f"last_h{t}1"] + ([f"last_ss{t - 1}"] if t else []), name=f"last_ss{t}")
        make_rstd(f"last_r{t}", t, f"last_ss{t}")
    for t in range(T):
        op("dve", lambda e, t=t: e.scalar_tensor_tensor(out=res[:, t, :], in0=h[:, t, :], scalar=rstd[:, t:t + 1],
                                                        in1=nf, op0=ALU.mult, op1=ALU.mult),
           after=[f"last_r{t}", has("norm_last")], name=f"last{t}")
        op("sp", lambda e, t=t: e.dma_start(out[t * P:(t + 1) * P, :], res[:, t, :]), after=[f"last{t}"],
           signal=out_done)
    op("sp", lambda e: e.nop(), after=[(out_done, T - 1), (er_out, 0)])

    with nc.Block() as block:
        @block.sync
        def _(e):
            plan.write("sp", e)

        @block.scalar
        def _(e):
            plan.write("act", e)

        @block.vector
        def _(e):
            plan.write("dve", e)

        @block.gpsimd
        def _(e):
            plan.write("pool", e)

        @block.tensor
        def _(e):
            plan.write("pe", e)


def shape_constants():
    f = np.float32
    freq = f(THETA) ** (-np.arange(0, ROT, 2, dtype=f) / f(ROT))
    ang = np.arange(S, dtype=f)[:, None] * freq[None, :]
    ang = np.concatenate([ang, ang], axis=-1).T
    rope = np.zeros((P, 2, S), f)
    rope[:, 0] = 1.0
    rot = np.zeros((HD, HD), f)
    for d in range(ROT // 2):
        rot[d + ROT // 2, d] = -1.0
        rot[d, d + ROT // 2] = 1.0
    for head in range(P // HD):
        rope[head * HD:head * HD + ROT, 0] = np.cos(ang)
        rope[head * HD:head * HD + ROT, 1] = np.sin(ang)
    mats = np.zeros((P, 5, P), f)
    for a in range(2):
        s = slice(a * HD, (a + 1) * HD)
        mats[s, 0, s] = rot
        for g in range(KV_2):
            mats[g * HD:(g + 1) * HD, 1 + 2 * g, s] = np.eye(HD, dtype=f)
            mats[g * HD:(g + 1) * HD, 2 + 2 * g, s] = rot
    qpos = np.arange(T)[None, :, None] * P + np.arange(P)[:, None, None]
    kpos = np.arange(S)[None, None, :]
    mask = np.where(np.abs(qpos - kpos) <= WINDOW, 0.0, NEG).astype(f)
    t = np.arange(S)
    inv = np.zeros((PG, 2, S), f)
    for g, w in enumerate(POOL_WINDOWS):
        for i in range(2):
            lo, hi = np.clip(t - w // 2 + i, 0, S), np.clip(t + w // 2 + i, 0, S)
            inv[g, i] = 0.5 / (hi - lo)
    return {"rope": rope, "mats": mats, "mask2": mask, "inv": inv}


def kernel(**inputs):
    import concourse.bacc as bacc
    from concourse.bass_utils import run_bass_kernel_spmd

    def flat(name, *shape):
        return np.ascontiguousarray(inputs[name]).reshape(shape)

    nm, nl = inputs["norm_mix"], inputs["norm_mlp"]
    vectors = {"norm_mix0": nm[0], "norm_mix1": nm[1], "norm_mlp0": nl[0], "norm_mlp1": nl[1],
               "norm_final": inputs["norm_final"], "ffn1_norm": inputs["ffn1_norm_2"],
               "mix_norm": inputs["mix_norm_2"], "ffn2_norm": inputs["ffn2_norm_2"], "b_in": inputs["rec_b_in"],
               "conv_b": inputs["rec_conv_b"], "b_ga": inputs["rec_b_ga"], "b_gx": inputs["rec_b_gx"],
               "a_param": inputs["rec_a_param"], "conv_w": inputs["rec_conv_w"],
               "pool_scale": inputs["pool_scale_2"]}
    arrays = {
        "x": flat("x", S, D), "vectors": np.concatenate([np.asarray(vectors[n]).reshape(-1, P) for n, _ in VECTORS]),
        "norm_final": flat("norm_final", D), "w_qkv": flat("attn_w_qkv", D, 3 * D), "w_o": flat("attn_w_o", D, D),
        "rel": flat("attn_rel_bias", N_HEADS, 2 * MAX_REL + 1), "w_in": flat("rec_w_in", D, 2 * D),
        "w_ga": flat("rec_w_ga", KB, P, P), "w_gx": flat("rec_w_gx", KB, P, P), "rec_w_o": flat("rec_w_o", D, D),
        "b_o": flat("rec_b_o", D), "w1": flat("mlp_w1", 2, D, D_FF), "w2": flat("mlp_w2", 2, D_FF, D),
        "f1_gate": flat("ffn1_w_gate_2", D, D_FF_2), "f1_up": flat("ffn1_w_up_2", D, D_FF_2),
        "f1_down": flat("ffn1_w_down_2", D_FF_2, D), "w_in2": flat("w_in_2", D, 1280),
        "sink": flat("sink_logits_2", HEADS_2), "pool_w": flat("pool_w_2", PG, P, P),
        "w_out": flat("w_out_2", D, D), "f2_gate": flat("ffn2_w_gate_2", D, D_FF_2),
        "f2_up": flat("ffn2_w_up_2", D, D_FF_2), "f2_down": flat("ffn2_w_down_2", D_FF_2, D),
        "norm_last": flat("final_norm_2", D),
    }
    arrays.update(shape_constants())
    nc = bacc.Bacc("TRN2", target_bir_lowering=False, num_devices=1)
    A = {k: nc.dram_tensor(f"in_{k}", a.shape, F32, kind="ExternalInput").ap() for k, a in arrays.items()}
    out = nc.dram_tensor("out", (1, S, D), F32, kind="ExternalOutput").ap()
    build(nc, A, out[0])
    r = run_bass_kernel_spmd(nc, [{f"in_{k}": a for k, a in arrays.items()}], core_ids=[0])
    return r.results[0]["out"]
```

```python
from contextlib import contextmanager

import numpy as np
import concourse.bass as bass
from concourse import mybir

F32 = mybir.dt.float32
F32R = mybir.dt.float32r
BF16 = mybir.dt.bfloat16
ACT = mybir.ActivationFunctionType
ALU = mybir.AluOpType

P = 128
S = 256
T = S // P
D = 1024
KB = D // P
EPS = 1e-6
HD = 64
QSCALE = HD ** -0.5
N_HEADS, CHUNK, MAX_REL = 16, 64, 128
CONV = 4
D_FF, D_FF_2 = 4096, 2816
HEADS_2, KV_2, WINDOW, ROT, THETA = 8, 2, 128, 16, 500000.0
POOL_WINDOWS = (2, 4, 8, 16)
PG = len(POOL_WINDOWS)
NEG = -1e30

PIECE = 2048
RING = 3
RAW = 6
LOOK = RING - 1
BODY = 6

VECTORS = [("norm_mix0", 8), ("norm_mlp0", 8), ("norm_mix1", 8), ("norm_mlp1", 8), ("norm_final", 8),
           ("ffn1_norm", 8), ("mix_norm", 8), ("ffn2_norm", 8), ("b_in", 16), ("conv_b", 8), ("b_ga", 8),
           ("b_gx", 8), ("a_param", 8), ("conv_w", 8 * CONV), ("pool_scale", PG)]


class Loop:

    def __init__(self, count):
        self.count, self.reg = count, None


class Step:

    def __init__(self, c, loop=None, per=0):
        self.c, self.loop, self.per = c, loop, per

    def of(self, mult=1, plus=0):
        return Step(self.c * mult + plus, self.loop, self.per * mult)

    def value(self):
        return self.c if self.loop is None else self.loop.reg * self.per + self.c

    def slot(self, n):
        assert self.loop is None or self.per % n == 0
        return self.c % n


def as_step(x):
    return x if isinstance(x, Step) else Step(x)


class Series:

    def __init__(self, nc, name, unit=1):
        self.sem, self.unit, self.claimed = nc.alloc_semaphore(name), unit, 0

    def claim(self, n):
        self.claimed += n
        return self.claimed - n


class Plan:

    def __init__(self, nc, engines):
        self.queues = {e: [] for e in engines}
        self.done = {e: Series(nc, f"{e}_done") for e in engines}
        self.named, self.loop_now = {}, None

    def op(self, engine, emit, after=(), name=None, signal=None):
        if name:
            assert signal is None and self.loop_now is None and name not in self.named, name
            signal = self.done[engine]
            self.named[name] = (signal, Step(signal.claim(1)))
        self.queues[engine].append((emit, list(after), signal))

    @contextmanager
    def loop(self, count):
        self.loop_now = loop = Loop(count)
        outer, self.queues = self.queues, {e: [] for e in self.queues}
        yield loop
        for e, body in self.queues.items():
            if body:
                outer[e].append((loop, body, None))
        self.queues, self.loop_now = outer, None

    def write(self, engine, e):
        self._write(e, self.queues[engine], {})

    def _write(self, e, entries, met):
        for emit, after, signal in entries:
            if isinstance(emit, Loop):
                with e.Fori(0, emit.count) as i:
                    emit.reg = i
                    self._write(e, after, dict(met))
                emit.reg = None
                continue
            for w in after:
                series, step = self.named[w] if isinstance(w, str) else w
                step = as_step(step)
                if step.loop is None:
                    need = (step.c + 1) * series.unit
                    if need <= met.get(series, 0):
                        continue
                    met[series] = need
                    e.wait_ge(series.sem, need)
                else:
                    e.wait_ge(series.sem, step.of(series.unit, series.unit).value())
            last = emit(e)
            if signal is not None:
                last.then_inc(signal.sem, signal.unit)


def steps(plan, first, count, per, body, straight=0):
    turns = (count - straight) // per
    if turns > 1:
        with plan.loop(turns) as loop:
            for k in range(per):
                body(Step(first + k, loop, per))
    else:
        turns = 0
    for k in range(first + turns * per, first + count):
        body(Step(k))


def bcast(ap, *dims):
    return bass.AP(tensor=ap.tensor, offset=ap.offset, ap=[list(ap.ap[0])] + [list(d) for d in dims])


def build(nc, A, out):
    plan = Plan(nc, ("sp", "act", "dve", "pool", "pe"))
    op = plan.op

    def sb(name, shape, dt=F32):
        return nc.alloc_sbuf_tensor(name, shape, dt)[tuple(slice(None) for _ in shape)]

    raw = [sb(f"raw{i}", [P, PIECE]) for i in range(RAW)]
    w_hi = [sb(f"w_hi{i}", [P, PIECE], F32R) for i in range(RING)]
    w_lo = [sb(f"w_lo{i}", [P, PIECE], F32R) for i in range(RING)]
    h = sb("h", [P, T, D])
    xT_hi, xT_lo = sb("xT_hi", [P, KB, S], F32R), sb("xT_lo", [P, KB, S], F32R)
    z_hi, z_lo = sb("z_hi", [P, 3, 2 * S], F32R), sb("z_lo", [P, 3, 2 * S], F32R)
    rms = sb("rms", [P, S])
    ident, ones = sb("ident", [P, P]), sb("ones", [P, S])
    zeros = sb("zeros", [P, P], BF16)
    diag = sb("diag", [P, T, P])
    rstd, ssq = sb("rstd", [P, 2 * T]), sb("ssq", [P, 2 * T])
    minus_half = sb("minus_half", [P, 1])
    ncols = sum(n for _, n in VECTORS)
    cols = sb("cols", [P, ncols])
    extra = sb("extra", [P, 4 * KB])
    gate_w = sb("gate_w", [P, 2, KB, P])
    pool_w = sb("pool_w", [P, PG, P])
    tiny = sb("tiny", [P, 6, 4])
    sink = sb("sink", [P, HEADS_2])
    work_bytes = 47 * 1024
    work = nc.alloc_sbuf_tensor("work", [P, work_bytes // 4], F32)
    bank = [nc.alloc_psum_tensor(f"bank{i}", [P, 512], F32)[:, :] for i in range(8)]
    acc = [[bank[0], bank[1]], [bank[2], bank[3]]]
    RMS_BANK = bank[7]

    def at(kib, *shape):
        n, o = int(np.prod(shape)), int(kib * 256)
        assert (o + n) * 4 <= work_bytes, (kib, shape)
        v = work[:, o:o + n]
        if len(shape) == 1:
            return v
        names = "abcd"[:len(shape)]
        return v.rearrange(f"p ({' '.join(names)}) -> p {' '.join(names)}", **dict(zip(names, shape)))

    def r32(ap):
        return ap.bitcast(F32)

    col_at, c = {}, 0
    for name, n in VECTORS:
        col_at[name], c = c, c + n

    def col(name, k):
        return cols[:, col_at[name] + k:col_at[name] + k + 1]

    def gain(name):
        return cols[:, col_at[name]:col_at[name] + KB]

    landed = [Series(nc, f"landed{i}", 16) for i in range(RAW)]
    hi_done = Series(nc, "hi_done")
    lo_done = Series(nc, "lo_done")
    used = Series(nc, "used")
    z_t = Series(nc, "z_t")
    z_g = Series(nc, "z_g")
    z_f = Series(nc, "z_f")
    zhi_done = Series(nc, "zhi_done")
    zlo_done = Series(nc, "zlo_done")
    acc_done = Series(nc, "acc_done")
    turned = Series(nc, "turned")
    x_full = Series(nc, "x_full")
    xhi_done = Series(nc, "xhi_done")
    xlo_done = [Series(nc, "xlo0_done"), Series(nc, "xlo1_done")]
    mix_hi = Series(nc, "mix_hi")
    mix_lo = Series(nc, "mix_lo")
    const_in = {}

    def load(name, dst, src, engine="pool", after=()):
        const_in[name] = Series(nc, f"in_{name}", 16)
        op(engine, lambda e: e.dma_start(dst, src), after=after, signal=const_in[name])

    def has(name):
        return (const_in[name], 0)

    class Stream:
        n = 0

    def u_src(w, cstep):
        v = w.rearrange("(k p) c -> p k c", p=P)
        return lambda: v[:, :, bass.ds(cstep.value(), 2 * P)]

    def d_src(w, rstep):
        return lambda: w[bass.ds(rstep.value(), 2 * P), :].rearrange("(k p) c -> p k c", p=P)

    def load_piece(n, src, kind):
        n, slot = as_step(n), as_step(n).slot(RAW)
        dst = raw[slot].rearrange("p (k c) -> p k c", k=KB if kind == "U" else 2)
        op("sp", lambda e: e.dma_start(dst, src()), after=[(lo_done, n.of(1, -RAW))] if free(n, RAW) else [],
           signal=landed[slot])

    def free(n, ring):
        return n.loop is not None or n.c >= ring

    def split_hi(n):
        n = as_step(n)
        s, r = n.slot(RING), n.slot(RAW)
        after = [(landed[r], Step(n.c // RAW, n.loop, n.per // RAW))]
        if free(n, RING):
            after.append((used, n.of(1, -RING)))
        op("act", lambda e: e.activation(w_hi[s], raw[r], ACT.Copy), after=after, signal=hi_done)

    def split_lo(n):
        n = as_step(n)
        s, r = n.slot(RING), n.slot(RAW)
        op("dve", lambda e: e.tensor_tensor(w_lo[s], raw[r], r32(w_hi[s]), ALU.subtract),
           after=[(hi_done, n)], signal=lo_done)

    def split_piece(n):
        if as_step(n).loop is not None or as_step(n).c < TOTAL:
            split_hi(n), split_lo(n)

    def split_now(n):
        return [(hi_done, n), (lo_done, n)]

    def u_piece(n, dst, after=(), after_k=None, between=None, freed=None):
        n, s = as_step(n), as_step(n).slot(RING)
        whi = w_hi[s].rearrange("p (k c) -> p k c", k=KB)
        wlo = w_lo[s].rearrange("p (k c) -> p k c", k=KB)

        def block(k):
            def emit(e):
                for b in range(2):
                    o = dst[:, b * S:(b + 1) * S]
                    for i, (w, x) in enumerate(((whi, xT_hi), (whi, xT_lo), (wlo, xT_hi))):
                        last = e.matmul(o, w[:, k, b * P:(b + 1) * P], x[:, k, :],
                                        start=(k == 0 and b == 0 and i == 0), stop=(k == KB - 1 and i == 2),
                                        skip_group_check=True)
                return last
            return emit
        for k in range(KB):
            op("pe", block(k), after=(list(after) + split_now(n) if k == 0 else []) + (after_k(k) if after_k else []),
               signal=used if k == KB - 1 else None, name=f"{freed}{k}" if freed and k < KB - 1 else None)
            if after_k and turn_later:
                turn_later.pop(0)()
            if between and k in between:
                between[k]()

    def d_part(n, lhs, t, kks, halves, first=False, last=False, after=(), signal=None):
        s = as_step(n).slot(RING)
        whi = w_hi[s].rearrange("p (k c) -> p k c", k=2)
        wlo = w_lo[s].rearrange("p (k c) -> p k c", k=2)

        def emit(e):
            for kk in kks:
                xhi, xlo = lhs(kk, t)
                for x, ws in ((xhi, (whi, wlo)), (xlo, (whi,))):
                    for w in ws:
                        for half in halves:
                            mm = e.matmul(acc[t][half], x, w[:, kk, half * 512:(half + 1) * 512],
                                          start=(first and kk == 0 and x is xhi and w is whi),
                                          stop=(last and kk == 1 and x is xlo), skip_group_check=True)
            return mm
        op("pe", emit, after=after, signal=signal)

    def d_piece(n, lhs, first=False, after=()):
        n = as_step(n)
        for t in range(T):
            d_part(n, lhs, t, (0, 1), (0, 1), first, after=list(after) + split_now(n) if t == 0 else (),
                   signal=used if t == T - 1 else None)

    def last_d_pieces(one, two, between=None):
        (n1, lhs1, after1), (n2, lhs2, after2) = one, two
        c = acc_done.claim(2)
        d_part(n1, lhs1, 0, (0, 1), (0, 1), after=list(after1) + split_now(n1))
        if between:
            between()
        d_part(n2, lhs2, 0, (0, 1), (0, 1), last=True, after=list(after2) + split_now(n2), signal=acc_done)
        closing.extend([
            lambda: d_part(n1, lhs1, 1, (0,), (0, 1)),
            lambda: d_part(n1, lhs1, 1, (1,), (0, 1), signal=used),
            lambda: d_part(n2, lhs2, 1, (0, 1), (0,), last=True, signal=acc_done),
            lambda: d_part(n2, lhs2, 1, (0,), (1,)),
            lambda: d_part(n2, lhs2, 1, (1,), (1,), last=True, signal=used)])
        return [[(acc_done, c)] * 2, [(acc_done, c + 1), (used, n2)]]

    closing, split_later = [], []

    def close(n=5):
        for part in closing[:n]:
            part()
        del closing[:n]

    vec_rows = at(0, 2, P)
    VEC_ROWS = [P, ncols - P]
    vec_in = [Series(nc, f"vec_in{g}", 16) for g in range(2)]
    for g, n in enumerate(VEC_ROWS):
        op("act", lambda e, g=g, n=n: e.dma_start(vec_rows[0:n, g, :], A["vectors"][g * P:g * P + n, :]),
           signal=vec_in[g])

    x_in = [Series(nc, f"x_in{t}", 16) for t in range(T)]
    for t in range(T):
        op("sp", lambda e, t=t: e.dma_start(h[:, t, :], A["x"][t * P:(t + 1) * P, :]), signal=x_in[t])

    op("pool", lambda e: e.memset(ident, 0.0), name="ident0")
    op("pool", lambda e: e.affine_select(out=ident, in_=ident, compare_op=ALU.not_equal, fill=1.0, base=0,
                                         pattern=[[-1, P]], channel_multiplier=1), after=["ident0"], name="ident")
    op("pool", lambda e: e.memset(ones, 1.0), name="ones")
    op("pool", lambda e: e.memset(minus_half, -0.5), name="minus_half")
    op("pool", lambda e: e.memset(zeros, 0.0), name="zeros")
    op("act", lambda e: e.activation(tiny[:, 0, 0:1], ones[:, 0:1], ACT.Copy), after=["ones"])

    def turn_vectors(g):
        rows = VEC_ROWS[g]
        return lambda e: e.transpose(bank[0][:, g * P:g * P + rows], vec_rows[0:rows, g, :], ident[0:rows, 0:rows])
    for g in range(2):
        op("pe", turn_vectors(g), after=["ident", (vec_in[g], 0)], name=f"vec_turn{g}")
    op("dve", lambda e: e.tensor_copy(cols, bank[0][:, 0:ncols]), after=["vec_turn1"], name="cols")

    norms, turn_later, QS = [], [], 4

    def turn_h(name, gains, acc0=None, scale=1.0, between=None, x_at=4,
               turn_banks=(5, 6, 7, 0), h_ready=()):
        j = len(norms)
        norms.append(name)
        base = turned.claim(QS * T)
        assert x_full.claim(QS * T) == xhi_done.claim(QS * T) == base == QS * T * j
        assert xlo_done[0].claim(QS) == xlo_done[1].claim(QS) == QS * j
        full = at(x_at, QS, 2 * P)
        banks = [bank[i] for i in turn_banks]

        def add(t, q):
            if acc0 is not None:
                op("dve", lambda e: e.scalar_tensor_tensor(
                    out=h[:, t, q * 2 * P:(q + 1) * 2 * P], in0=acc[t][q // 2][:, (q % 2) * 2 * P:(q % 2 + 1) * 2 * P],
                    scalar=scale, in1=h[:, t, q * 2 * P:(q + 1) * 2 * P], op0=ALU.mult, op1=ALU.add),
                    after=[acc0[t][q // 2]] + list(h_ready), name=f"{name}_h{t}{q}")

        def turn(t, q):
            def emit(e):
                for i in range(2):
                    k = 2 * q + i
                    tr = e.transpose(banks[q][:, i * P:(i + 1) * P], h[:, t, k * P:(k + 1) * P], ident)
                return tr
            have = [f"{name}_h{t}{q}"] if acc0 is not None else [(x_in[t], 0)]
            op("pe", emit, after=have + ["ident"] + ([(x_full, base + q)] if t else []), signal=turned)

        def gained(t, q):
            op("dve", lambda e: e.tensor_tensor(
                full[:, q, :].rearrange("p (k s) -> p k s", k=2),
                banks[q][:, 0:2 * P].rearrange("p (k s) -> p k s", k=2),
                bcast(gains[:, q * 2:q * 2 + 2], [1, 2], [0, P]), ALU.mult),
                after=[(turned, base + QS * t + q), "cols"] + ([(xlo_done[0], QS * j + q)] if t else []),
                signal=x_full)

        def halves(t, q):
            i = base + QS * t + q
            src = full[:, q, :].rearrange("p (k s) -> p k s", k=2)
            hi, lo = (x[:, q * 2:q * 2 + 2, t * P:(t + 1) * P] for x in (xT_hi, xT_lo))
            op("act", lambda e: e.activation(hi, src, ACT.Copy), after=[(x_full, i)], signal=xhi_done)
            op("dve" if t else "pool", lambda e: e.tensor_tensor(lo, src, r32(hi), ALU.subtract),
               after=[(xhi_done, i)], signal=xlo_done[t])

        junk = at(0, D)

        def square(t):
            have = [f"{name}_h{t}3"] if acc0 is not None else [(x_in[t], 0)]
            op("act", lambda e, t=t: e.activation(junk, h[:, t, :], ACT.Square, accum_out=ssq[:, t:t + 1]),
               after=have + ([f"{name}_ss0"] if t else ["cols"]), name=f"{name}_ss{t}")

        for t in range(T):
            add(t, 0)
            for q in range(QS + 1):
                if q + 1 < QS:
                    add(t, q + 1)
                if q < QS:
                    gained(t, q)
                if q:
                    halves(t, q - 1)
            if t == 0:
                for n in split_later:
                    split_hi(n)
            if (t == 0) == (acc0 is None):
                for n in split_later:
                    split_lo(n)
        split_later.clear()
        square(0), square(1)
        if acc0 is None:
            for t in range(T):
                for q in range(QS):
                    turn(t, q)
        else:
            close(1)
            turn(0, 0), turn(0, 1)
            close(1)
            turn(0, 2), turn(0, 3)
            close(2)
            turn(1, 0)
            close(1)
            turn(1, 1)
            turn_later.extend([lambda q=q: turn(1, q) for q in range(2, QS)])
        for t in range(T):
            make_rstd(f"{name}_r{t}", t, f"{name}_ss{t}")
        last = "r"
        if between is not None:
            for t in range(T):
                op("dve", lambda e, t=t: e.scalar_tensor_tensor(
                    out=h[:, t, :], in0=h[:, t, :], scalar=rstd[:, t:t + 1], in1=between, op0=ALU.mult,
                    op1=ALU.mult),
                   after=[f"{name}_r{t}", f"{name}_ss{t}", (turned, base + QS * t + QS - 1), has("norm_final")],
                   name=f"{name}_n{t}")
                op("act", lambda e, t=t: e.activation(junk, h[:, t, :], ACT.Square,
                                                      accum_out=ssq[:, T + t:T + t + 1]),
                   after=[f"{name}_n{t}", f"{name}_ns{t - 1}" if t else f"{name}_ss{T - 1}"], name=f"{name}_ns{t}")
            for t in range(T):
                make_rstd(f"{name}_nr{t}", T + t, f"{name}_ns{t}")
                op("pool", lambda e, t=t: e.tensor_tensor(rstd[:, t:t + 1], rstd[:, t:t + 1],
                                                          rstd[:, T + t:T + t + 1], ALU.mult),
                   after=[f"{name}_nr{t}", f"{name}_n{t}"], name=f"{name}_rr{t}")
            last = "rr"
        for t in range(T):
            op("pool", lambda e, t=t: e.tensor_scalar(diag[:, t, :], ident, rstd[:, t:t + 1], None, ALU.mult),
               after=[f"{name}_{last}{t}"], name=f"{name}_diag{t}")

    def make_rstd(name, i, ss):
        v = rstd[:, i:i + 1]
        op("pool", lambda e: e.tensor_scalar(v, ssq[:, i:i + 1], 1.0 / D, EPS, ALU.mult, ALU.add), after=[ss],
           name=f"{name}_v")
        op("pool", lambda e: e.tensor_tensor(v, v, minus_half, ALU.pow), after=[f"{name}_v", "minus_half"],
           name=name)

    def spread_rms(name):
        for t in range(T):
            op("pe", lambda e, t=t: e.matmul(RMS_BANK[:, t * P:(t + 1) * P], ones[:, 0:P], diag[:, t, :],
                                             start=True, stop=True),
               after=[f"{name}_diag{t}", "ones", (xlo_done[1], QS * len(norms) - 1)], name=f"{name}_spread{t}")
        op("dve", lambda e: e.tensor_copy(rms, RMS_BANK[:, 0:S]), after=[f"{name}_spread{T - 1}"],
           name=f"{name}_rms")

    def x_block_ready(j):
        return lambda k: [(xlo_done[t], QS * (j - 1) + k // 2) for t in range(T)]

    def rms_pair():
        return bcast(rms, [0, 2], [1, S])

    def pair(ap):
        return ap.rearrange("p (b s) -> p b s", b=2)

    def feed_forward(name, ups, down, width, straight=0):
        pairs, nu = width // (2 * P), len(ups)
        each, n0, bufs = nu + 1, Stream.n, (3 if nu == 1 else 2)
        b_zt, b_zf = z_t.claim(pairs), z_f.claim(pairs)
        b_zg = z_g.claim(pairs) if nu == 2 else 0
        b_hi, b_lo = zhi_done.claim(pairs), zlo_done.claim(pairs)
        j = len(norms)
        tmp = [at(0, 2 * S), at(2, 2 * S), at(4, 2 * S)]

        def ups_at(p):
            return Step(n0) if p.loop is None and p.c == 0 else p.of(each, n0 - 1)

        def d_at(p):
            return p.of(each, n0 + each - 1) if p.loop is None and p.c == pairs - 1 \
                else p.of(each, n0 + 2 * each - 2)

        def psum_of(p, i):
            return bank[4 + p.slot(bufs) * nu + i]

        def up(p):
            n = ups_at(p)
            for i, w in enumerate(ups):
                load_piece(n.of(1, i), u_src(w, p.of(2 * P)), "U")
            for i in range(nu):
                after = []
                if free(p, bufs):
                    after = [(z_t, p.of(1, b_zt - bufs))]
                first = p.loop is None and p.c == 0 and i == 0
                u_piece(n.of(1, i), psum_of(p, i), after=after, after_k=x_block_ready(j) if first else None)

        def down_of(p):
            n = d_at(p)
            load_piece(n, d_src(down, p.of(2 * P)), "D")
            s = p.slot(bufs)
            return n, lambda kk, t: (z_hi[:, s, kk * S + t * P:kk * S + (t + 1) * P],
                                     z_lo[:, s, kk * S + t * P:kk * S + (t + 1) * P]), \
                [(zhi_done, p.of(1, b_hi)), (zlo_done, p.of(1, b_lo))]

        def finish_z(p):
            s, src = p.slot(bufs), psum_of(p, nu - 1)
            freed = []
            if free(p, bufs):
                freed = [(used, p.of(each, n0 + 2 * each - 2 - bufs * each))]
            here = [(used, ups_at(p).of(1, nu - 1)), f"{name}_rms"]
            if nu == 1:
                t, z = tmp[0], tmp[1]
                op("dve", lambda e: e.scalar_tensor_tensor(out=pair(t), in0=pair(src), scalar=0.0, in1=rms_pair(),
                                                           op0=ALU.max, op1=ALU.mult),
                   after=here + [(zhi_done, p.of(1, b_hi - 1))], signal=z_t)
                op("dve", lambda e: e.tensor_tensor(z, t, t, ALU.mult), after=[(z_t, p.of(1, b_zt))], signal=z_f)
                op("act", lambda e: e.activation(z_hi[:, s, :], t, ACT.Square),
                   after=[(z_t, p.of(1, b_zt))] + freed, signal=zhi_done)
            else:
                g, u, z = tmp
                op("dve", lambda e: e.tensor_tensor(pair(g), pair(psum_of(p, 0)), rms_pair(), ALU.mult),
                   after=here, name=None, signal=z_g)
                op("act", lambda e: e.activation(g, g, ACT.Silu), after=[(z_g, p.of(1, b_zg))], signal=z_s)
                op("dve", lambda e: e.tensor_tensor(pair(u), pair(src), rms_pair(), ALU.mult), signal=z_t)
                op("dve", lambda e: e.tensor_tensor(z, g, u, ALU.mult),
                   after=[(z_s, p.of(1, b_zg)), (z_t, p.of(1, b_zt)), (zhi_done, p.of(1, b_hi - 1))], signal=z_f)
                op("act", lambda e: e.activation(z_hi[:, s, :], z, ACT.Copy),
                   after=[(z_f, p.of(1, b_zf))] + freed, signal=zhi_done)
            op("dve", lambda e: e.tensor_tensor(z_lo[:, s, :], z, r32(z_hi[:, s, :]), ALU.subtract),
               after=[(zhi_done, p.of(1, b_hi)), (z_f, p.of(1, b_zf))], signal=zlo_done)

        up(Step(0))
        split_piece(n0 + LOOK)
        spread_rms(name)
        for half in range(4):
            op("pe", lambda e, half=half: e.matmul(bank[half][:, 0:2], zeros, zeros[:, 0:2], start=True, stop=False,
                                                   skip_group_check=True), after=["zeros"])
        for i in range(1, nu):
            split_piece(n0 + i + LOOK)
        finish_z(Step(0))

        def turn(p):
            up(p)
            n, lhs, after = down_of(p.of(1, -1))
            d_piece(n, lhs, after=after)
            n = ups_at(p)
            for i in range(each - 1):
                split_piece(n.of(1, i + LOOK))
            finish_z(p)
            split_piece(n.of(1, each - 1 + LOOK))
        steps(plan, 1, pairs - 2, BODY // each, turn, straight=straight)
        last = Step(pairs - 1)
        up(last)
        ready = last_d_pieces(down_of(last.of(1, -1)), down_of(last))
        n = ups_at(last)
        for i in range(each - 1):
            split_piece(n.of(1, i + LOOK))
        finish_z(last)
        split_piece(n.of(1, each - 1 + LOOK))
        split_later.append(n0 + each * pairs - 1 + LOOK)
        Stream.n += each * pairs
        return ready

    z_s = Series(nc, "z_s")

    def projection(w, order, ready):
        n0 = Stream.n
        Stream.n += len(order)
        for m, i in enumerate(order):
            load_piece(n0 + m, d_src(w, Step(i * 2 * P)), "D")
        return [(Step(n0 + m), lambda kk, t, i=i: (xT_hi[:, 2 * i + kk, t * P:(t + 1) * P],
                                                   xT_lo[:, 2 * i + kk, t * P:(t + 1) * P]), ready(i))
                for m, i in enumerate(order)]

    def project(w, order, ready):
        pieces = projection(w, order, ready)
        for m, (n, lhs, after) in enumerate(pieces[:-2]):
            d_piece(n, lhs, first=(m == 0), after=after)
            split_piece(n.of(1, LOOK))
        return end_projection(pieces)

    def end_projection(pieces, between=None):
        split_piece(pieces[-2][0].of(1, LOOK))
        split_later.append(pieces[-1][0].c + LOOK)
        return last_d_pieces(*pieces[-2:], between=between)

    def projection_beside(turn, piece, first=False):
        n, lhs, after = piece

        def products(steps_):
            steps_[0]()
            d_part(n, lhs, 0, (0, 1), (0, 1), first, after=list(after) + split_now(n))
            steps_[1](), steps_[2]()
            d_part(n, lhs, 1, (0, 1), (0, 1), first, signal=used)
            steps_[3]()
        turn(lambda: split_hi(n.of(1, LOOK)), products, lambda: split_lo(n.of(1, LOOK)))

    def attention(name, pairs, widths, masks, qT, kT, v, o, pt, pp, ready, ready_qk=lambda j: [], sinks=False,
                  bank7_free=(), mix_at=None, bank6_free=[]):
        A_ = {k: Series(nc, f"{name}_{k}") for k in
              ("qkhi", "qklo", "s", "tm", "nm", "ex", "tr", "pt0", "pt1", "pv", "rc", "o", "sd", "es", "sa")}
        off = [0, widths[0]]
        tiles = [(t, kt) for t in range(T) for kt in range(widths[t] // P)]

        def halves_of(j):
            return [(zz[:, j.c % 2, 0:S], zz[:, j.c % 2, S:2 * S]) for zz in (z_hi, z_lo)]

        mx, nm, sm, rc, sd, es = (tiny[:, i, :] for i in range(6))

        def prev(series, j, n=1, plus=0):
            return [(series, j.of(n, plus))] if j.c * n + plus >= 0 else []

        def split_qk(j, engine):
            (q_hi, k_hi), (q_lo, k_lo) = halves_of(j)
            for i, (x, xh, xl) in enumerate(((qT, q_hi, q_lo), (kT, k_hi, k_lo))):
                if engine == "act":
                    op("act", lambda e, x=x, xh=xh: e.activation(xh, x[:, j.c, :], ACT.Copy),
                       after=prev(A_["s"], j, 2, -3) + ready_qk(j), signal=A_["qkhi"])
                else:
                    op("dve", lambda e, x=x, xh=xh, xl=xl: e.tensor_tensor(xl, x[:, j.c, :], r32(xh), ALU.subtract),
                       after=[(A_["qkhi"], j.of(2, i))], signal=A_["qklo"])

        def scores(j):
            (q_hi, k_hi), (q_lo, k_lo) = halves_of(j)
            for hd in range(2):
                r = slice(hd * HD, (hd + 1) * HD)

                def emit(e, r=r, hd=hd):
                    for t in range(T):
                        dst = bank[4 + hd][:, off[t]:off[t] + widths[t]]
                        for i, (q_, k_) in enumerate(((q_hi, k_hi), (q_hi, k_lo), (q_lo, k_hi))):
                            mm = e.matmul(dst, q_[r, t * P:(t + 1) * P], k_[r, 0:widths[t]], start=(i == 0),
                                          stop=(i == 2))
                    return mm
                op("pe", emit, after=[(A_["qklo"], j.of(2, 1))] + prev(A_["tm"], j, 4, 2 * hd - 3),
                   signal=A_["s"])

        def mask_and_max(j, hd):
            for t in range(T):
                m = masks(j, hd, t)
                sl = slice(off[t], off[t] + widths[t])
                c = 2 * hd + t
                op("dve", lambda e, m=m, sl=sl, c=c: e.tensor_tensor_reduce(
                    pp[hd][:, sl], bank[4 + hd][:, sl], m, 1.0, NEG, ALU.add, ALU.max, mx[:, c:c + 1]),
                   after=[(A_["s"], j.of(2, hd))] + prev(A_["tr"], j, 2, hd - 2) + ready, signal=A_["tm"])
            c = slice(2 * hd, 2 * hd + 2)
            done = [(A_["tm"], j.of(4, 2 * hd + 1))]
            if sinks:
                mine = sink[:, 2 * j.c + hd:2 * j.c + hd + 1]
                op("dve", lambda e: e.tensor_scalar(mx[:, c], mx[:, c], mine, None, ALU.max),
                   after=done + [has("sink")], signal=A_["sd"])
                done = [(A_["sd"], j.of(4, 2 * hd))]
                op("dve", lambda e: e.tensor_scalar(sd[:, c], mx[:, c], -1.0, mine, ALU.mult, ALU.add),
                   after=done + prev(A_["es"], j, 1, -1), signal=A_["sd"])
            op("dve", lambda e: e.tensor_scalar(nm[:, c], mx[:, c], -1.0, None, ALU.mult),
               after=done + prev(A_["ex"], j, 2, hd - 2), signal=A_["nm"])

        def exps(j, hd):
            for t in range(T):
                sl = slice(off[t], off[t] + widths[t])
                c = 2 * hd + t
                op("act", lambda e, sl=sl, c=c: e.activation(pp[hd][:, sl], pp[hd][:, sl], ACT.Exp,
                                                             bias=nm[:, c:c + 1], accum_out=sm[:, c:c + 1]),
                   after=[(A_["nm"], j.of(2, hd))], signal=A_["ex"] if t == T - 1 else None)
            if sinks and hd == 1:
                op("act", lambda e: e.activation(es, sd, ACT.Exp), after=[(A_["sd"], j.of(4, 3))],
                   signal=A_["es"])

        def turn_weights(j, hd):
            def emit(e):
                for i, (t, kt) in enumerate(tiles):
                    a = off[t] + kt * P
                    tr = e.transpose(bank[7][:, i * P:(i + 1) * P], pp[hd][:, a:a + P], ident)
                return tr
            left = [(A_["pt0"], j)] if hd else prev(A_["pt1"], j, 1, -1)
            op("pe", emit, after=[(A_["ex"], j.of(2, hd))] + left + list(bank7_free), signal=A_["tr"])

        def copy_turned(j, hd):
            n = len(tiles) * P
            after = [(A_["tr"], j.of(2, hd))] + prev(A_["pv"], j, 1, -1)
            if hd:
                op("act", lambda e: e.activation(pt[hd][:, 0:n], bank[7][:, 0:n], ACT.Copy), after=after,
                   signal=A_["pt1"])
            else:
                op("dve", lambda e: e.tensor_copy(pt[hd][:, 0:n], bank[7][:, 0:n]), after=after,
                   signal=A_["pt0"])

        def apply_weights(j):
            def emit(e):
                for hd in range(2):
                    for t in range(T):
                        mine = [(i, kt) for i, (tt, kt) in enumerate(tiles) if tt == t]
                        for m, (i, kt) in enumerate(mine):
                            mm = e.matmul(bank[6][:, (2 * hd + t) * P:(2 * hd + t + 1) * P],
                                          pt[hd][:, i * P:(i + 1) * P], v[:, kt, j.c * P:(j.c + 1) * P],
                                          start=(m == 0), stop=(m == len(mine) - 1))
                return mm
            op("pe", emit, after=[(A_["pt0"], j), (A_["pt1"], j)] + prev(A_["o"], j, 1, -1) + ready + bank6_free,
               signal=A_["pv"])

        def recips(j):
            done = [(A_["ex"], j.of(2, 1))]
            if sinks:
                op("dve", lambda e: e.tensor_tensor(sm, sm, es, ALU.add), after=done + [(A_["es"], j)],
                   signal=A_["sa"])
                done = [(A_["sa"], j)]
            op("dve", lambda e: e.reciprocal(rc, sm), after=done + prev(A_["o"], j, 1, -1), signal=A_["rc"])

        def store_o(j):
            def emit(e):
                return e.tensor_tensor(o[:, j.c, :, :].rearrange("p t (h d) -> p h t d", h=2),
                                       bass.AP(tensor=bank[6].tensor, offset=bank[6].offset,
                                               ap=[list(bank[6].ap[0]), [2 * P + HD, 2], [P, 2], [1, HD]]),
                                       bcast(rc, [2, 2], [1, 2], [0, HD]), ALU.mult)
            op("dve", emit, after=[(A_["pv"], j), (A_["rc"], j), (A_["qklo"], j.of(2, 1))], signal=A_["o"])

        def beside(j, leave, hi, piece, lo):
            before, j = Step(j - 1), Step(j)
            leave()
            if j.c % 2 == 0:
                split_qk(j, "act"), split_qk(j, "dve"), split_qk(j.of(1, 1), "act")
            if before.c >= 0:
                recips(before)
                copy_turned(before, 0)
            hi()
            if before.c >= 0:
                copy_turned(before, 1)
            for hd in range(2):
                mask_and_max(j, hd)
                exps(j, hd)
            if j.c % 2 == 0:
                split_qk(j.of(1, 1), "dve")
            lo()
            if before.c >= 0:
                piece([lambda: turn_weights(before, 0), lambda: scores(j), lambda: turn_weights(before, 1),
                       lambda: apply_weights(before)])
                store_o(before)
            else:
                piece([lambda: None, lambda: scores(j), lambda: None, lambda: None])

        def last_pair():
            last = Step(pairs - 1)
            recips(last)
            for hd in range(2):
                turn_weights(last, hd)
                copy_turned(last, hd)
            apply_weights(last)
            store_o(last)

        def to_xT(m, dst, after):
            def emit(e):
                for i in range(4):
                    tr = e.transpose(dst[:, i * P:(i + 1) * P], o[:, 2 * m + i // 2, i % 2, :], ident)
                return tr
            op("pe", emit, after=[(A_["o"], 2 * m + 1)] + list(after), name=f"{name}_oT{m}")
            op("act", lambda e: e.activation(xT_hi[:, 2 * m:2 * m + 2, :], pair(dst), ACT.Copy),
               after=[f"{name}_oT{m}"], signal=mix_hi)
            op("dve", lambda e: e.tensor_tensor(xT_lo[:, 2 * m:2 * m + 2, :], pair(dst),
                                                r32(xT_hi[:, 2 * m:2 * m + 2, :]), ALU.subtract),
               after=[(mix_hi, mix_at(m))], signal=mix_lo)

        return beside, last_pair, to_xT, A_


    TOTAL = 4 + 8 + 4 + 2 * (D_FF // 256) + 8 + 4 + 2 * (D_FF // 256) + 3 * (D_FF_2 // 256) + 5 + 4 \
        + 3 * (D_FF_2 // 256)

    split_later.append(0)
    turn_h("L0", gain("norm_mix0"), x_at=40, turn_banks=(5, 6, 7, 4))
    split_piece(1)
    ER, FAR = 384, 2 * MAX_REL
    table, er = at(4, FAR + 1), at(5.5, ER)
    load("rel", table[0:N_HEADS, :], A["rel"])
    sp = [at(7 + i / 16, KB) for i in range(6)]
    a_ = cols[:, col_at["a_param"]:col_at["a_param"] + KB]
    spp, spn, gg = extra[:, 0:KB], extra[:, KB:2 * KB], extra[:, 2 * KB:3 * KB]
    conv_bias = extra[:, 3 * KB:]
    chain = []

    def small(fn, extra_after=()):
        def queue():
            prior = [chain[-1]] if chain else ["cols"]
            chain.append(f"sp{len(chain)}")
            op("dve", fn, after=prior + list(extra_after), name=chain[-1])
        smalls.append(queue)

    def small_steps(n):
        for queue in smalls[:n]:
            queue()
        del smalls[:n]
    smalls = []

    small(lambda e: e.tensor_scalar(sp[0], a_, -1.0, None, ALU.mult))
    small(lambda e: e.tensor_tensor(sp[1], a_, sp[0], ALU.min))
    small_steps(2)
    op("act", lambda e: e.activation(sp[2], sp[1], ACT.Exp), after=[chain[-1]], name="sp_exp")
    small(lambda e: e.tensor_scalar(sp[3], sp[2], 2.0, None, ALU.add), ["sp_exp"])
    small(lambda e: e.reciprocal(sp[4], sp[3]))
    small(lambda e: e.tensor_tensor(sp[3], sp[2], sp[4], ALU.mult))
    small(lambda e: e.tensor_tensor(sp[4], sp[3], sp[3], ALU.mult))
    TERMS = 9
    small(lambda e: e.tensor_scalar(sp[5], sp[4], 1.0 / (2 * TERMS + 1), 1.0 / (2 * TERMS - 1), ALU.mult, ALU.add))
    for m in range(TERMS - 2, -1, -1):
        small(lambda e: e.tensor_tensor(sp[5], sp[5], sp[4], ALU.mult))
        small(lambda e, m=m: e.tensor_scalar(sp[5], sp[5], 1.0 / (2 * m + 1), None, ALU.add))
    small(lambda e: e.tensor_tensor(sp[5], sp[5], sp[3], ALU.mult))
    small(lambda e: e.tensor_scalar(sp[0], sp[0], 0.0, None, ALU.max))
    small(lambda e: e.scalar_tensor_tensor(out=sp[5], in0=sp[5], scalar=2.0, in1=sp[0], op0=ALU.mult, op1=ALU.add))
    small(lambda e: e.tensor_scalar(spp, sp[5], 8.0, None, ALU.mult))
    small(lambda e: e.tensor_scalar(spn, sp[5], -8.0, None, ALU.mult))
    small(lambda e: e.tensor_tensor(gg, cols[:, col_at["norm_final"]:col_at["norm_final"] + KB],
                                    cols[:, col_at["ffn1_norm"]:col_at["ffn1_norm"] + KB], ALU.mult))

    def vec(name, i=0):
        return cols[:, col_at[name] + i * KB:col_at[name] + (i + 1) * KB]
    small(lambda e: e.tensor_tensor(conv_bias, vec("conv_w"), vec("conv_w", 1), ALU.add))
    for tap in range(2, CONV):
        small(lambda e, tap=tap: e.tensor_tensor(conv_bias, conv_bias, vec("conv_w", tap), ALU.add))
    small(lambda e: e.tensor_tensor(conv_bias, conv_bias, vec("b_in"), ALU.mult))
    small(lambda e: e.tensor_tensor(conv_bias, conv_bias, vec("conv_b"), ALU.add))

    w_qkv = A["w_qkv"]
    qT, kT, v = at(24, KB, S), at(32, KB, S), None
    j0 = len(norms)
    acc0 = project(w_qkv[:, 2 * D:3 * D], range(4),
                   lambda i: [(xlo_done[t], QS * (j0 - 1) + i) for t in range(T)])
    close()
    op("dve", lambda e: e.tensor_copy(er[0:N_HEADS, 0:FAR], table[0:N_HEADS, 1:FAR + 1]), after=[has("rel")],
       name="er_near")
    op("dve", lambda e: e.tensor_copy(er[0:N_HEADS, FAR:ER], bcast(table[0:N_HEADS, FAR:FAR + 1], [0, ER - FAR])),
       name="er_far")
    er_dram = nc.dram_tensor("er_scratch", [N_HEADS, ER], F32, kind="Internal").ap()
    er_out = Series(nc, "er_out", 16)
    op("pool", lambda e: e.dma_start(er_dram, er[0:N_HEADS, :]), after=["er_far"], signal=er_out)
    bias = at(8, N_HEADS, S)
    load("bias", bias, bass.AP(tensor=er_dram.tensor, offset=0, ap=[[1, P], [ER, N_HEADS], [1, S]]),
         after=[(er_out, 0)])
    op("pool", lambda e: e.memset(bias[0:CHUNK, :, 0:CHUNK], NEG), after=[has("bias")], name="bias")
    load("gate_a", gate_w[:, 0], A["w_ga"].rearrange("n c e -> c n e"), engine="pool")
    load("gate_x", gate_w[:, 1], A["w_gx"].rearrange("n c e -> c n e"), engine="pool")
    load("pool_w", pool_w, A["pool_w"].rearrange("n c e -> c n e"), engine="pool")
    load("sink", sink, bass.AP(tensor=A["sink"].tensor, offset=A["sink"].offset, ap=[[0, P], [1, HEADS_2]]),
         engine="pool")

    v = vbuf = sb("v", [P, T, D])
    for t in range(T):
        for half in range(2):
            op("act", lambda e, t=t, half=half: e.activation(v[:, t, half * 512:(half + 1) * 512], acc[t][half],
                                                             ACT.Copy, scale=rstd[:, t:t + 1]),
               after=[acc0[t][half], f"L0_r{t}"], name=f"v{t}{half}")
    split_piece(split_later.pop())
    spread_rms("L0")
    n0, b_zt = Stream.n, z_t.claim(8)
    pp = [at(0, 384), at(1.5, 384)]
    pt = [at(3, 384), at(4.5, 384)]
    seen = [P, S]
    mb = mix_hi.claim(KB // 2)
    assert mix_lo.claim(KB // 2) == mb
    bank6_free = []
    beside, last_pair, to_xT, _ = attention(
        "a1", KB, seen, lambda j, hd, t: bias[:, 2 * j.c + hd, 0:seen[t]][:, ::-1], qT, kT, v,
        o=qT.rearrange("p j (t c) -> p j t c", t=T), pt=pt, pp=pp, ready=["v11", "bias", "L0_ss1"],
        ready_qk=lambda j: [(z_t, b_zt + j.c // 2 * 2 + 1)], bank7_free=["L0_rms"], mix_at=lambda m: mb + m,
        bank6_free=bank6_free)
    def qk_leave(m):
        to = (kT if m % 2 else qT)[:, m // 2 * 2:m // 2 * 2 + 2, :]
        op("dve", lambda e: e.scalar_tensor_tensor(
            out=to, in0=pair(bank[1 + m % 3]), scalar=1.0 if m % 2 else QSCALE, in1=rms_pair(), op0=ALU.mult,
            op1=ALU.mult), after=[(used, n0 + m), "L0_rms"], signal=z_t)

    def qk_piece(m, steps_=None):
        between = dict(zip((1, 3, 4, 6), steps_)) if steps_ else None
        u_piece(n0 + m, bank[1 + m % 3], after=[(z_t, b_zt + m - 3)] if m >= 3 else [["v01", "v10", "v11"][m]],
                between=between)
    for m in range(8):
        load_piece(n0 + m, u_src(w_qkv, Step(m % 2 * D + m // 2 * 2 * P)), "U")
        if m < 2:
            if m:
                qk_leave(m - 1)
            qk_piece(m)
            split_piece(n0 + m + LOOK)
            small_steps(4)
        else:
            beside(m - 2, lambda: qk_leave(m - 1), lambda: split_hi(n0 + m + LOOK),
                   lambda between: qk_piece(m, between), lambda: (split_lo(n0 + m + LOOK), small_steps(7)))
    qk_leave(7)
    Stream.n += 8
    assert not smalls
    wo = projection(A["w_o"], range(4), lambda i: [(mix_lo, mb + i), (z_t, b_zt + 7)])
    to_xT(0, bank[0], [])
    to_xT(1, bank[3], [(z_t, b_zt + 5)])
    projection_beside(lambda hi, products, lo: beside(6, lambda: None, hi, products, lo), wo[0], first=True)
    to_xT(2, bank[6], [])
    bank6_free.append((mix_lo, mb + 2))
    projection_beside(lambda hi, products, lo: beside(7, lambda: None, hi, products, lo), wo[1])

    def last_heads():
        last_pair()
        to_xT(3, bank[4], [])
    a0 = end_projection(wo, between=last_heads)
    turn_h("M0", gain("norm_mlp0"), a0)
    a0 = feed_forward("M0", [A["w1"][0]], A["w2"][0], D_FF)

    turn_h("L1", gain("norm_mix1"), a0)
    BP = S + CONV - 1
    xb, xc, rr, nt = at(4, KB, BP), at(13, KB, S), at(21, KB, S), at(29, KB, S)
    ig, sq = [at(37 + i, S) for i in range(2)], [at(39 + i, S) for i in range(2)]
    bo = at(41, D)
    load("b_o", bo, bass.AP(tensor=A["b_o"].tensor, offset=A["b_o"].offset, ap=[[0, P], [1, D]]), after=["L1_h13"])
    op("dve", lambda e: e.tensor_scalar(xb[:, :, 0:CONV - 1],
                                        bcast(cols[:, col_at["b_in"]:col_at["b_in"] + 1], [1, KB], [0, CONV - 1]),
                                        -1.0, None, ALU.mult),
       after=["L1_ss1", (xlo_done[1], QS * len(norms) - 1)], name="conv_pad")
    w_in = A["w_in"]
    n0, b_zt, j1 = Stream.n, z_t.claim(8), len(norms)

    def x_pair(p):
        op("dve", lambda e: e.tensor_tensor(xb[:, 2 * p:2 * p + 2, CONV - 1:], pair(bank[4 + p % 3]), rms_pair(),
                                            ALU.mult), after=[(used, n0 + p), "L1_rms", "L1_ss1"], signal=z_t)

    def conv(p):
        for n in (2 * p, 2 * p + 1):
            op("pool", lambda e, n=n: e.tensor_scalar(xc[:, n, :], xb[:, n, 0:S], col("conv_w", n),
                                                      conv_bias[:, n:n + 1], ALU.mult, ALU.add),
               after=[(z_t, b_zt + p), "conv_pad"], name=f"conv{n}_0")
        for n in (2 * p, 2 * p + 1):
            for tap in range(1, CONV):
                op("dve", lambda e, n=n, tap=tap: e.scalar_tensor_tensor(
                    out=xc[:, n, :], in0=xb[:, n, tap:tap + S], scalar=col("conv_w", tap * KB + n), in1=xc[:, n, :],
                    op0=ALU.mult, op1=ALU.add), after=[f"conv{n}_{tap - 1}"], name=f"conv{n}_{tap}")

    def gates(n):
        dst = bank[n % 4]

        def emit(e):
            e.matmul(dst[:, 0:S], gate_w[:, 0, n, :], xc[:, n, :], start=True, stop=True)
            return e.matmul(dst[:, S:2 * S], gate_w[:, 1, n, :], xc[:, n, :], start=True, stop=True)
        op("pe", emit, after=[f"conv{n}_{CONV - 1}", has("gate_a"), has("gate_x")] +
           ([f"ig{n - 4}"] if n >= 4 else []), name=f"gates{n}")
        op("act", lambda e: e.activation(rr[:, n, :], dst[:, 0:S], ACT.Sigmoid, bias=col("b_ga", n)),
           after=[f"gates{n}", chain[-1]], name=f"r{n}")
        op("act", lambda e: e.activation(ig[n % 2], dst[:, S:2 * S], ACT.Sigmoid, bias=col("b_gx", n)),
           after=[f"bx{n - 2}"] if n >= 2 else [], name=f"ig{n}")
        op("act", lambda e: e.activation(nt[:, n, :], rr[:, n, :], ACT.Tanh, scale=spp[:, n:n + 1]),
           after=[f"r{n}"], name=f"nt{n}")
        op("pool", lambda e: e.tensor_tensor(xc[:, n, :], xc[:, n, :], ig[n % 2], ALU.mult), after=[f"ig{n}"],
           name=f"bx{n}")

    def decays():
        for n in range(KB):
            op("act", lambda e, n=n: e.activation(rr[:, n, :], rr[:, n, :], ACT.Exp, scale=spn[:, n:n + 1]),
               after=[f"nt{n}"], name=f"a{n}")
            op("pool", lambda e, n=n: e.tensor_tensor(sq[n % 2], rr[:, n, :], rr[:, n, :], ALU.mult),
               after=[f"a{n}"] + ([f"m{n - 2}"] if n >= 2 else []), name=f"sq{n}")
            op("dve", lambda e, n=n: e.scalar_tensor_tensor(out=nt[:, n, :], in0=sq[n % 2], scalar=1.0,
                                                            in1=nt[:, n, :], op0=ALU.add, op1=ALU.mult),
               after=[f"sq{n}"], name=f"m{n}")

    def roots():
        for n in range(KB):
            op("act", lambda e, n=n: e.activation(nt[:, n, :], nt[:, n, :], ACT.Sqrt), after=[f"m{n}"],
               name=f"mult{n}")

    def scans(blocks):
        for n in blocks:
            op("dve" if n < KB // 2 else "pool", lambda e, n=n: e.tensor_tensor(xc[:, n, :], xc[:, n, :],
                                                                                nt[:, n, :], ALU.mult),
               after=[f"mult{n}", f"bx{n}"], name=f"b{n}")
            op("dve", lambda e, n=n: e.tensor_tensor_scan(nt[:, n, :], rr[:, n, :], xc[:, n, :], 0.0, ALU.mult,
                                                          ALU.add), after=[f"b{n}"], name=f"hs{n}")

    def y_pair(p):
        op("dve", lambda e: e.tensor_tensor(xb[:, 2 * p:2 * p + 2, 0:S], pair(bank[[5, 6, 7, 4][p]]), rms_pair(),
                                            ALU.mult),
           after=[(used, n0 + 4 + p)] + [f"conv{n}_{CONV - 1}" for n in range(2 * p, 2 * p + 2)], signal=z_t)

    def mixed(p):
        for n in (2 * p, 2 * p + 1):
            op("act", lambda e, n=n: e.activation(xb[:, n, 0:S], xb[:, n, 0:S], ACT.Gelu_apprx_tanh,
                                                  bias=col("b_in", KB + n)), after=[(z_t, b_zt + 4 + p)],
               name=f"y{n}")
            op("dve", lambda e, n=n: e.tensor_tensor(xc[:, n, :], xb[:, n, 0:S], nt[:, n, :], ALU.mult),
               after=[f"y{n}", f"hs{n}"], name=f"o{n}")
        for n in (2 * p, 2 * p + 1):
            op("act", lambda e, n=n: e.activation(xT_hi[:, n, :], xc[:, n, :], ACT.Copy),
               after=[f"o{n}", f"xT_read{n}" if n < KB - 1 else (used, n0 + 7)], signal=mix_hi)
            op("dve", lambda e, n=n: e.tensor_tensor(xT_lo[:, n, :], xc[:, n, :], r32(xT_hi[:, n, :]), ALU.subtract),
               after=[(mix_hi, mbr + n)], signal=mix_lo)

    mbr = mix_hi.claim(KB)
    assert mix_lo.claim(KB) == mbr

    def rec_piece(m, leave=None, convolve=None, gate=None):
        load_piece(n0 + m, u_src(w_in, Step(m * 2 * P)), "U")
        if m + LOOK < 8:
            split_hi(n0 + m + LOOK)
        if leave:
            leave(m - 1 if m <= 4 else m - 5)
        if m + LOOK < 8:
            split_lo(n0 + m + LOOK)
        if convolve:
            conv(m - 1)
        after = [(z_t, b_zt + m - 3)] if m == 3 else []
        between = {3: lambda: gates(2 * m - 4), 6: lambda: gates(2 * m - 3)} if gate else None
        u_piece(n0 + m, bank[4 + m % 3] if m < 4 else bank[[5, 6, 7, 4][m - 4]], after=after +
                ([(z_t, b_zt + {4: 1, 5: 2, 6: 2, 7: 3}[m])] if m >= 4 else []) +
                (["L1_rms"] if m == 6 else []),
                after_k=x_block_ready(j1) if m == 0 else None, between=between, freed="xT_read" if m == 7 else None)
    rec_piece(0)
    spread_rms("L1")
    rec_piece(1, x_pair, True)
    rec_piece(2, x_pair, True, True)
    rec_piece(3, x_pair, True, True)
    rec_piece(4, x_pair, True, True)
    rec_piece(5, y_pair, False, True)
    decays()
    rec_piece(6, y_pair)
    split_piece(n0 + 8)
    roots()
    scans(range(0, 2))
    rec_piece(7)
    mixed(0)
    scans(range(2, 8))
    split_piece(n0 + 9)
    y_pair(2)
    mixed(1)
    y_pair(3)
    mixed(2), mixed(3)
    for t in range(T):
        op("pool", lambda e, t=t: e.tensor_tensor(h[:, t, :], h[:, t, :], bo, ALU.add),
           after=[has("b_o"), (turned, QS * T * len(norms) - 1), f"L1_ss{t}"], name=f"h_bo{t}")
    Stream.n += 8
    a0 = project(A["rec_w_o"], range(4), lambda i: [(mix_lo, mbr + 2 * i + 1)])
    turn_h("M1", gain("norm_mlp1"), a0, h_ready=["h_bo1"])
    nf = at(8, D)
    load("norm_final", nf, bass.AP(tensor=A["norm_final"].tensor, offset=A["norm_final"].offset,
                                   ap=[[0, P], [1, D]]), after=["M1_h13"])
    a0 = feed_forward("M1", [A["w1"][1]], A["w2"][1], D_FF)

    turn_h("F1", gg, a0, between=nf)
    a0 = feed_forward("F1", [A["f1_gate"], A["f1_up"]], A["f1_down"], D_FF_2)

    turn_h("X", gain("mix_norm"), a0, scale=0.5)
    q2, k2, v2 = at(24, 4, S), at(28, 4, S), vbuf.rearrange("p t (a b) -> p t a b", a=2)[:, :, 0, :]
    cs_t, mats, mask2 = at(18, 2, S), at(20, 5, P), at(32, T, S)
    pc, csums, dd = at(4, PG, S), [at(8, S + 17), at(22.5, S + 17)], [at(i, S) for i in (10, 11, 12, 13)]
    inv, kv = at(36, PG, 2, S), at(12, 2 * S)
    qf, tq = at(14, 2 * S), at(16, 2 * S)
    load("tables", cs_t, A["rope"], after=["X_h13"])
    load("mats", mats, A["mats"], after=["X_h13"])
    load("mask2", mask2, A["mask2"], after=["X_h13"])
    load("inv", inv.rearrange("p g w s -> p (g w s)"),
         bass.AP(tensor=A["inv"].tensor, offset=A["inv"].offset, ap=[[0, P], [1, PG * 2 * S]]), after=["X_h13"])
    w2_in = A["w_in2"]
    j2, n0, b_zt = len(norms), Stream.n, z_t.claim(5)
    first_col = [512, 0, 768, 256, 1024]

    def mix_load(m):
        load_piece(n0 + m, u_src(w2_in, Step(first_col[m])), "U")

    def mix_piece(m, between=None):
        u_piece(n0 + m, bank[1 + m % 3], after=[(z_t, b_zt + m - 3)] if m >= 3 else [],
                after_k=x_block_ready(j2) if m == 0 else None, between=between)

    def leave(m, dst, scale=1.0, after=()):
        op("dve", lambda e: e.scalar_tensor_tensor(out=dst, in0=pair(bank[1 + m % 3]), scalar=scale, in1=rms_pair(),
                                                   op0=ALU.mult, op1=ALU.mult),
           after=[(used, n0 + m), "X_rms", "X_ss1"] + list(after), signal=z_t)

    for i in range(2):
        op("pool", lambda e, i=i: e.memset(csums[i][:, 0:9], 0.0),
           after=["X_ss1", (xlo_done[1], QS * len(norms) - 1)], name=f"csum_zero{i}")

    def pool_group(g):
        half, csum = POOL_WINDOWS[g] // 2, csums[g % 2]
        d = dd[2 * (g % 2):2 * (g % 2) + 2]
        op("dve", lambda e: e.tensor_tensor_scan(csum[:, 9:9 + S], ones, pc[:, g, :], 0.0, ALU.mult, ALU.add),
           after=[(z_t, b_zt + 2 + g // 2 * 2), f"csum_zero{g % 2}"] + ([f"d{g - 2}_2"] if g >= 2 else []),
           name=f"cs{g}_0")
        op("dve", lambda e: e.tensor_copy(csum[:, 9 + S:17 + S], bcast(csum[:, 8 + S:9 + S], [0, 8])),
           after=[f"cs{g}_0"], name=f"cs{g}_1")
        for w in range(2):
            a, b = 8 - half + w, 8 + half + w
            op("pool", lambda e, a=a, b=b, w=w: e.tensor_tensor(d[w], csum[:, b:b + S], csum[:, a:a + S],
                                                                ALU.subtract),
               after=[f"cs{g}_1", "v_turn1"] + ([f"pool{g - 2}"] if g >= 2 else []), name=f"d{g}_{1 + w}")
            op("pool", lambda e, w=w: e.tensor_tensor(d[w], d[w], inv[:, g, w, :], ALU.mult),
               after=[has("inv"), f"d{g}_{1 + w}"], name=f"e{g}_{w}")
        op("pool", lambda e: e.tensor_tensor(d[0], d[0], d[1], ALU.add), after=[f"e{g}_0", f"e{g}_1"],
           name=f"mean{g}")
        op("pool", lambda e: e.tensor_tensor(pc[:, g, :], d[0], pc[:, g, :], ALU.subtract), after=[f"mean{g}"],
           name=f"pool{g}")

    cos, sin = cs_t[:, 0, :], cs_t[:, 1, :]

    def two(ap):
        return bcast(ap, [0, 2], [1, S])

    def turn_kv():
        for g in range(KV_2):
            def emit(e, g=g):
                e.matmul(bank[4 + g][:, 0:S], mats[:, 1 + 2 * g, :], kv[:, 0:S], start=True, stop=True)
                return e.matmul(bank[4 + g][:, S:2 * S], mats[:, 2 + 2 * g, :], kv[:, 0:S], start=True, stop=True)
            op("pe", emit, after=[(z_t, b_zt), has("mats")], name=f"k_rot{g}")
        for t in range(T):
            op("pe", lambda e, t=t: e.transpose(bank[7][:, t * P:(t + 1) * P], kv[:, S + t * P:S + (t + 1) * P],
                                                ident), after=["X_rms"], name=f"v_turn{t}")

    def rope_k():
        for t in range(T):
            for g in range(KV_2):
                op("act", lambda e, t=t, g=g: e.activation(
                    v2[:, t, g * 4 * HD:(g + 1) * 4 * HD].rearrange("p (r d) -> p r d", d=HD),
                    bcast(bank[7][:, t * P + g * HD:t * P + (g + 1) * HD], [0, 4], [1, HD]), ACT.Copy),
                   after=["v_turn1"], name=f"v2_{t}{g}")
        for g in range(KV_2):
            op("dve", lambda e, g=g: e.tensor_tensor(tq[:, 0:S], bank[4 + g][:, 0:S], cos, ALU.mult),
               after=[f"k_rot{g}", has("tables")] + ([f"k2_{g - 1}"] if g else []), name=f"kc{g}")
            op("dve", lambda e, g=g: e.tensor_tensor(tq[:, S:2 * S], bank[4 + g][:, S:2 * S], sin, ALU.mult),
               name=f"ks{g}")
            op("dve", lambda e, g=g: e.tensor_tensor(k2[:, 2 * g:2 * g + 2, :], two(tq[:, 0:S]), two(tq[:, S:2 * S]),
                                                     ALU.add), after=[f"kc{g}", f"ks{g}"], name=f"k2_{g}")

    def q_rot(i):
        op("pe", lambda e: e.matmul(bank[0], mats[:, 0, :], qf, start=True, stop=True),
           after=[(z_t, b_zt + 1 + 2 * i), "k2_1"] + (["qsin0"] if i else []), name=f"q_rot{i}")

    def rope_q(i):
        op("dve", lambda e: e.tensor_tensor(q2[:, 2 * i:2 * i + 2, :], pair(qf), two(cos), ALU.mult),
           after=[(z_t, b_zt + 1 + 2 * i)], name=f"qcos{i}")
        op("dve", lambda e: e.tensor_tensor(pair(tq), pair(bank[0]), two(sin), ALU.mult), after=[f"q_rot{i}"],
           name=f"qsin{i}")
        op("dve", lambda e: e.tensor_tensor(q2[:, 2 * i:2 * i + 2, :], q2[:, 2 * i:2 * i + 2, :], pair(tq), ALU.add),
           after=[f"qcos{i}", f"qsin{i}"], name=f"q2_{i}")

    mp = mix_hi.claim(PG + 2)
    assert mix_lo.claim(PG + 2) == mp
    mix_order = ["pool0", "pool1", "heads0", "pool2", "pool3", "heads1"]

    def pool_products(p, dst, after):
        for g in (2 * p, 2 * p + 1):
            op("pe", lambda e, g=g: e.matmul(dst[:, (g % 2) * S:(g % 2 + 1) * S], pool_w[:, g, :], pc[:, g, :],
                                             start=True, stop=True),
               after=[f"pool{g}", has("pool_w")] + list(after), name=f"pool_y{g}")

    def pool_split(p, dst):
        for g in (2 * p, 2 * p + 1):
            src, i = dst[:, (g % 2) * S:(g % 2 + 1) * S], mp + mix_order.index(f"pool{g}")
            op("act", lambda e, g=g, src=src: e.activation(xT_hi[:, 4 + g, :], src, ACT.Copy,
                                                           scale=col("pool_scale", g)),
               after=[f"pool_y{2 * p + 1}", (used, n0 + 4)], signal=mix_hi)
        for g in (2 * p, 2 * p + 1):
            src, i = dst[:, (g % 2) * S:(g % 2 + 1) * S], mp + mix_order.index(f"pool{2 * p + 1}")
            op("dve", lambda e, g=g, src=src: e.scalar_tensor_tensor(
                out=xT_lo[:, 4 + g, :], in0=src, scalar=col("pool_scale", g), in1=r32(xT_hi[:, 4 + g, :]),
                op0=ALU.mult, op1=ALU.subtract), after=[(mix_hi, i)], signal=mix_lo)

    pp2 = [at(0, 2 * S), at(2, 2 * S)]
    pt2 = [at(34, 2 * S), at(44, 2 * S)]
    bank6_free_2 = []
    beside, last_pair, to_xT, a2 = attention(
        "a2", HEADS_2 // 2, [S, S], lambda j, hd, t: mask2[:, t, :], q2, k2, v2,
        o=q2.rearrange("p j (t c) -> p j t c", t=T), pt=pt2, pp=pp2, ready=["v2_11", has("mask2"), "X_ss1"],
        ready_qk=lambda j: [f"q2_{j.c // 2}", "k2_1"], sinks=True, bank7_free=["v2_11"],
        mix_at=lambda m: mp + mix_order.index(f"heads{m}"), bank6_free=bank6_free_2)

    def nothing():
        pass

    mix_load(0)
    mix_piece(0)
    spread_rms("X")
    split_piece(n0 + LOOK)
    mix_load(1)
    leave(0, pair(kv))
    mix_piece(1, {6: turn_kv})
    rope_k()
    split_piece(n0 + 1 + LOOK)
    mix_load(2)
    leave(1, pair(qf), scale=QSCALE)
    mix_piece(2, {4: lambda: q_rot(0)})
    rope_q(0)
    split_piece(n0 + 2 + LOOK)
    mix_load(3)
    beside(0, lambda: (leave(2, pc[:, 0:2, :]), pool_group(0), pool_group(1)), lambda: split_hi(n0 + 3 + LOOK),
           lambda st: mix_piece(3, {4: st[1]}), lambda: split_lo(n0 + 3 + LOOK))
    mix_load(4)
    beside(1, lambda: leave(3, pair(qf), scale=QSCALE, after=["q2_0", "qsin0"]), lambda: split_hi(n0 + 4 + LOOK),
           lambda st: mix_piece(4, {0: st[0], 3: st[1], 4: st[2], 6: lambda: (
               q_rot(1), st[3](), pool_products(0, bank[3], [(z_t, b_zt + 2)]))}),
           lambda: (rope_q(1), pool_split(0, bank[3])))
    Stream.n += 5
    waits = {i: [(mix_lo, mp + mix_order.index(n)), (z_t, b_zt + 4), "qsin1"]
             for i, n in enumerate(["heads0", "heads1", "pool1", "pool3"])}
    wo = projection(A["w_out"], [2, 0, 3, 1], waits.get)
    projection_beside(lambda hi, products, lo: beside(
        2, lambda: (leave(4, pc[:, 2:4, :]), pool_group(2), pool_group(3)), hi, products,
        lambda: (split_lo(n0 + 4 + LOOK), lo())), wo[0],
        first=True)
    to_xT(0, bank[6], [])
    bank6_free_2.append((mix_lo, mp + mix_order.index("heads0")))
    projection_beside(lambda hi, products, lo: beside(3, nothing, hi, products, lo), wo[1])
    pool_split(1, bank[5])
    pool_products(1, bank[5], [(a2["tm"], 4 * 3 + 3)])

    def last_heads_2():
        last_pair()
        to_xT(1, bank[4], [])
    a0 = end_projection(wo, between=last_heads_2)
    turn_h("F2", gain("ffn2_norm"), a0)
    load("norm_last", nf, bass.AP(tensor=A["norm_last"].tensor, offset=A["norm_last"].offset,
                                  ap=[[0, P], [1, D]]), after=["F2_h13"])
    a0 = feed_forward("F2", [A["f2_gate"], A["f2_up"]], A["f2_down"], D_FF_2, straight=2)
    assert Stream.n == TOTAL, (Stream.n, TOTAL)
    close()
    junk, res = at(12, D), at(16, T, D)
    out_done = Series(nc, "out_done", 16)
    for t in range(T):
        for half in range(2):
            hh = h[:, t, half * 512:(half + 1) * 512]
            op("dve", lambda e, hh=hh, a=acc[t][half]: e.scalar_tensor_tensor(
                out=hh, in0=a, scalar=0.5, in1=hh, op0=ALU.mult, op1=ALU.add), after=[a0[t][half]],
               name=f"last_h{t}{half}")
        op("act", lambda e, t=t: e.activation(junk, h[:, t, :], ACT.Square, accum_out=ssq[:, t:t + 1]),
           after=[f"last_h{t}0", f"last_h{t}1"] + ([f"last_ss{t - 1}"] if t else []), name=f"last_ss{t}")
        make_rstd(f"last_r{t}", t, f"last_ss{t}")
    for t in range(T):
        op("dve", lambda e, t=t: e.scalar_tensor_tensor(out=res[:, t, :], in0=h[:, t, :], scalar=rstd[:, t:t + 1],
                                                        in1=nf, op0=ALU.mult, op1=ALU.mult),
           after=[f"last_r{t}", has("norm_last")], name=f"last{t}")
        op("sp", lambda e, t=t: e.dma_start(out[t * P:(t + 1) * P, :], res[:, t, :]), after=[f"last{t}"],
           signal=out_done)
    op("sp", lambda e: e.nop(), after=[(out_done, T - 1), (er_out, 0)])

    with nc.Block() as block:
        @block.sync
        def _(e):
            plan.write("sp", e)

        @block.scalar
        def _(e):
            plan.write("act", e)

        @block.vector
        def _(e):
            plan.write("dve", e)

        @block.gpsimd
        def _(e):
            plan.write("pool", e)

        @block.tensor
        def _(e):
            plan.write("pe", e)


def shape_constants():
    f = np.float32
    freq = f(THETA) ** (-np.arange(0, ROT, 2, dtype=f) / f(ROT))
    ang = np.arange(S, dtype=f)[:, None] * freq[None, :]
    ang = np.concatenate([ang, ang], axis=-1).T
    rope = np.zeros((P, 2, S), f)
    rope[:, 0] = 1.0
    rot = np.zeros((HD, HD), f)
    for d in range(ROT // 2):
        rot[d + ROT // 2, d] = -1.0
        rot[d, d + ROT // 2] = 1.0
    for head in range(P // HD):
        rope[head * HD:head * HD + ROT, 0] = np.cos(ang)
        rope[head * HD:head * HD + ROT, 1] = np.sin(ang)
    mats = np.zeros((P, 5, P), f)
    for a in range(2):
        s = slice(a * HD, (a + 1) * HD)
        mats[s, 0, s] = rot
        for g in range(KV_2):
            mats[g * HD:(g + 1) * HD, 1 + 2 * g, s] = np.eye(HD, dtype=f)
            mats[g * HD:(g + 1) * HD, 2 + 2 * g, s] = rot
    qpos = np.arange(T)[None, :, None] * P + np.arange(P)[:, None, None]
    kpos = np.arange(S)[None, None, :]
    mask = np.where(np.abs(qpos - kpos) <= WINDOW, 0.0, NEG).astype(f)
    t = np.arange(S)
    inv = np.zeros((PG, 2, S), f)
    for g, w in enumerate(POOL_WINDOWS):
        for i in range(2):
            lo, hi = np.clip(t - w // 2 + i, 0, S), np.clip(t + w // 2 + i, 0, S)
            inv[g, i] = 0.5 / (hi - lo)
    return {"rope": rope, "mats": mats, "mask2": mask, "inv": inv}


def kernel(**inputs):
    import concourse.bacc as bacc
    from concourse.bass_utils import run_bass_kernel_spmd

    def flat(name, *shape):
        return np.ascontiguousarray(inputs[name]).reshape(shape)

    nm, nl = inputs["norm_mix"], inputs["norm_mlp"]
    vectors = {"norm_mix0": nm[0], "norm_mix1": nm[1], "norm_mlp0": nl[0], "norm_mlp1": nl[1],
               "norm_final": inputs["norm_final"], "ffn1_norm": inputs["ffn1_norm_2"],
               "mix_norm": inputs["mix_norm_2"], "ffn2_norm": inputs["ffn2_norm_2"], "b_in": inputs["rec_b_in"],
               "conv_b": inputs["rec_conv_b"], "b_ga": inputs["rec_b_ga"], "b_gx": inputs["rec_b_gx"],
               "a_param": inputs["rec_a_param"], "conv_w": inputs["rec_conv_w"],
               "pool_scale": inputs["pool_scale_2"]}
    arrays = {
        "x": flat("x", S, D), "vectors": np.concatenate([np.asarray(vectors[n]).reshape(-1, P) for n, _ in VECTORS]),
        "norm_final": flat("norm_final", D), "w_qkv": flat("attn_w_qkv", D, 3 * D), "w_o": flat("attn_w_o", D, D),
        "rel": flat("attn_rel_bias", N_HEADS, 2 * MAX_REL + 1), "w_in": flat("rec_w_in", D, 2 * D),
        "w_ga": flat("rec_w_ga", KB, P, P), "w_gx": flat("rec_w_gx", KB, P, P), "rec_w_o": flat("rec_w_o", D, D),
        "b_o": flat("rec_b_o", D), "w1": flat("mlp_w1", 2, D, D_FF), "w2": flat("mlp_w2", 2, D_FF, D),
        "f1_gate": flat("ffn1_w_gate_2", D, D_FF_2), "f1_up": flat("ffn1_w_up_2", D, D_FF_2),
        "f1_down": flat("ffn1_w_down_2", D_FF_2, D), "w_in2": flat("w_in_2", D, 1280),
        "sink": flat("sink_logits_2", HEADS_2), "pool_w": flat("pool_w_2", PG, P, P),
        "w_out": flat("w_out_2", D, D), "f2_gate": flat("ffn2_w_gate_2", D, D_FF_2),
        "f2_up": flat("ffn2_w_up_2", D, D_FF_2), "f2_down": flat("ffn2_w_down_2", D_FF_2, D),
        "norm_last": flat("final_norm_2", D),
    }
    arrays.update(shape_constants())
    nc = bacc.Bacc("TRN2", target_bir_lowering=False, num_devices=1)
    A = {k: nc.dram_tensor(f"in_{k}", a.shape, F32, kind="ExternalInput").ap() for k, a in arrays.items()}
    out = nc.dram_tensor("out", (1, S, D), F32, kind="ExternalOutput").ap()
    build(nc, A, out[0])
    r = run_bass_kernel_spmd(nc, [{f"in_{k}": a for k, a in arrays.items()}], core_ids=[0])
    return r.results[0]["out"]
```
